# Optimizing a Trainium2 kernel written in Bass

```python
import jax, jax.numpy as jnp
from jax import lax
import numpy as np

D_MODEL = 1024
BATCH = 1
SEQ = 256
DEPTH = 2

CHUNK = 64
D_POOL = D_MODEL // 4
POOL_WINDOWS = (2, 4, 8, 16)
N_POOL_GROUPS = len(POOL_WINDOWS)
POOL_GROUP = D_POOL // N_POOL_GROUPS
D_GMLP = 3 * D_MODEL // 8
GMLP_HEADS = 4
GMLP_HEAD_DIM = D_GMLP // GMLP_HEADS
GMLP_BLOCK = 128
D_CONV = D_MODEL - D_POOL - D_GMLP
CONV_WIDTH = 31
D_MIX = D_POOL + D_GMLP + D_CONV
D_IN = D_POOL + 2 * D_GMLP + 2 * D_CONV
D_FF = 2816
N_EXPERTS = 8
TOP_K = 2
D_FF_EXPERT = 3584
N_DENSE = (DEPTH + 1) // 2
N_MOE = DEPTH // 2
EPS = 1e-6


def rms_norm(x, g):
    xf = x.astype(jnp.float32)
    y = xf * lax.rsqrt(jnp.mean(xf * xf, axis=-1, keepdims=True) + EPS)
    return (y * g.astype(jnp.float32)).astype(x.dtype)

def layer_norm(x, g, b):
    xf = x.astype(jnp.float32)
    mu = jnp.mean(xf, axis=-1, keepdims=True)
    var = jnp.mean(jnp.square(xf - mu), axis=-1, keepdims=True)
    y = (xf - mu) * lax.rsqrt(var + EPS)
    return (y * g.astype(jnp.float32) + b.astype(jnp.float32)).astype(x.dtype)

def pool_mixer(a, w, scale):
    B, S, _ = a.shape
    af = a.astype(jnp.float32)
    csum = jnp.cumsum(af, axis=1)
    t = jnp.arange(1, S + 1, dtype=jnp.float32)
    outs = []
    for gi, win in enumerate(POOL_WINDOWS):
        sl = slice(gi * POOL_GROUP, (gi + 1) * POOL_GROUP)
        c = csum[..., sl]
        c_prev = jnp.pad(c[:, :-win], ((0, 0), (win, 0), (0, 0)))
        mean = (c - c_prev) / jnp.minimum(t, float(win))[None, :, None]
        outs.append(mean - af[..., sl])
    y = jnp.stack(outs, axis=2).astype(a.dtype)
    y = jnp.einsum('bsgc,gcd->bsgd', y, w).reshape(B, S, D_POOL)
    return y * scale

def gmlp_mixer(u, v, g, ws, b):
    B, S, _ = u.shape
    v = rms_norm(v, g)
    n_blk = S // GMLP_BLOCK
    vb = v.reshape(B, n_blk, GMLP_BLOCK, GMLP_HEADS, GMLP_HEAD_DIM)
    ci = jnp.arange(GMLP_BLOCK) // CHUNK
    mask = ci[:, None] >= ci[None, :]
    ws_m = jnp.where(mask[None], ws, jnp.zeros_like(ws))
    z = jnp.einsum('hij,bnjhc->bnihc', ws_m, vb) + b.T[None, None, :, :, None]
    return u * z.reshape(B, S, D_GMLP)

def conv_module(val, gate, w_dw, b_dw, ln_g, ln_b, w_pw, b_pw):
    h = val * jax.nn.sigmoid(gate)
    h = lax.conv_general_dilated(
        h, w_dw[:, None, :], window_strides=(1,),
        padding=((CONV_WIDTH - 1, 0),),
        dimension_numbers=('NWC', 'WIO', 'NWC'),
        feature_group_count=D_CONV) + b_dw
    h = jax.nn.silu(layer_norm(h, ln_g, ln_b))
    return h @ w_pw + b_pw

def swiglu(h, wg, wu, wd):
    return (jax.nn.silu(h @ wg) * (h @ wu)) @ wd

def moe_swiglu(h, router, wg, wu, wd):
    B, S, D = h.shape
    t = h.reshape(B * S, D)
    logits = t.astype(jnp.float32) @ router.astype(jnp.float32)
    top_v, top_i = lax.top_k(logits, TOP_K)
    top_w = jax.nn.softmax(top_v, axis=-1)
    gates = jnp.sum(jax.nn.one_hot(top_i, N_EXPERTS, dtype=jnp.float32)
                    * top_w[..., None], axis=1)
    out = jnp.zeros_like(t)
    for e in range(N_EXPERTS):
        out = out + gates[:, e:e + 1].astype(t.dtype) * swiglu(t, wg[e], wu[e], wd[e])
    return out.reshape(B, S, D)

def first_inputs(seed: int = 0) -> dict:
    key = jax.random.key(seed)
    k = jax.random.split(key, 26)
    f32 = jnp.float32
    nrm = lambda kk, shape, s: jax.random.normal(kk, shape, f32) * s
    return {
        "x": nrm(k[0], (BATCH, SEQ, D_MODEL), 1.0),
        "norm1_g": 1.0 + nrm(k[1], (DEPTH, D_MODEL), 0.05),
        "w_in": nrm(k[2], (DEPTH, D_MODEL, D_IN), D_MODEL ** -0.5),
        "pool_w": nrm(k[3], (DEPTH, N_POOL_GROUPS, POOL_GROUP, POOL_GROUP), POOL_GROUP ** -0.5),
        "pool_scale": 1.0 + nrm(k[4], (DEPTH, D_POOL), 0.1),
        "gm_norm_g": 1.0 + nrm(k[5], (DEPTH, D_GMLP), 0.05),
        "gm_ws": nrm(k[6], (DEPTH, GMLP_HEADS, GMLP_BLOCK, GMLP_BLOCK), 0.5 * GMLP_BLOCK ** -0.5),
        "gm_b": 1.0 + nrm(k[7], (DEPTH, GMLP_HEADS, GMLP_BLOCK), 0.1),
        "conv_dw_w": nrm(k[8], (DEPTH, CONV_WIDTH, D_CONV), CONV_WIDTH ** -0.5),
        "conv_dw_b": nrm(k[9], (DEPTH, D_CONV), 0.02),
        "conv_ln_g": 1.0 + nrm(k[10], (DEPTH, D_CONV), 0.05),
        "conv_ln_b": nrm(k[11], (DEPTH, D_CONV), 0.02),
        "conv_pw_w": nrm(k[12], (DEPTH, D_CONV, D_CONV), D_CONV ** -0.5),
        "conv_pw_b": nrm(k[13], (DEPTH, D_CONV), 0.02),
        "w_out": nrm(k[14], (DEPTH, D_MIX, D_MODEL), D_MIX ** -0.5),
        "norm2_g": 1.0 + nrm(k[15], (DEPTH, D_MODEL), 0.05),
        "ffn_wg": nrm(k[16], (N_DENSE, D_MODEL, D_FF), D_MODEL ** -0.5),
        "ffn_wu": nrm(k[17], (N_DENSE, D_MODEL, D_FF), D_MODEL ** -0.5),
        "ffn_wd": nrm(k[18], (N_DENSE, D_FF, D_MODEL), D_FF ** -0.5),
        "moe_router": nrm(k[19], (N_MOE, D_MODEL, N_EXPERTS), D_MODEL ** -0.5),
        "moe_wg": nrm(k[20], (N_MOE, N_EXPERTS, D_MODEL, D_FF_EXPERT), D_MODEL ** -0.5),
        "moe_wu": nrm(k[21], (N_MOE, N_EXPERTS, D_MODEL, D_FF_EXPERT), D_MODEL ** -0.5),
        "moe_wd": nrm(k[22], (N_MOE, N_EXPERTS, D_FF_EXPERT, D_MODEL), D_FF_EXPERT ** -0.5),
        "final_g": 1.0 + nrm(k[23], (D_MODEL,), 0.05),
    }

def first_block(x, norm1_g, w_in, pool_w, pool_scale, gm_norm_g, gm_ws, gm_b,
              conv_dw_w, conv_dw_b, conv_ln_g, conv_ln_b, conv_pw_w, conv_pw_b,
              w_out, norm2_g, ffn_wg, ffn_wu, ffn_wd,
              moe_router, moe_wg, moe_wu, moe_wd, final_g):
    splits = [D_POOL, D_POOL + D_GMLP, D_POOL + 2 * D_GMLP,
              D_POOL + 2 * D_GMLP + D_CONV]
    for l in range(DEPTH):
        h = rms_norm(x, norm1_g[l])
        p = h @ w_in[l]
        a, u, v, cv, cg = jnp.split(p, splits, axis=-1)
        ya = pool_mixer(a, pool_w[l], pool_scale[l])
        yb = gmlp_mixer(u, v, gm_norm_g[l], gm_ws[l], gm_b[l])
        yc = conv_module(cv, cg, conv_dw_w[l], conv_dw_b[l], conv_ln_g[l],
                         conv_ln_b[l], conv_pw_w[l], conv_pw_b[l])
        x = x + jnp.concatenate([ya, yb, yc], axis=-1) @ w_out[l]
        h = rms_norm(x, norm2_g[l])
        if l % 2 == 0:
            j = l // 2
            x = x + swiglu(h, ffn_wg[j], ffn_wu[j], ffn_wd[j])
        else:
            j = l // 2
            x = x + moe_swiglu(h, moe_router[j], moe_wg[j], moe_wu[j], moe_wd[j])
    return rms_norm(x, final_g)


HEAD_DIM = 64
SWA_Q_HEADS = 8
SWA_KV_HEADS = 2
SWA_G = SWA_Q_HEADS // SWA_KV_HEADS
DSA_Q_HEADS = 8
DSA_KV_HEADS = 1
DSA_G = DSA_Q_HEADS // DSA_KV_HEADS
IDX_HEADS = 8
IDX_DIM = 32
TOPK_MAX = 256
WINDOW = 128
BLOCK = 128
ROPE_THETA = 10000.0
PLE_DIM = 256
MIX_WIDTH = (SWA_Q_HEADS + DSA_Q_HEADS) * HEAD_DIM
D_FF_2 = -(-(8 * D_MODEL) // (3 * 256)) * 256
DN_ALPHA = (2 * DEPTH) ** 0.25
DN_BETA = (8 * DEPTH) ** -0.25
LN_EPS = 1e-5
NEG = -1e30
IN_SIZES = (SWA_Q_HEADS * HEAD_DIM, SWA_KV_HEADS * HEAD_DIM, SWA_KV_HEADS * HEAD_DIM,
            DSA_Q_HEADS * HEAD_DIM, DSA_KV_HEADS * HEAD_DIM, DSA_KV_HEADS * HEAD_DIM,
            IDX_HEADS * IDX_DIM, IDX_DIM, IDX_HEADS)
IN_COLS = sum(IN_SIZES)


def layer_norm_2(x, g, b):
    xf = x.astype(jnp.float32)
    mu = xf.mean(-1, keepdims=True)
    var = jnp.square(xf - mu).mean(-1, keepdims=True)
    y = (xf - mu) * lax.rsqrt(var + LN_EPS)
    return (y * g.astype(jnp.float32) + b.astype(jnp.float32)).astype(x.dtype)

def rope(x, positions):
    half = x.shape[-1] // 2
    inv = ROPE_THETA ** (-jnp.arange(half, dtype=jnp.float32) / half)
    ang = positions.astype(jnp.float32)[..., None] * inv
    ang = ang.reshape(ang.shape[:2] + (1,) * (x.ndim - 3) + (half,))
    cos, sin = jnp.cos(ang), jnp.sin(ang)
    x1 = x[..., :half].astype(jnp.float32)
    x2 = x[..., half:].astype(jnp.float32)
    return jnp.concatenate([x1 * cos - x2 * sin, x2 * cos + x1 * sin], -1).astype(x.dtype)

def swa_sink_attention(q, k, v, sinks):
    B, S, Hkv, G, D = q.shape
    nb = S // BLOCK
    qb = q.reshape(B, nb, BLOCK, Hkv, G, D)
    kb = k.reshape(B, nb, BLOCK, Hkv, D)
    vb = v.reshape(B, nb, BLOCK, Hkv, D)
    prev = lambda t: jnp.concatenate([jnp.zeros_like(t[:, :1]), t[:, :-1]], axis=1)
    kk = jnp.concatenate([prev(kb), kb], axis=2)
    vv = jnp.concatenate([prev(vb), vb], axis=2)
    s = jnp.einsum('bnqhgd,bnkhd->bnhgqk', qb, kk).astype(jnp.float32) * (D ** -0.5)
    i = jnp.arange(BLOCK)[:, None]
    j = jnp.arange(2 * BLOCK)[None, :]
    diff = BLOCK + i - j
    band = (diff >= 0) & (diff < WINDOW)
    not_pad = (jnp.arange(nb)[:, None, None] > 0) | (j[None] >= BLOCK)
    mask = band[None] & not_pad
    s = jnp.where(mask[None, :, None, None], s, NEG)
    sink = sinks.astype(jnp.float32)[None, None, :, :, None, None]
    m = jnp.maximum(s.max(-1, keepdims=True), sink)
    pr = jnp.exp(s - m)
    denom = pr.sum(-1, keepdims=True) + jnp.exp(sink - m)
    o = jnp.einsum('bnhgqk,bnkhd->bnqhgd', (pr / denom).astype(v.dtype), vv)
    return o.reshape(B, S, Hkv * G * D)

def dsa_sparse_attention(q, k, v, qi, ki, wi, k_top):
    B, S, Hkv, G, D = q.shape
    nb = S // BLOCK
    to_blocks = lambda t: jnp.moveaxis(t.reshape((B, nb, BLOCK) + t.shape[2:]), 1, 0)
    gather = jax.vmap(lambda kv, ix: kv[ix])
    key_pos = jnp.arange(S)

    def one_block(args):
        n, qb, qib, wib = args
        t = n * BLOCK + jnp.arange(BLOCK)
        sc = jnp.einsum('bqhd,bsd->bqhs', qib, ki).astype(jnp.float32)
        idx_score = jnp.einsum('bqhs,bqh->bqs', jax.nn.relu(sc), wib.astype(jnp.float32))
        causal = key_pos[None, :] <= t[:, None]
        idx_score = jnp.where(causal[None], idx_score, NEG)
        _, sel = lax.top_k(idx_score, k_top)
        ks = gather(k, sel)
        vs = gather(v, sel)
        s = jnp.einsum('bqhgd,bqjhd->bqhgj', qb, ks).astype(jnp.float32) * (D ** -0.5)
        valid = sel <= t[None, :, None]
        s = jnp.where(valid[:, :, None, None, :], s, NEG)
        pr = jax.nn.softmax(s, axis=-1)
        o = jnp.einsum('bqhgj,bqjhd->bqhgd', pr.astype(v.dtype), vs)
        return o.reshape(B, BLOCK, Hkv * G * D)

    out = lax.map(one_block, (jnp.arange(nb), to_blocks(q), to_blocks(qi), to_blocks(wi)))
    return jnp.moveaxis(out, 0, 1).reshape(B, S, Hkv * G * D)

def hybrid_layer(x, p_i, positions, w_in, sinks, idx_k_g, idx_k_b, w_o, ln1_g, ln1_b,
                 w_gu, w_down, w_pg, w_pp, ln2_g, ln2_b):
    B, S, _ = x.shape
    k_top = min(TOPK_MAX, S // 4)
    h = x @ w_in
    cuts = [int(c) for c in np.cumsum(IN_SIZES)[:-1]]
    qa, ka, va, qb, kb, vb, qi, ki, wi = jnp.split(h, cuts, axis=-1)
    qa = rope(qa.reshape(B, S, SWA_KV_HEADS, SWA_G, HEAD_DIM), positions)
    ka = rope(ka.reshape(B, S, SWA_KV_HEADS, HEAD_DIM), positions)
    va = va.reshape(B, S, SWA_KV_HEADS, HEAD_DIM)
    qb = rope(qb.reshape(B, S, DSA_KV_HEADS, DSA_G, HEAD_DIM), positions)
    kb = rope(kb.reshape(B, S, DSA_KV_HEADS, HEAD_DIM), positions)
    vb = vb.reshape(B, S, DSA_KV_HEADS, HEAD_DIM)
    qi = rope(qi.reshape(B, S, IDX_HEADS, IDX_DIM), positions)
    ki = rope(layer_norm_2(ki, idx_k_g, idx_k_b), positions)
    wi = wi * (IDX_HEADS ** -0.5 * IDX_DIM ** -0.5)
    oa = swa_sink_attention(qa, ka, va, sinks.reshape(SWA_KV_HEADS, SWA_G))
    ob = dsa_sparse_attention(qb, kb, vb, qi, ki, wi, k_top)
    mix = jnp.concatenate([oa, ob], axis=-1) @ w_o
    x = layer_norm_2(DN_ALPHA * x + mix, ln1_g, ln1_b)
    g, u = jnp.split(x @ w_gu, 2, axis=-1)
    ffn = (jax.nn.silu(g) * u) @ w_down
    ple = (p_i @ w_pp) * jax.nn.sigmoid(x @ w_pg)
    return layer_norm_2(DN_ALPHA * x + ffn + ple, ln2_g, ln2_b)

def second_inputs(seed: int = 0) -> dict:
    key = jax.random.key(seed)
    ks = jax.random.split(key, 20)
    nrm = lambda k, shape, scale: jax.random.normal(k, shape, jnp.float32) * scale
    L = DEPTH
    offs = jax.random.randint(ks[2], (BATCH, 1), 0, 1024)
    positions = (offs + jnp.arange(SEQ)[None, :]).astype(jnp.int32)
    return {
        "x": nrm(ks[0], (BATCH, SEQ, D_MODEL), 1.0),
        "p": nrm(ks[1], (DEPTH, BATCH, SEQ, PLE_DIM), 1.0),
        "positions": positions,
        "ln_in_g": 1.0 + nrm(ks[3], (D_MODEL,), 0.02),
        "ln_in_b": nrm(ks[4], (D_MODEL,), 0.02),
        "w_in": nrm(ks[5], (L, D_MODEL, IN_COLS), D_MODEL ** -0.5),
        "attn_sinks": nrm(ks[6], (L, SWA_Q_HEADS), 0.5),
        "idx_k_g": 1.0 + nrm(ks[7], (L, IDX_DIM), 0.02),
        "idx_k_b": nrm(ks[8], (L, IDX_DIM), 0.02),
        "w_o": nrm(ks[9], (L, MIX_WIDTH, D_MODEL), DN_BETA * MIX_WIDTH ** -0.5),
        "ln1_g": 1.0 + nrm(ks[10], (L, D_MODEL), 0.02),
        "ln1_b": nrm(ks[11], (L, D_MODEL), 0.02),
        "w_gu": nrm(ks[12], (L, D_MODEL, 2 * D_FF_2), D_MODEL ** -0.5),
        "w_down": nrm(ks[13], (L, D_FF_2, D_MODEL), DN_BETA * D_FF_2 ** -0.5),
        "w_pg": nrm(ks[14], (L, D_MODEL, D_MODEL), D_MODEL ** -0.5),
        "w_pp": nrm(ks[15], (L, PLE_DIM, D_MODEL), DN_BETA * PLE_DIM ** -0.5),
        "ln2_g": 1.0 + nrm(ks[16], (L, D_MODEL), 0.02),
        "ln2_b": nrm(ks[17], (L, D_MODEL), 0.02),
    }

def second_block(x, p, positions, ln_in_g, ln_in_b, w_in, attn_sinks, idx_k_g, idx_k_b, w_o,
              ln1_g, ln1_b, w_gu, w_down, w_pg, w_pp, ln2_g, ln2_b):
    x = layer_norm_2(x, ln_in_g, ln_in_b)
    for i in range(DEPTH):
        x = hybrid_layer(x, p[i], positions, w_in[i], attn_sinks[i], idx_k_g[i], idx_k_b[i],
                         w_o[i], ln1_g[i], ln1_b[i], w_gu[i], w_down[i], w_pg[i], w_pp[i],
                         ln2_g[i], ln2_b[i])
    return x


def setup_inputs(seed=0):
    out = dict(first_inputs(seed))
    for name, value in second_inputs(seed + 1).items():
        if name != "x":
            out[name + "_2"] = value
    return out


def reference(
    x, norm1_g, w_in, pool_w, pool_scale, gm_norm_g, gm_ws, gm_b, conv_dw_w, conv_dw_b,
    conv_ln_g, conv_ln_b, conv_pw_w, conv_pw_b, w_out, norm2_g, ffn_wg, ffn_wu, ffn_wd,
    moe_router, moe_wg, moe_wu, moe_wd, final_g, p_2, positions_2, ln_in_g_2, ln_in_b_2, w_in_2,
    attn_sinks_2, idx_k_g_2, idx_k_b_2, w_o_2, ln1_g_2, ln1_b_2, w_gu_2, w_down_2, w_pg_2,
    w_pp_2, ln2_g_2, ln2_b_2,
):
    x = first_block(
        x, norm1_g, w_in, pool_w, pool_scale, gm_norm_g, gm_ws, gm_b, conv_dw_w, conv_dw_b,
        conv_ln_g, conv_ln_b, conv_pw_w, conv_pw_b, w_out, norm2_g, ffn_wg, ffn_wu, ffn_wd,
        moe_router, moe_wg, moe_wu, moe_wd, final_g,
    )
    return second_block(
        x, p_2, positions_2, ln_in_g_2, ln_in_b_2, w_in_2, attn_sinks_2, idx_k_g_2, idx_k_b_2,
        w_o_2, ln1_g_2, ln1_b_2, w_gu_2, w_down_2, w_pg_2, w_pp_2, ln2_g_2, ln2_b_2,
    )


_drawn_inputs = setup_inputs


def setup_inputs(seed=0):
    import zlib

    import numpy as np

    out = dict(_drawn_inputs(seed))
    spreads = {}
    factors = {'attn_sinks_2': 8.0, 'idx_k_g_2': 8.0, 'idx_k_b_2': 8.0}
    for name, (base, spread) in spreads.items():
        noise = np.random.default_rng([zlib.crc32(name.encode()), seed]).standard_normal(out[name].shape)
        drawn = base * np.exp(spread * noise) if base else spread * noise
        out[name] = __import__('jax').numpy.asarray(drawn.astype(out[name].dtype))
    for name, factor in factors.items():
        out[name] = (out[name] * factor).astype(out[name].dtype)
    return out
```

```python
from contextlib import ExitStack

import numpy as np

import concourse.bass as bass
from concourse import mybir


P128 = 128
SEQ, D = 256, 1024
NB = SEQ // P128
KT = D // P128
DEPTH = 2
D_POOL, D_GM, D_CONV = 256, 384, 384
WINDOWS = (2, 4, 8, 16)
GROUP = D_POOL // len(WINDOWS)
GM_HEADS = 4
GM_HD = D_GM // GM_HEADS
CHUNK = 64
TAPS = 31
D_IN = D_POOL + 2 * D_GM + 2 * D_CONV
U0, V0 = D_POOL, D_POOL + D_GM
CV0, CG0 = V0 + D_GM, V0 + D_GM + D_CONV
D_FF, D_FF_E, EXPERTS = 2816, 3584, 8
EPS, LN_EPS = 1e-6, 1e-5
HD, Q_HEADS = 64, 8
IDX_HEADS, IDX_DIM = 8, 32
PLE = 256
TOPK = 64
ALPHA = (2 * DEPTH) ** 0.25
NEG, TAKEN = -1e30, -3e38
QA, KA, VA = 0, 512, 640
QB, KB, VB = 768, 1280, 1344
QI, KI, WI = 1408, 1664, 1696
IN2 = 1704
C1, C2 = D_IN // 4, IN2 // 4
FN = 256
STEPS, STEPS_E = D_FF // FN, D_FF_E // FN
MOE_STEP0 = STEPS
B2_STEP0 = MOE_STEP0 + EXPERTS * STEPS_E
R_N1, R_N2, R_DWB, R_LNG, R_LNB, R_PWB, R_PSC, R_DW = 0, 2, 4, 6, 8, 10, 12, 14
R_GMB = R_DW + DEPTH * TAPS
ROWS = R_GMB + DEPTH * GM_HEADS


def shape_constants():
    f32 = np.float32
    s = np.arange(SEQ)
    band = np.zeros((SEQ, len(WINDOWS), SEQ), f32)
    for g, w in enumerate(WINDOWS):
        inside = (s[:, None] <= s[None, :]) & (s[None, :] - s[:, None] < w)
        band[:, g] = inside / np.minimum(s + 1, w)[None, :].astype(f32) - np.eye(SEQ)
    i = np.arange(P128)
    causal = np.where(i[None, :] <= i[:, None], 0.0, NEG)
    older = np.where(i[None, :] > i[:, None], 0.0, NEG)
    masks = np.stack([np.concatenate([older, causal], 1),
                      np.concatenate([np.zeros_like(causal), causal], 1)], 1).astype(f32)
    freq = np.concatenate([
        f32(10000.0) ** (-np.arange(h, dtype=f32) / f32(h)) for h in (HD // 2, IDX_DIM // 2)]).astype(f32)
    e = np.arange(EXPERTS)
    lower = (e[None, :] < e[:, None]).astype(f32).reshape(1, -1)
    return {"c_ident": np.eye(P128, dtype=f32), "c_band": band, "c_masks": masks,
            "c_freq": freq.reshape(1, -1), "c_lower": lower}


def build_program(nc, T):
    f32 = mybir.dt.float32
    ALU = mybir.AluOpType
    ACT = mybir.ActivationFunctionType
    AX = mybir.AxisListType

    ctx = ExitStack()
    with ctx:
        def sb(name, shape, dt=f32):
            return ctx.enter_context(nc.sbuf_tensor(name, shape, dt))

        def sem(name):
            return ctx.enter_context(nc.semaphore(name))

        ident = sb("ident", [128, 128])
        band = sb("band", [128, NB, 4, SEQ])
        masks = sb("masks", [128, 2, 256])
        freq = sb("freq", [128, 48])
        lower = sb("lower", [128, EXPERTS, EXPERTS])
        parc = sb("parc", [128, KT, ROWS])
        router = sb("router", [128, KT, EXPERTS])
        poolw = sb("poolw", [128, DEPTH, 2, 128])
        wst = sb("wst", [128, DEPTH, GM_HEADS, 128])
        gmg = sb("gmg", [128, DEPTH, D_GM])
        sink = sb("sink", [128, DEPTH, Q_HEADS])
        ikg = sb("ikg", [128, DEPTH, IDX_DIM])
        ikb = sb("ikb", [128, DEPTH, IDX_DIM])
        pin = sb("pin", [128, NB, PLE])
        lnp = sb("lnp", [128, DEPTH, 4, D])
        lni = sb("lni", [128, 3, D])
        X = sb("X", [128, NB, D])
        hT = sb("hT", [128, KT, SEQ])
        XN = sb("XN", [128, NB, D])
        ringA = sb("ringA", [128, 2, 4096])
        ringD = sb("ringD", [128, 2, 2048])
        sil = sb("sil", [128, 2, NB, FN])
        am = sb("am", [128, 2, NB, FN])
        aT = sb("aT", [128, 2, 2, SEQ])
        gates = sb("gates", [128, NB, EXPERTS])
        cosA = sb("cosA", [128, NB, HD])
        sinA = sb("sinA", [128, NB, HD])
        cosI = sb("cosI", [128, NB, IDX_DIM])
        sinI = sb("sinI", [128, NB, IDX_DIM])
        small = sb("small", [128, 512])
        posi = sb("posi", [128, NB], mybir.dt.int32)
        SCR = sb("SCR", [128, 16600])
        ps = ctx.enter_context(nc.psum_tensor("ps", [128, 8, 512], f32))
        psf = ps[:, :, :].rearrange("p b n -> p (b n)")

        taken = [0]

        def col(n):
            taken[0] += n
            assert taken[0] <= 512
            return small[:, taken[0] - n:taken[0]]

        eps1, eps2, spare = col(1), col(1), col(1)
        ss, std, rstd = col(2), col(2), col(2)
        gm_ss, gm_std, gm_rstd = col(2), col(2), col(2)
        bst = col(2 * 2 * 6).rearrange("p (b c s) -> p b c s", b=2, c=2)
        mv = col(4).rearrange("p (b s) -> p b s", b=2)
        lstd, lrstd = col(2), col(2)
        posf = col(2)
        logit = col(16).rearrange("p (b e) -> p b e", b=2)
        gmax, gneg, gden, grec = col(2), col(2), col(2), col(2)
        gexp = col(16).rearrange("p (b e) -> p b e", b=2)
        rank = col(16).rearrange("p (b e) -> p b e", b=2)
        swa_m, swa_nm, swa_es, swa_den, swa_rd = (col(8) for _ in range(5))
        dsa_m, dsa_nm, dsa_den, dsa_rd = (col(8) for _ in range(4))
        top8 = col(8)
        wi = col(16).rearrange("p (b e) -> p b e", b=2)

        at = [0]

        def scr(n):
            at[0] += n
            assert at[0] <= 16600
            return SCR[:, at[0] - n:at[0]]

        Pm = scr(2 * D_IN).rearrange("p (b n) -> p b n", b=2)
        GH = scr(2 * D_CONV).rearrange("p (b n) -> p b n", b=2)
        CT = scr(3 * (SEQ + TAPS - 1)).rearrange("p (t n) -> p t n", t=3)
        ACC = scr(3 * SEQ).rearrange("p (t n) -> p t n", t=3)
        CN = scr(2 * D_CONV).rearrange("p (b n) -> p b n", b=2)
        HC = scr(3 * SEQ).rearrange("p (t n) -> p t n", t=3)
        GV = scr(2 * D_GM).rearrange("p (b n) -> p b n", b=2)
        YB = scr(2 * D_GM).rearrange("p (b n) -> p b n", b=2)
        YT = scr(2 * SEQ).rearrange("p (t n) -> p t n", t=2)
        MT = scr(KT * SEQ).rearrange("p (t n) -> p t n", t=KT)
        at[0] = 0
        par = scr(D)
        wsr = scr(DEPTH * GM_HEADS * 128).rearrange("p (l h n) -> p l h n", l=DEPTH, h=GM_HEADS)
        at[0] = 12000
        ang = scr(2 * 48).rearrange("p (b n) -> p b n", b=2)
        turn = scr(2 * 2 * 48).rearrange("p (c b n) -> p c b n", c=2, b=2)
        arg = scr(2 * 2 * 48).rearrange("p (c b n) -> p c b n", c=2, b=2)
        trig = scr(2 * 2 * 48).rearrange("p (c b n) -> p c b n", c=2, b=2)
        at[0] = 0
        P2 = scr(2 * IN2).rearrange("p (b n) -> p b n", b=2)
        region = at[0]
        RQ = scr(2 * 16 * HD).rearrange("p (b h d) -> p b h d", b=2, h=16)
        RK = scr(2 * 6 * HD).rearrange("p (b k u d) -> p b k u d", b=2, k=3, u=2)
        RQI = scr(2 * 256).rearrange("p (b h d) -> p b h d", b=2, h=8)
        RKI = scr(2 * 128).rearrange("p (b u d) -> p b u d", b=2, u=4)
        at[0] = region
        Sswa = scr(2048)
        Sdsa = scr(2048)
        TT = scr(14 * SEQ).rearrange("p (t n) -> p t n", t=14)
        pt_om = at[0]
        PT = scr(2048).rearrange("p (k h q) -> p k h q", k=2, h=8)
        OM = scr(2048).rearrange("p (b n) -> p b n", b=2)
        at[0] = pt_om
        T2 = scr(2 * 19 * HD).rearrange("p (b h c d) -> p b h c d", b=2, h=19, c=2)
        T2I = scr(2 * 8 * 32).rearrange("p (b h c d) -> p b h c d", b=2, h=8, c=2)
        T2K = scr(2 * 32).rearrange("p (b c d) -> p b c d", b=2, c=2)
        KN = scr(2 * 32).rearrange("p (b d) -> p b d", b=2)
        at[0] = pt_om + 4096
        score = scr(256)
        work = scr(256)
        dbias = scr(256)
        PPT = scr(2 * SEQ).rearrange("p (k n) -> p k n", k=2)
        MT2 = PT.rearrange("p k h q -> p (k h q)").rearrange("p (t n) -> p t n", t=KT)
        SGP = Sswa
        PLEO = Sdsa
        RL = XN[:, :, :].rearrange("p b n -> p (b n)")

        ident_loaded, x_loaded, par_loaded, mixer_loaded, attn_loaded, ln_loaded, pin_loaded = (
            sem(n) for n in ("ident_loaded", "x_loaded", "par_loaded", "mixer_loaded", "attn_loaded", "ln_loaded",
                             "pin_loaded"))
        zeroed = sem("zeroed")
        A_loaded = [sem("A_loaded0"), sem("A_loaded1")]
        D_loaded = [sem("D_loaded0"), sem("D_loaded1")]
        stored = sem("stored")
        pool_chain, act_chain, dve_chain = sem("pool_chain"), sem("act_chain"), sem("dve_chain")
        par_psum, parc_ready, wst_psum, wst_ready = sem("par_psum"), sem("parc_ready"), sem("wst_psum"), sem("wst_ready")
        args_ready, trig_ready, rope_tables = sem("args_ready"), sem("trig_ready"), sem("rope_tables")
        std_ready, xn_ready, hT_psum, hT_ready = sem("std_ready"), sem("xn_ready"), sem("hT_psum"), sem("hT_ready")
        proj_psum, proj_evac = sem("proj_psum"), sem("proj_evac")
        sg_ready, glu_ready, gluT_psum, ct_ready = sem("sg_ready"), sem("glu_ready"), sem("gluT_psum"), sem("ct_ready")
        gm_std_ready, gm_rstd_ready, gn_ready, gv_ready = sem("gm_std_ready"), sem("gm_rstd_ready"), sem("gn_ready"), sem("gv_ready")
        pool1_psum, yt_ready, pool2_psum, mt_ready = sem("pool1_psum"), sem("yt_ready"), sem("pool2_psum"), sem("mt_ready")
        z_psum, zb_ready, yb_ready, ybT_psum = sem("z_psum"), sem("zb_ready"), sem("yb_ready"), sem("ybT_psum")
        conv_ready, cl_psum, cl_var, cl_std, cn_ready, cnT_psum, hc_ready, pw_psum = (
            sem(n) for n in ("conv_ready", "cl_psum", "cl_var", "cl_std", "cn_ready", "cnT_psum", "hc_ready", "pw_psum"))
        mix_psum, x_ready = sem("mix_psum"), sem("x_ready")
        router_psum = sem("router_psum")
        gl_ready, ge_ready = sem("gl_ready"), sem("ge_ready")
        gu_psum, silu_ready, act_ready, aT_psum, aT_ready, down_done, ffn_evac = (
            sem(n) for n in ("gu_psum", "silu_ready", "act_ready", "aT_psum", "aT_ready", "down_done", "ffn_evac"))
        ln_var, ln_std, xln_ready = sem("ln_var"), sem("ln_std"), sem("xln_ready")
        ik_var, ik_std, cos_part, rope_ready = sem("ik_var"), sem("ik_std"), sem("cos_part"), sem("rope_ready")
        qkT_psum, qkT_act, qkT_dve = sem("qkT_psum"), sem("qkT_act"), sem("qkT_dve")
        idx_psum, relu_ready, swa_psum, dsa_psum = sem("idx_psum"), sem("relu_ready"), sem("swa_psum"), sem("dsa_psum")
        swa_scored, dsa_scored = sem("swa_scored"), sem("dsa_scored")
        swa_exp, dsa_exp, pt_psum, pt_ready = sem("swa_exp"), sem("dsa_exp"), sem("pt_psum"), sem("pt_ready")
        pv_psum, om_ready, omT_psum, mt2_act, mt2_dve = (
            sem(n) for n in ("pv_psum", "om_ready", "omT_psum", "mt2_act", "mt2_dve"))
        pT_psum, pT_ready, pg_psum, pp_psum, sgp_ready, ple_read = (
            sem(n) for n in ("pT_psum", "pT_ready", "pg_psum", "pp_psum", "sgp_ready", "ple_read"))

        class Chain:

            def __init__(self, eng, s):
                self.eng, self.s, self.base, self.n, self.outer = eng, s, 0, 0, []

            def then(self, ins):
                self.n += 1
                ins.then_inc(self.s, 1)

            def wait(self, back=0):
                self.eng.wait_ge(self.s, self.base + self.n - back)

            def link(self, ins):
                self.then(ins)
                self.wait()

            def enter(self, turn, per):
                self.outer.append((self.base, self.n))
                self.base, self.n = (self.base + self.n) + turn * per, 0

            def leave(self, per, turns):
                assert self.n == per, (self.n, per)
                self.base, self.n = self.outer.pop()
                self.n += per * turns

        def place(h):
            return (h % 2) * 4 + h // 2

        def wait(eng, s, value):
            if not isinstance(value, int) or value > 0:
                eng.wait_ge(s, value)

        block = ctx.enter_context(nc.Block())

        @block.sync
        def _(sp):
            def cut(w, e, r0, rows, c0, n):
                return w[bass.ds(e, 1), bass.ds(r0, rows), bass.ds(c0, n)].rearrange("o (k p) n -> p (o k) n", p=128)

            def columns(slot, w, e, c0, n):
                dst = ringA[:, slot, 0:KT * n].rearrange("p (k n) -> p k n", k=KT)
                sp.dma_start(dst, cut(w, e, 0, D, c0, n)).then_inc(A_loaded[slot], 32)

            def gate_up(slot, wg, wu, e, cg, cu):
                dst = ringA[:, slot, :].rearrange("p (k u n) -> p k u n", k=KT, u=2)
                sp.dma_start(dst[:, :, 0, :], cut(wg, e, 0, D, cg, FN)).then_inc(A_loaded[slot], 16)
                sp.dma_start(dst[:, :, 1, :], cut(wu, e, 0, D, cu, FN)).then_inc(A_loaded[slot], 16)

            def rows(slot, w, e, r0):
                dst = ringD[:, slot, :].rearrange("p (k n) -> p k n", k=2)
                sp.dma_start(dst, cut(w, e, r0, FN, 0, D)).then_inc(D_loaded[slot], 16)

            def feed_forward(wg, wu, wd, e, up0, s0, n):
                gate_up(1, wg, wu, e, FN, up0 + FN)
                wait(sp, down_done, s0 - 1)
                rows(1, wd, e, 0)
                with sp.Fori(0, (n - 2) // 2) as i:
                    for j in range(2):
                        step = 2 * i + 2 + j
                        sp.wait_ge(gu_psum, s0 + 2 * i + j + 1)
                        gate_up(j, wg, wu, e, step * FN, step * FN + up0)
                        wait(sp, down_done, s0 + 2 * i + j)
                        rows(j, wd, e, (step - 1) * FN)
                if n % 2:
                    sp.wait_ge(gu_psum, s0 + n - 2)
                    gate_up(0, wg, wu, e, (n - 1) * FN, (n - 1) * FN + up0)
                    sp.wait_ge(down_done, s0 + n - 3)
                    rows(0, wd, e, (n - 2) * FN)
                sp.wait_ge(down_done, s0 + n - 2)
                rows(n % 2, wd, e, (n - 1) * FN)

            for l in range(DEPTH):
                for c in range(4):
                    if c >= 2:
                        sp.wait_ge(proj_psum, 4 * l + c - 1)
                    elif l:
                        sp.wait_ge(gu_psum, STEPS)
                    columns(c % 2, T["w_in"], l, D_IN - C1 * (c + 1), C1)
                if l:
                    sp.wait_ge(down_done, STEPS)
                sp.dma_start(ringD[:, 0, 0:3 * D_CONV].rearrange("p (k n) -> p k n", k=3),
                             cut(T["conv_pw_w"], l, 0, D_CONV, 0, D_CONV)).then_inc(D_loaded[0], 16)
                for n in range(2):
                    sp.wait_ge(proj_psum, 4 * l + n + 3)
                    columns(n, T["w_out"], l, 512 * n, 512)
                if l == 0:
                    sp.wait_ge(mix_psum, 1)
                    gate_up(0, T["ffn_wg"], T["ffn_wu"], 0, 0, 0)
                    sp.wait_ge(mix_psum, 2)
                    feed_forward(T["ffn_wg"], T["ffn_wu"], T["ffn_wd"], 0, 0, 0, STEPS)
            EG, EU, ED = T["moe_wg"], T["moe_wu"], T["moe_wd"]
            sp.wait_ge(mix_psum, 3)
            gate_up(0, EG, EU, 0, 0, 0)
            sp.wait_ge(mix_psum, 4)
            feed_forward(EG, EU, ED, 0, 0, MOE_STEP0, STEPS_E)
            with sp.Fori(1, EXPERTS) as e:
                s0 = MOE_STEP0 + STEPS_E * e
                sp.wait_ge(gu_psum, s0 - 1)
                gate_up(0, EG, EU, e, 0, 0)
                sp.wait_ge(gu_psum, s0)
                feed_forward(EG, EU, ED, e, 0, s0, STEPS_E)
            with sp.Fori(0, DEPTH) as l:
                q = l + 2
                s0 = B2_STEP0 + STEPS * l
                sp.wait_ge(gu_psum, s0)
                for c in range(4):
                    if c >= 2:
                        sp.wait_ge(proj_psum, 4 * q + c - 1)
                    columns(c % 2, T["w_in_2"], l, C2 * c, C2)
                sp.wait_ge(down_done, s0)
                rows(0, T["w_pp_2"], l, 0)
                sp.dma_start(pin[:, :, :], T["p_2"][bass.ds(l, 1), 0, :, :].rearrange("o (b p) n -> p (o b) n", p=128)
                             ).then_inc(pin_loaded, 16)
                for n in range(2):
                    sp.wait_ge(proj_psum, 4 * q + n + 3)
                    columns(n, T["w_o_2"], l, 512 * n, 512)
                for n in range(2):
                    sp.wait_ge(mix_psum, 2 * q + n + 1)
                    columns(n, T["w_pg_2"], l, 512 * n, 512)
                sp.wait_ge(pg_psum, 2 * l + 1)
                gate_up(0, T["w_gu_2"], T["w_gu_2"], l, 0, D_FF)
                sp.wait_ge(pp_psum, l + 1)
                feed_forward(T["w_gu_2"], T["w_gu_2"], T["w_down_2"], l, D_FF, s0, STEPS)
            sp.wait_ge(xln_ready, 1 + 2 * DEPTH)
            sp.dma_start(T["out"].rearrange("o (b p) d -> p (o b) d", p=128), X[:, :, :]).then_inc(stored, 16)
            sp.wait_ge(stored, 16)

        @block.tensor
        def _(pe):
            mm = nc.tensor.matmul

            def tr(out, in_, n=128):
                return nc.tensor.transpose(out, in_, ident[0:n, 0:n])

            def slotA(slot, n):
                return ringA[:, slot, 0:KT * n].rearrange("p (k n) -> p k n", k=KT)

            def to_features(t, src):
                for k in range(KT):
                    for b in range(NB):
                        c = (k % 2) * SEQ + b * 128
                        m = tr(ps[:, k // 2, c:c + 128], src[:, b, k * 128:(k + 1) * 128])
                    if k % 2:
                        m.then_inc(hT_psum, 1)
                pe.wait_ge(hT_ready, 8 * (t + 1))

            def project(q, c, n, use):
                pe.wait_ge(A_loaded[c % 2], 32 * use)
                if c >= 2:
                    pe.wait_ge(proj_evac, 4 * q + c - 1)
                w = slotA(c % 2, n)
                for k in range(KT):
                    for b in range(NB):
                        m = mm(ps[:, 4 + 2 * (c % 2) + b, 0:n], hT[:, k, b * 128:(b + 1) * 128], w[:, k, :],
                               start=(k == 0), stop=(k == KT - 1))
                m.then_inc(proj_psum, 1)

            def full_depth(lhs, slot, use, bank_of, done):
                pe.wait_ge(A_loaded[slot], 32 * use)
                w = slotA(slot, 512)
                for k in range(KT):
                    for b in range(NB):
                        m = mm(ps[:, bank_of(b), :], lhs[:, k, b * 128:(b + 1) * 128], w[:, k, :],
                               start=(k == 0), stop=(k == KT - 1))
                m.then_inc(done, 1)

            def up(s, par_, use, reused=True):
                pe.wait_ge(A_loaded[par_], 32 * use)
                if reused:
                    pe.wait_ge(aT_ready, s - 1)
                w = slotA(par_, 512)
                for k in range(KT):
                    for b in range(NB):
                        m = mm(ps[:, 2 * par_ + b, :], hT[:, k, b * 128:(b + 1) * 128], w[:, k, :],
                               start=(k == 0), stop=(k == KT - 1))
                m.then_inc(gu_psum, 1)

            def turn_act(s, par_):
                pe.wait_ge(act_ready, s + 1)
                for f in range(2):
                    for b in range(NB):
                        c = f * SEQ + b * 128
                        m = tr(ps[:, 2 * par_, c:c + 128], am[:, par_, b, f * 128:(f + 1) * 128])
                m.then_inc(aT_psum, 1)

            def down(s, par_, use, first=False, last=False):
                slot = (par_ + 1) % 2
                pe.wait_ge(aT_ready, s + 1)
                pe.wait_ge(D_loaded[slot], 16 * use)
                w = ringD[:, slot, :].rearrange("p (k n) -> p k n", k=2)
                for f in range(2):
                    for n in range(2):
                        for b in range(NB):
                            m = mm(ps[:, 4 + 2 * b + n, :], aT[:, par_, f, b * 128:(b + 1) * 128],
                                   w[:, f, n * 512:(n + 1) * 512],
                                   start=(first and f == 0), stop=(last and f == 1))
                m.then_inc(down_done, 1)

            pe.wait_ge(ident_loaded, 16)
            pe.wait_ge(par_loaded, 16 * 9)
            for k in range(KT):
                m = tr(ps[:, k // 4, (k % 4) * 128:(k % 4) * 128 + ROWS], par[0:ROWS, k * 128:(k + 1) * 128], ROWS)
            m.then_inc(par_psum, 1)
            pe.wait_ge(mixer_loaded, 16 * 5)
            for l in range(DEPTH):
                for h in range(GM_HEADS):
                    m = tr(ps[:, 2 + l, h * 128:(h + 1) * 128], wsr[:, l, h, :])
            m.then_inc(wst_psum, 1)
            pe.wait_ge(parc_ready, 2)
            pe.wait_ge(wst_ready, 2)

            def pipeline(s0, a0, a1, d0, d1, n, reused):
                up(s0, 0, a0 + 1, reused)
                up(s0 + 1, 1, a1 + 1, reused)
                turn_act(s0, 0)
                up(s0 + 2, 0, a0 + 2)
                turn_act(s0 + 1, 1)
                down(s0, 0, d1 + 1, first=True)
                with pe.Fori(0, (n - 3) // 2) as i:
                    s = s0 + 2 * i + 3
                    up(s, 1, a1 + 2 + i)
                    turn_act(s - 1, 0)
                    down(s - 2, 1, d0 + 1 + i)
                    up(s + 1, 0, a0 + 3 + i)
                    turn_act(s, 1)
                    down(s - 1, 0, d1 + 2 + i)
                s = s0 + n
                if n % 2:
                    turn_act(s - 1, 0)
                    down(s - 2, 1, d0 + n // 2)
                    down(s - 1, 0, d1 + n // 2 + 1, last=True)
                else:
                    up(s - 1, 1, a1 + n // 2)
                    turn_act(s - 2, 0)
                    down(s - 3, 1, d0 + n // 2 - 1)
                    turn_act(s - 1, 1)
                    down(s - 2, 0, d1 + n // 2)
                    down(s - 1, 1, d0 + n // 2, last=True)

            a_base = [(0, 0), (9, 8)]
            for l in range(DEPTH):
                pe.wait_ge(xn_ready, 2 * (2 * l + 1))
                to_features(2 * l, XN)
                a0, a1 = a_base[l]
                for c in range(3):
                    project(l, c, C1, (a0, a1)[c % 2] + c // 2 + 1)
                pe.wait_ge(glu_ready, l + 1)
                for t in range(3):
                    for b in range(NB):
                        c = (t % 2) * SEQ + b * 128
                        m = tr(ps[:, t // 2, c:c + 128], GH[:, b, t * 128:(t + 1) * 128])
                m.then_inc(gluT_psum, 1)
                project(l, 3, C1, a1 + 2)
                pe.wait_ge(proj_evac, 4 * l + 4)
                for g in range(2):
                    for b in range(NB):
                        m = mm(ps[:, 2 + g, :], Pm[:, b, g * 128:(g + 1) * 128],
                               band[:, b, 2 * g:2 * g + 2, :], start=(b == 0), stop=(b == NB - 1))
                m.then_inc(pool1_psum, 1)
                pe.wait_ge(gv_ready, l + 1)
                for b in range(NB):
                    for h in range(GM_HEADS):
                        m = mm(ps[:, 4 + b, h * GM_HD:(h + 1) * GM_HD], wst[:, l, h, :],
                               GV[:, b, h * GM_HD:(h + 1) * GM_HD], start=True, stop=True)
                m.then_inc(z_psum, 1)
                pe.wait_ge(yt_ready, 4 * (l + 1))
                for g in range(2):
                    m = mm(ps[:, 2, g * SEQ:(g + 1) * SEQ], poolw[:, l, g, :], YT[:, g, :], start=True, stop=True)
                m.then_inc(pool2_psum, 1)
                pe.wait_ge(yb_ready, l + 1)
                for t in range(3):
                    for b in range(NB):
                        c = (t % 2) * SEQ + b * 128
                        m = tr(ps[:, 6 + t // 2, c:c + 128], YB[:, b, t * 128:(t + 1) * 128])
                m.then_inc(ybT_psum, 1)
                pe.wait_ge(conv_ready, 3 * (l + 1))
                for b in range(NB):
                    for t in range(3):
                        m = tr(ps[:, b, t * 128:(t + 1) * 128], ACC[:, t, b * 128:(b + 1) * 128])
                m.then_inc(cl_psum, 1)
                pe.wait_ge(cn_ready, l + 1)
                pe.wait_ge(mt_ready, 7 * l + 4)
                for t in range(3):
                    for b in range(NB):
                        c = (t % 2) * SEQ + b * 128
                        m = tr(ps[:, 2 + t // 2, c:c + 128], CN[:, b, t * 128:(t + 1) * 128])
                m.then_inc(cnT_psum, 1)
                pe.wait_ge(hc_ready, 3 * (l + 1))
                pe.wait_ge(D_loaded[0], 16 * (6 * l + 1))
                pw = ringD[:, 0, 0:3 * D_CONV].rearrange("p (k n) -> p k n", k=3)
                for d in range(3):
                    for k in range(3):
                        m = mm(ps[:, d // 2, (d % 2) * SEQ:(d % 2 + 1) * SEQ], pw[:, k, d * 128:(d + 1) * 128],
                               HC[:, k, :], start=(k == 0), stop=(k == 2))
                m.then_inc(pw_psum, 1)
                pe.wait_ge(mt_ready, 7 * (l + 1))
                for n in range(2):
                    full_depth(MT, n, (a0, a1)[n] + 3, lambda b: 4 + 2 * b + n, mix_psum)
                pe.wait_ge(xn_ready, 2 * (2 * l + 2))
                to_features(2 * l + 1, XN)
                if l == 0:
                    pipeline(0, 3, 3, 1, 0, STEPS, False)
            pe.wait_ge(attn_loaded, 16 * 8)
            for b in range(NB):
                for k in range(KT):
                    m = mm(ps[:, 4, b * EXPERTS:(b + 1) * EXPERTS], hT[:, k, b * 128:(b + 1) * 128], router[:, k, :],
                           start=(k == 0), stop=(k == KT - 1))
            m.then_inc(router_psum, 1)
            pe.wait_ge(gl_ready, 1)
            s = MOE_STEP0
            up(s, 0, 13, False)
            up(s + 1, 1, 12, False)
            turn_act(s, 0)

            def pairs(e, s):
                a, d = 12 + 7 * e, 7 + 7 * e
                up(s + 2, 0, a + 2)
                turn_act(s + 1, 1)
                if not isinstance(e, int):
                    pe.wait_ge(ffn_evac, e)
                down(s, 0, d, first=True)
                up(s + 3, 1, a + 1)
                turn_act(s + 2, 0)
                down(s + 1, 1, d + 1)
                with pe.Fori(0, STEPS_E // 2 - 2) as i:
                    t = s + 2 * i + 4
                    up(t, 0, a + 3 + i)
                    turn_act(t - 1, 1)
                    down(t - 2, 0, d + 1 + i)
                    up(t + 1, 1, a + 2 + i)
                    turn_act(t, 0)
                    down(t - 1, 1, d + 2 + i)

            pairs(0, s)
            with pe.Fori(1, EXPERTS) as e:
                s = MOE_STEP0 + STEPS_E * e
                a, d = 12 + 7 * e, 7 + 7 * e
                up(s, 0, a + 1)
                turn_act(s - 1, 1)
                down(s - 2, 0, d - 1)
                up(s + 1, 1, a)
                turn_act(s, 0)
                down(s - 1, 1, d, last=True)
                pairs(e, s)
            s = MOE_STEP0 + STEPS_E * EXPERTS
            turn_act(s - 1, 1)
            down(s - 2, 0, 62)
            down(s - 1, 1, 63, last=True)

            with pe.Fori(0, DEPTH) as l:
                q = l + 2
                a0, a1, d0, d1 = 68 + 10 * l, 67 + 9 * l, 63 + 6 * l, 62 + 6 * l
                pe.wait_ge(xln_ready, 2 * l + 1)
                to_features(2 * l + 4, X)
                for c in range(4):
                    project(q, c, C2, (a0, a1)[c % 2] + c // 2 + 1)
                pe.wait_ge(rope_ready, l + 1)
                flat = [RQI[:, :, 0:4, :], RQI[:, :, 4:8, :], RKI[:, :, :, :],
                        RK[:, :, 2, :, :], RK[:, :, 0, :, :], RK[:, :, 1, :, :]]
                flat += [RQ[:, :, 2 * t:2 * t + 2, :] for t in range(8)]
                for t in range(14):
                    for b in range(NB):
                        c = (t % 2) * SEQ + b * 128
                        m = tr(ps[:, t // 2, c:c + 128], flat[t][:, b].rearrange("p u d -> p (u d)"))
                    if t % 2:
                        m.then_inc(qkT_psum, 1)
                pe.wait_ge(qkT_act, 4 * (l + 1))
                pe.wait_ge(qkT_dve, 3 * (l + 1))
                for b in range(NB):
                    nk = 128 * (b + 1)
                    tok = slice(b * 128, (b + 1) * 128)
                    if b:
                        pe.wait_ge(dsa_scored, 2 * l + b)
                    for h in range(IDX_HEADS):
                        r = slice(32 * (h % 4), 32 * (h % 4) + 32)
                        m = mm(ps[:, h % 4, h // 4 * nk:(h // 4 + 1) * nk], TT[r, h // 4, tok], TT[r, 2, 0:nk],
                               start=True, stop=True)
                    m.then_inc(idx_psum, 1)
                    if b:
                        pe.wait_ge(om_ready, 4 * l + 2)
                    for h in range(Q_HEADS):
                        r = slice(64 * (h % 2), 64 * (h % 2) + 64)
                        c = 2048 + place(h) * nk
                        m = mm(psf[:, c:c + nk], TT[r, 6 + h // 2, tok], TT[r, 4 + h // 4, 0:nk], start=True, stop=True)
                    m.then_inc(swa_psum, 1)
                    pe.wait_ge(relu_ready, 2 * l + b + 1)
                    for h in range(Q_HEADS):
                        r = slice(64 * (h % 2), 64 * (h % 2) + 64)
                        c = place(h) * nk
                        m = mm(psf[:, c:c + nk], TT[r, 10 + h // 2, tok], TT[r, 3, 0:nk], start=True, stop=True)
                    m.then_inc(dsa_psum, 1)
                    for kind, S, expd, vcol in ((0, Sswa, swa_exp, lambda h: VA + HD * (h // 4)),
                                                (1, Sdsa, dsa_exp, lambda h: VB)):
                        pe.wait_ge(expd, 8 * (2 * l + b + 1))
                        g0 = 12 * l + 4 * b + 2 * (b + 1) * kind
                        for g in range(2 * (b + 1)):
                            if kind or g >= 2 or b:
                                pe.wait_ge(pt_ready, g0 + g - 1)
                            kt, h0 = g // 2, 4 * (g % 2)
                            for h in range(h0, h0 + 4):
                                m = tr(ps[:, 4 + g % 2, (h - h0) * 128:(h - h0 + 1) * 128],
                                       S[:, h * nk + kt * 128:h * nk + (kt + 1) * 128])
                            m.then_inc(pt_psum, 1)
                        pe.wait_ge(pt_ready, g0 + 2 * (b + 1))
                        for h in range(Q_HEADS):
                            p = place(h)
                            for kt in range(b + 1):
                                m = mm(ps[:, 6 + kind, p * HD:(p + 1) * HD], PT[:, kt, p, :],
                                       P2[:, kt, vcol(h):vcol(h) + HD], start=(kt == 0), stop=(kt == b))
                        m.then_inc(pv_psum, 1)
                pe.wait_ge(om_ready, 4 * (l + 1))
                for t in range(KT):
                    for b in range(NB):
                        c = (t % 2) * SEQ + b * 128
                        m = tr(ps[:, t // 2, c:c + 128], OM[:, b, t * 128:(t + 1) * 128])
                    if t % 2:
                        m.then_inc(omT_psum, 1)
                pe.wait_ge(mt2_act, 2 * (l + 1))
                pe.wait_ge(mt2_dve, 2 * (l + 1))
                for n in range(2):
                    full_depth(MT2, n, (a0, a1)[n] + 3, lambda b: 4 + 2 * b + n, mix_psum)
                pe.wait_ge(pin_loaded, 16 * (l + 1))
                for k in range(2):
                    for b in range(NB):
                        c = k * SEQ + b * 128
                        m = tr(ps[:, 0, c:c + 128], pin[:, b, k * 128:(k + 1) * 128])
                m.then_inc(pT_psum, 1)
                pe.wait_ge(pT_ready, l + 1)
                pe.wait_ge(xln_ready, 2 * l + 2)
                to_features(2 * l + 5, X)
                for n in range(2):
                    full_depth(hT, n, (a0, a1)[n] + 4, lambda b: 4 + 2 * b + n, pg_psum)
                pe.wait_ge(D_loaded[0], 16 * (d0 + 1))
                w = ringD[:, 0, :].rearrange("p (k n) -> p k n", k=2)
                for k in range(2):
                    for n in range(2):
                        for b in range(NB):
                            m = mm(ps[:, 2 * b + n, :], PPT[:, k, b * 128:(b + 1) * 128], w[:, k, n * 512:(n + 1) * 512],
                                   start=(k == 0), stop=(k == 1))
                m.then_inc(pp_psum, 1)
                pe.wait_ge(ple_read, l + 1)
                pipeline(B2_STEP0 + STEPS * l, a0 + 4, a1 + 4, d0 + 1, d1, STEPS, False)

        @block.gpsimd
        def _(pool):
            TTn = nc.gpsimd.tensor_tensor
            nc.gpsimd.memset(par, 0.0).then_inc(zeroed, 1)
            nc.gpsimd.memset(poolw[:, :, :, :], 0.0).then_inc(zeroed, 1)
            nc.gpsimd.memset(CT[:, :, 0:TAPS - 1], 0.0).then_inc(zeroed, 1)
            nc.gpsimd.memset(wst[:, :, :, 0:64], 0.0).then_inc(zeroed, 1)
            nc.gpsimd.memset(eps1, EPS).then_inc(zeroed, 1)
            nc.gpsimd.memset(eps2, LN_EPS).then_inc(zeroed, 1)
            pool.wait_ge(mixer_loaded, 16 * 5)
            for l in range(DEPTH):
                pool.wait_ge(gn_ready, 2 * (l + 1))
                TTn(GV, GV, gmg[:, l, :].unsqueeze(1).broadcast_to([128, NB, D_GM]), ALU.mult).then_inc(gv_ready, 1)
                pool.wait_ge(zb_ready, 8 * (l + 1))
                TTn(YB, YB, Pm[:, :, U0:U0 + D_GM], ALU.mult).then_inc(yb_ready, 1)
            pool.wait_ge(rope_tables, 8)
            with pool.Fori(0, DEPTH) as l:
                pool.wait_ge(proj_evac, 4 * l + 12)

                def heads(c0, n, d):
                    return P2[:, :, c0:c0 + n * d].rearrange("p b (h d) -> p b h d", d=d)

                def over(table, n, d):
                    return table[:, :, :].unsqueeze(2).broadcast_to([128, NB, n, d])

                TTn(RQI, heads(QI, 8, 32), over(cosI, 8, 32), ALU.mult).then_inc(cos_part, 1)
                TTn(RQ[:, :, 0:8, :], heads(QA, 8, HD), over(cosA, 8, HD), ALU.mult).then_inc(cos_part, 1)
                TTn(RQ[:, :, 8:16, :], heads(QB, 8, HD), over(cosA, 8, HD), ALU.mult).then_inc(cos_part, 1)
                for k, c0 in ((0, KA), (1, KA + HD), (2, KB)):
                    TTn(RK[:, :, k, :, :], P2[:, :, c0:c0 + HD].unsqueeze(2).broadcast_to([128, NB, 2, HD]),
                        over(cosA, 2, HD), ALU.mult).then_inc(cos_part, 1)

        @block.scalar
        def _(act):
            fn = nc.scalar.activation
            chain = Chain(act, act_chain)

            def load(dst, src, s):
                act.dma_start(dst, src).then_inc(s, 16)

            def rep(ap):
                return ap.partition_broadcast(128)

            load(ident[:, :], T["c_ident"], ident_loaded)
            load(X[:, :, :], T["x"].rearrange("o (b p) d -> p (o b) d", p=128), x_loaded)
            act.wait_ge(zeroed, 6)
            for r, n in ((R_N1, "norm1_g"), (R_N2, "norm2_g"), (R_DWB, "conv_dw_b"), (R_LNG, "conv_ln_g"),
                         (R_LNB, "conv_ln_b"), (R_PWB, "conv_pw_b"), (R_PSC, "pool_scale")):
                load(par[r:r + DEPTH, 0:T[n].shape[1]], T[n], par_loaded)
            load(par[R_DW:R_DW + DEPTH * TAPS, 0:D_CONV], T["conv_dw_w"].rearrange("l t c -> (l t) c"), par_loaded)
            load(par[R_GMB:ROWS, 0:128], T["gm_b"].rearrange("l h i -> (l h) i"), par_loaded)
            load(wsr, T["gm_ws"].rearrange("l h i j -> i l h j"), mixer_loaded)
            for g in range(2):
                load(poolw[64 * g:64 * g + 64, :, :, 64 * g:64 * g + 64],
                     T["pool_w"].rearrange("l (r g) c d -> g c l r d", g=2)[g], mixer_loaded)
            load(gmg[:, :, :], rep(T["gm_norm_g"]), mixer_loaded)
            load(band[:, :, :, :], T["c_band"].rearrange("(b p) w t -> p b w t", p=128), mixer_loaded)
            load(masks[:, :, :], T["c_masks"], attn_loaded)
            load(freq[:, :], rep(T["c_freq"][0]), attn_loaded)
            load(lower[:, :, :].rearrange("p a b -> p (a b)"), rep(T["c_lower"][0]), attn_loaded)
            with nc.allow_non_contiguous_dma(reason="256 positions, one per partition"):
                load(posi[:, :], T["positions_2"].rearrange("o (b p) -> p (o b)", p=128), attn_loaded)
            load(sink[:, :, :], rep(T["attn_sinks_2"]), attn_loaded)
            load(ikg[:, :, :], rep(T["idx_k_g_2"]), attn_loaded)
            load(ikb[:, :, :], rep(T["idx_k_b_2"]), attn_loaded)
            load(router[:, :, :], T["moe_router"][0].rearrange("(k p) e -> p k e", p=128), attn_loaded)
            for k, n in enumerate(("final_g", "ln_in_g_2", "ln_in_b_2")):
                load(lni[:, k, :], rep(T[n]), ln_loaded)
            for k, n in enumerate(("ln1_g_2", "ln1_b_2", "ln2_g_2", "ln2_b_2")):
                load(lnp[:, :, k, :], rep(T[n]), ln_loaded)

            def rms(t):
                for b in range(NB):
                    chain.then(fn(XN[:, b, :], X[:, b, :], ACT.Square, accum_out=ss[:, b:b + 1]))
                chain.wait()
                fn(std, ss, ACT.Sqrt, scale=1.0 / D, bias=eps1).then_inc(std_ready, 1)

            def features(t, gain):
                for k in range(4):
                    act.wait_ge(hT_psum, 4 * t + k // 2 + 1)
                    src = ps[:, k // 2, (k % 2) * SEQ:(k % 2 + 1) * SEQ]
                    fn(hT[:, k, :], src, ACT.Copy, scale=1.0 if gain is None else gain(k)).then_inc(hT_ready, 1)

            def silu(s, par_):
                act.wait_ge(gu_psum, s + 1)
                wait(act, act_ready, s - 1)
                fn(sil[:, par_, :, :], ps[:, 2 * par_:2 * par_ + 2, 0:FN], ACT.Silu).then_inc(silu_ready, 1)

            def act_out(s, par_):
                act.wait_ge(aT_psum, s + 1)
                wait(act, down_done, s - 1)
                fn(aT[:, par_, :, :].rearrange("p f n -> p (f n)"), ps[:, 2 * par_, :], ACT.Copy).then_inc(aT_ready, 1)

            def feed_forward(s0, n):
                silu(s0, 0)
                silu(s0 + 1, 1)
                act_out(s0, 0)
                with act.Fori(0, (n - 2) // 2) as i:
                    s = s0 + 2 * i + 2
                    silu(s, 0)
                    act_out(s - 1, 1)
                    silu(s + 1, 1)
                    act_out(s, 0)
                if n % 2:
                    silu(s0 + n - 1, 0)
                    act_out(s0 + n - 2, 1)
                act_out(s0 + n - 1, (n - 1) % 2)

            def evac_proj(q, c, dst):
                act.wait_ge(proj_psum, 4 * q + c + 1)
                fn(dst, ps[:, 4 + 2 * (c % 2):6 + 2 * (c % 2), 0:dst.shape[2]], ACT.Copy).then_inc(proj_evac, 1)

            act.wait_ge(x_loaded, 16)
            rms(0)
            act.wait_ge(par_psum, 1)
            for g in range(2):
                fn(parc[:, 4 * g:4 * g + 4, :], ps[:, g, :].rearrange("p (k n) -> p k n", k=4)[:, :, 0:ROWS],
                   ACT.Copy).then_inc(parc_ready, 1)
            act.wait_ge(wst_psum, 1)
            raw = ps[:, 2:4, :].rearrange("p l (h i) -> p (l h) i", h=GM_HEADS)
            wsf = wst[:, :, :, :].rearrange("p l h i -> p (l h) i")
            fn(wsf[0:64, :, :], raw[0:64, :, :], ACT.Copy).then_inc(wst_ready, 1)
            fn(wsf[64:128, :, 64:128], raw[64:128, :, 64:128], ACT.Copy).then_inc(wst_ready, 1)
            act.wait_ge(parc_ready, 2)
            for l in range(DEPTH):
                if l:
                    act.wait_ge(x_ready, 2)
                    rms(2)
                features(2 * l, lambda k: parc[:, k, R_N1 + l:R_N1 + l + 1])

                def cols(c):
                    c0 = D_IN - C1 * (c + 1)
                    return Pm[:, :, c0:c0 + C1]

                evac_proj(l, 0, cols(0))
                evac_proj(l, 1, cols(1))
                act.wait_ge(proj_evac, 4 * l + 2)
                fn(GH, Pm[:, :, CG0:CG0 + D_CONV], ACT.Sigmoid).then_inc(sg_ready, 1)
                evac_proj(l, 2, cols(2))
                act.wait_ge(proj_evac, 4 * l + 3)
                for b in range(NB):
                    chain.then(fn(GV[:, b, :], Pm[:, b, V0:V0 + D_GM], ACT.Square, accum_out=gm_ss[:, b:b + 1]))
                chain.wait()
                fn(gm_std, gm_ss, ACT.Sqrt, scale=1.0 / D_GM, bias=eps1).then_inc(gm_std_ready, 1)
                act.wait_ge(gluT_psum, l + 1)
                fn(CT[:, 0:2, TAPS - 1:], ps[:, 0, :].rearrange("p (t n) -> p t n", t=2), ACT.Copy).then_inc(ct_ready, 1)
                fn(CT[:, 2, TAPS - 1:], ps[:, 1, 0:SEQ], ACT.Copy).then_inc(ct_ready, 1)
                act.wait_ge(gm_rstd_ready, l + 1)
                for b in range(NB):
                    fn(GV[:, b, :], Pm[:, b, V0:V0 + D_GM], ACT.Copy, scale=gm_rstd[:, b:b + 1]).then_inc(gn_ready, 1)
                evac_proj(l, 3, cols(3))
                act.wait_ge(pool1_psum, l + 1)
                for g in range(2):
                    for h in range(2):
                        r = slice(64 * h, 64 * h + 64)
                        fn(YT[r, g, :], ps[r, 2 + g, h * SEQ:(h + 1) * SEQ], ACT.Copy).then_inc(yt_ready, 1)
                act.wait_ge(z_psum, l + 1)
                for b in range(NB):
                    for h in range(GM_HEADS):
                        c = slice(h * GM_HD, (h + 1) * GM_HD)
                        r = R_GMB + l * GM_HEADS + h
                        fn(YB[:, b, c], ps[:, 4 + b, c], ACT.Identity, bias=parc[:, 0, r:r + 1]).then_inc(zb_ready, 1)
                act.wait_ge(pool2_psum, l + 1)
                for g in range(2):
                    fn(MT[:, g, :], ps[:, 2, g * SEQ:(g + 1) * SEQ], ACT.Copy,
                       scale=parc[:, g, R_PSC + l:R_PSC + l + 1]).then_inc(mt_ready, 1)
                act.wait_ge(ybT_psum, l + 1)
                fn(MT[:, 2:4, :], ps[:, 6, :].rearrange("p (t n) -> p t n", t=2), ACT.Copy).then_inc(mt_ready, 1)
                fn(MT[:, 4, :], ps[:, 7, 0:SEQ], ACT.Copy).then_inc(mt_ready, 1)
                act.wait_ge(cl_var, l + 1)
                fn(lstd, mv[:, :, 1], ACT.Sqrt, bias=eps1).then_inc(cl_std, 1)
                act.wait_ge(cnT_psum, l + 1)
                for t in range(3):
                    fn(HC[:, t, :], ps[:, 2 + t // 2, (t % 2) * SEQ:(t % 2 + 1) * SEQ], ACT.Silu,
                       scale=parc[:, t, R_LNG + l:R_LNG + l + 1], bias=parc[:, t, R_LNB + l:R_LNB + l + 1]).then_inc(hc_ready, 1)
                act.wait_ge(pw_psum, l + 1)
                for d in range(3):
                    fn(MT[:, 5 + d, :], ps[:, d // 2, (d % 2) * SEQ:(d % 2 + 1) * SEQ], ACT.Identity,
                       bias=parc[:, d, R_PWB + l:R_PWB + l + 1]).then_inc(mt_ready, 1)
                act.wait_ge(x_ready, 2 * l + 1)
                rms(2 * l + 1)
                features(2 * l + 1, lambda k: parc[:, k, R_N2 + l:R_N2 + l + 1])
                if l == 0:
                    feed_forward(0, STEPS)
                    act.wait_ge(args_ready, 1)
                    fn(trig, arg, ACT.Sin).then_inc(trig_ready, 1)
            act.wait_ge(gl_ready, 1)
            for b in range(NB):
                fn(gexp[:, b, :], logit[:, b, :], ACT.Exp, bias=gneg[:, b:b + 1]).then_inc(ge_ready, 1)
            feed_forward(MOE_STEP0, EXPERTS * STEPS_E)
            act.wait_ge(ffn_evac, EXPERTS)
            rms(4)

            def ln_std_of(i):
                act.wait_ge(ln_var, i + 1)
                fn(lstd, mv[:, :, 1], ACT.Sqrt, bias=eps2).then_inc(ln_std, 1)

            ln_std_of(0)
            with act.Fori(0, DEPTH) as l:
                features(2 * l + 4, None)
                for c in range(4):
                    evac_proj(l + 2, c, P2[:, :, c * C2:(c + 1) * C2])
                act.wait_ge(ik_var, l + 1)
                fn(lstd, mv[:, :, 1], ACT.Sqrt, bias=eps2).then_inc(ik_std, 1)
                for i in range(0, 7, 2):
                    act.wait_ge(qkT_psum, 7 * l + i + 1)
                    fn(TT[:, 2 * i:2 * i + 2, :].rearrange("p t n -> p (t n)"), ps[:, i, :], ACT.Copy).then_inc(qkT_act, 1)
                for b in range(NB):
                    nk = 128 * (b + 1)
                    act.wait_ge(idx_psum, 2 * l + b + 1)
                    fn(RL[:, 0:8 * nk].rearrange("p (r n) -> p r n", r=4), ps[:, 0:4, 0:2 * nk], ACT.Relu).then_inc(relu_ready, 1)
                    for kind, S, scored, nm, den, done in ((0, Sswa, swa_scored, swa_nm, swa_den, swa_exp),
                                                           (1, Sdsa, dsa_scored, dsa_nm, dsa_den, dsa_exp)):
                        act.wait_ge(scored, 2 * l + b + 1)
                        if kind == 0:
                            fn(swa_es, swa_es, ACT.Exp)
                        for h in range(Q_HEADS):
                            fn(S[:, h * nk:(h + 1) * nk], S[:, h * nk:(h + 1) * nk], ACT.Exp, bias=nm[:, h:h + 1],
                               accum_out=den[:, h:h + 1]).then_inc(done, 1)
                        g0 = 12 * l + 4 * b + 2 * (b + 1) * kind
                        for g in range(2 * (b + 1)):
                            act.wait_ge(pt_psum, g0 + g + 1)
                            h0 = 4 * (g % 2)
                            fn(PT[:, g // 2, h0:h0 + 4, :].rearrange("p h q -> p (h q)"), ps[:, 4 + g % 2, :],
                               ACT.Copy).then_inc(pt_ready, 1)
                for i in range(2):
                    act.wait_ge(omT_psum, 4 * l + i + 1)
                    fn(MT2[:, 2 * i:2 * i + 2, :].rearrange("p t n -> p (t n)"), ps[:, i, :], ACT.Copy).then_inc(mt2_act, 1)
                act.wait_ge(pT_psum, l + 1)
                fn(PPT.rearrange("p k n -> p (k n)"), ps[:, 0, :], ACT.Copy).then_inc(pT_ready, 1)
                ln_std_of(2 * l + 1)
                features(2 * l + 5, None)
                act.wait_ge(pg_psum, 2 * l + 2)
                fn(SGP, psf[:, 2048:4096], ACT.Sigmoid).then_inc(sgp_ready, 1)
                feed_forward(B2_STEP0 + STEPS * l, STEPS)
                ln_std_of(2 * l + 2)

        @block.vector
        def _(dve):
            V = nc.vector
            chain = Chain(dve, dve_chain)
            link, then = chain.link, chain.then

            def pause():
                V.memset(spare, 0.0)

            MAGIC, TURN = 1.5 * 2.0 ** 23, 2.0 * np.pi
            T1_ = 6.28125
            T2_ = float(np.round((TURN - T1_) * 2.0 ** 21) / 2.0 ** 21)
            T3_ = float(TURN - T1_ - T2_)
            PI = 3.1415925
            dve.wait_ge(attn_loaded, 16 * 8)
            link(V.tensor_copy(posf, posi[:, :]))
            for b in range(NB):
                then(V.tensor_scalar(ang[:, b, :], freq[:, :], posf[:, b:b + 1], None, ALU.mult))
            chain.wait()
            for c in range(2):
                then(V.tensor_scalar(turn[:, c], ang, 1.0 / TURN, 0.25 * c, ALU.mult, ALU.add))
            chain.wait()
            link(V.tensor_scalar(turn, turn, MAGIC, MAGIC, ALU.add, ALU.subtract))
            for c in range(2):
                then(V.scalar_tensor_tensor(arg[:, c], turn[:, c], -T1_, ang, ALU.mult, ALU.add))
            chain.wait()
            for part in (T2_, T3_):
                link(V.scalar_tensor_tensor(arg, turn, -part, arg, ALU.mult, ALU.add))
            link(V.tensor_scalar(arg[:, 1], arg[:, 1], np.pi / 2, None, ALU.add))
            V.tensor_scalar(arg, arg, PI, -PI, ALU.min, ALU.max).then_inc(args_ready, 1)

            def normed(t):
                dve.wait_ge(std_ready, t + 1)
                link(V.reciprocal(rstd, std))
                for b in range(NB):
                    V.tensor_scalar(XN[:, b, :], X[:, b, :], rstd[:, b:b + 1], None, ALU.mult).then_inc(xn_ready, 1)

            def features(t, gain):
                for k in range(4, KT):
                    dve.wait_ge(hT_psum, 4 * t + k // 2 + 1)
                    src = ps[:, k // 2, (k % 2) * SEQ:(k % 2 + 1) * SEQ]
                    if gain is None:
                        ins = V.tensor_copy(hT[:, k, :], src)
                    else:
                        ins = V.tensor_scalar(hT[:, k, :], src, gain(k), None, ALU.mult)
                    ins.then_inc(hT_ready, 1)

            def act_mul(s, par_):
                dve.wait_ge(silu_ready, s + 1)
                wait(dve, aT_psum, s - 1)
                V.tensor_tensor(am[:, par_, :, :], sil[:, par_, :, :], ps[:, 2 * par_:2 * par_ + 2, FN:2 * FN],
                                ALU.mult).then_inc(act_ready, 1)

            def feed_forward(s0, n):
                act_mul(s0, 0)
                act_mul(s0 + 1, 1)
                with dve.Fori(1, n // 2) as i:
                    act_mul(s0 + 2 * i, 0)
                    act_mul(s0 + 2 * i + 1, 1)
                if n % 2:
                    act_mul(s0 + n - 1, 0)

            def add_down(done, gate=None):
                for b in range(NB):
                    src = psf[:, 2048 + 1024 * b:3072 + 1024 * b]
                    if gate is None:
                        ins = V.tensor_tensor(X[:, b, :], X[:, b, :], src, ALU.add)
                    else:
                        ins = V.scalar_tensor_tensor(X[:, b, :], src, gate(b), X[:, b, :], ALU.mult, ALU.add)
                    done(b, ins)

            for l in range(DEPTH):
                normed(2 * l)
                if l == 0:
                    dve.wait_ge(parc_ready, 2)
                features(2 * l, lambda k: parc[:, k, R_N1 + l:R_N1 + l + 1])
                dve.wait_ge(sg_ready, l + 1)
                V.tensor_tensor(GH, GH, Pm[:, :, CV0:CV0 + D_CONV], ALU.mult).then_inc(glu_ready, 1)
                dve.wait_ge(gm_std_ready, l + 1)
                V.reciprocal(gm_rstd, gm_std).then_inc(gm_rstd_ready, 1)
                dve.wait_ge(ct_ready, 2 * (l + 1))
                for t in range(3):
                    then(V.tensor_scalar(ACC[:, t, :], CT[:, t, 0:SEQ], parc[:, t, R_DW + TAPS * l:R_DW + TAPS * l + 1],
                                         parc[:, t, R_DWB + l:R_DWB + l + 1], ALU.mult, ALU.add))
                with dve.Fori(0, TAPS - 2) as i:
                    chain.enter(i, 3)
                    for t in range(3):
                        chain.wait(back=2)
                        then(V.scalar_tensor_tensor(ACC[:, t, :], CT[:, t, bass.ds(i + 1, SEQ)],
                                                    parc[:, t, bass.ds(i + R_DW + TAPS * l + 1, 1)], ACC[:, t, :],
                                                    ALU.mult, ALU.add))
                chain.leave(3, TAPS - 2)
                for t in range(3):
                    chain.wait(back=2 - t)
                    V.scalar_tensor_tensor(ACC[:, t, :], CT[:, t, TAPS - 1:TAPS - 1 + SEQ],
                                           parc[:, t, R_DW + TAPS * l + TAPS - 1:R_DW + TAPS * l + TAPS], ACC[:, t, :],
                                           ALU.mult, ALU.add).then_inc(conv_ready, 1)
                dve.wait_ge(cl_psum, l + 1)
                for b in range(NB):
                    then(V.bn_stats(bst[:, b, 0, :], ps[:, b, 0:D_CONV]))
                chain.wait()
                for b in range(NB):
                    ins = V.bn_aggr(mv[:, b, :], bst[:, b, 0, :])
                ins.then_inc(cl_var, 1)
                dve.wait_ge(cl_std, l + 1)
                link(V.reciprocal(lrstd, lstd))
                for b in range(NB):
                    ins = V.tensor_scalar(CN[:, b, :], ps[:, b, 0:D_CONV], mv[:, b, 0:1], lrstd[:, b:b + 1],
                                          ALU.subtract, ALU.mult)
                ins.then_inc(cn_ready, 1)
                for n in range(2):
                    dve.wait_ge(mix_psum, 2 * l + n + 1)
                    for b in range(NB):
                        x = X[:, b, 512 * n:512 * n + 512]
                        ins = V.tensor_tensor(x, x, ps[:, 4 + 2 * b + n, :], ALU.add)
                ins.then_inc(x_ready, 1)
                dve.wait_ge(x_ready, 2 * l + 1)
                normed(2 * l + 1)
                features(2 * l + 1, lambda k: parc[:, k, R_N2 + l:R_N2 + l + 1])
                if l == 0:
                    feed_forward(0, STEPS)
                    dve.wait_ge(down_done, STEPS)
                    add_down(lambda b, ins: ins.then_inc(x_ready, 1) if b else None)
                    dve.wait_ge(trig_ready, 1)
                    for tc, tsn, h, f in ((cosA, sinA, HD // 2, slice(0, 32)), (cosI, sinI, IDX_DIM // 2, slice(32, 48))):
                        for half in range(2):
                            V.tensor_copy(tc[:, :, half * h:(half + 1) * h], trig[:, 1, :, f]).then_inc(rope_tables, 1)
                            V.tensor_scalar(tsn[:, :, half * h:(half + 1) * h], trig[:, 0, :, f], 2.0 * half - 1.0, None,
                                            ALU.mult).then_inc(rope_tables, 1)
                    dve.wait_ge(x_ready, 2)
            dve.wait_ge(router_psum, 1)
            link(V.tensor_copy(logit, ps[:, 4, 0:NB * EXPERTS].rearrange("p (b e) -> p b e", b=NB)))
            then(V.tensor_reduce(gmax, logit, AX.X, ALU.max))
            for b in range(NB):
                other = logit[:, b, :].unsqueeze(1).broadcast_to([128, EXPERTS, EXPERTS])
                own = logit[:, b, :].unsqueeze(2).broadcast_to([128, EXPERTS, EXPERTS])
                beats = score[:, 64 * b:64 * b + 64].rearrange("p (e f) -> p e f", e=EXPERTS)
                ties = work[:, 64 * b:64 * b + 64].rearrange("p (e f) -> p e f", e=EXPERTS)
                then(V.tensor_tensor(beats, other, own, ALU.is_gt))
                link(V.tensor_tensor(ties, other, own, ALU.is_equal))
                link(V.tensor_tensor(ties, ties, lower[:, :, :], ALU.mult))
                link(V.tensor_tensor(beats, beats, ties, ALU.add))
                link(V.tensor_reduce(rank[:, b, :], beats, AX.X, ALU.add))
            V.tensor_scalar(gneg, gmax, -1.0, None, ALU.mult).then_inc(gl_ready, 1)
            link(V.tensor_scalar(rank, rank, 2.0, None, ALU.is_lt))
            dve.wait_ge(ge_ready, NB)
            link(V.tensor_tensor(gexp, gexp, rank, ALU.mult))
            link(V.tensor_reduce(gden, gexp, AX.X, ALU.add))
            link(V.reciprocal(grec, gden))
            for b in range(NB):
                then(V.tensor_scalar(gates[:, b, :], gexp[:, b, :], grec[:, b:b + 1], None, ALU.mult))
            feed_forward(MOE_STEP0, STEPS_E)
            with dve.Fori(1, EXPERTS) as e:
                s0 = MOE_STEP0 + STEPS_E * e
                act_mul(s0, 0)
                act_mul(s0 + 1, 1)
                dve.wait_ge(down_done, s0)
                wait_gates = chain.wait()
                add_down(lambda b, ins: ins.then_inc(ffn_evac, 1) if b else None,
                         lambda b: gates[:, b, bass.ds(e - 1, 1)])
                with dve.Fori(0, STEPS_E // 2 - 1) as i:
                    act_mul(s0 + 2 * i + 2, 0)
                    act_mul(s0 + 2 * i + 3, 1)
                dve.wait_ge(ffn_evac, e)
            dve.wait_ge(down_done, B2_STEP0)
            add_down(lambda b, ins: ins.then_inc(ffn_evac, 1) if b else None,
                     lambda b: gates[:, b, EXPERTS - 1:EXPERTS])

            def layer_norm(i, g, b_):
                for b in range(NB):
                    for c in range(2):
                        then(V.bn_stats(bst[:, b, c, :], X[:, b, 512 * c:512 * c + 512]))
                chain.wait()
                pause()
                for b in range(NB):
                    ins = V.bn_aggr(mv[:, b, :], bst[:, b, :, :].rearrange("p c s -> p (c s)"))
                ins.then_inc(ln_var, 1)
                dve.wait_ge(ln_std, i + 1)
                link(V.reciprocal(lrstd, lstd))
                for b in range(NB):
                    then(V.scalar_tensor_tensor(X[:, b, :], X[:, b, :], mv[:, b, 0:1], g, ALU.subtract, ALU.mult))
                chain.wait()
                for b in range(NB):
                    ins = V.scalar_tensor_tensor(X[:, b, :], X[:, b, :], lrstd[:, b:b + 1], b_, ALU.mult, ALU.add)
                ins.then_inc(xln_ready, 1)

            dve.wait_ge(std_ready, 5)
            dve.wait_ge(ln_loaded, 16 * 7)
            link(V.reciprocal(rstd, std))
            for b in range(NB):
                then(V.scalar_tensor_tensor(X[:, b, :], X[:, b, :], rstd[:, b:b + 1], lni[:, 0, :], ALU.mult, ALU.mult))
            chain.wait()
            layer_norm(0, lni[:, 1, :], lni[:, 2, :])

            PER_LAYER = 106
            with dve.Fori(0, DEPTH) as l:
                chain.enter(l, PER_LAYER)
                features(2 * l + 4, None)
                dve.wait_ge(proj_evac, 4 * l + 12)

                def halves(c0, n, d):
                    return P2[:, :, c0:c0 + n * d].rearrange("p b (h c d) -> p b h c d", c=2, d=d // 2)

                def over(table, half, n, d):
                    return table[:, :, half * d // 2:(half + 1) * d // 2].unsqueeze(2).broadcast_to([128, NB, n, d // 2])

                for b in range(NB):
                    then(V.bn_stats(bst[:, b, 0, :], P2[:, b, KI:KI + IDX_DIM]))
                chain.wait()
                pause()
                for b in range(NB):
                    ins = V.bn_aggr(mv[:, b, :], bst[:, b, 0, :])
                ins.then_inc(ik_var, 1)
                for c0, h0, n in ((QA, 0, 10), (QB, 10, 9)):
                    for half in range(2):
                        then(V.tensor_tensor(T2[:, :, h0:h0 + n, half, :], halves(c0, n, HD)[:, :, :, 1 - half, :],
                                             over(sinA, half, n, HD), ALU.mult))
                for half in range(2):
                    then(V.tensor_tensor(T2I[:, :, :, half, :], halves(QI, 8, IDX_DIM)[:, :, :, 1 - half, :],
                                         over(sinI, half, 8, IDX_DIM), ALU.mult))
                then(V.tensor_scalar(wi, P2[:, :, WI:WI + IDX_HEADS], IDX_HEADS ** -0.5 * IDX_DIM ** -0.5, None, ALU.mult))
                dve.wait_ge(ik_std, l + 1)
                link(V.reciprocal(lrstd, lstd))
                for b in range(NB):
                    then(V.tensor_scalar(KN[:, b, :], P2[:, b, KI:KI + IDX_DIM], mv[:, b, 0:1], lrstd[:, b:b + 1],
                                         ALU.subtract, ALU.mult))
                chain.wait()

                def both(row):
                    return row.broadcast_to([128, NB, IDX_DIM])

                link(V.tensor_tensor(KN, KN, both(ikg[:, bass.ds(l, 1), :]), ALU.mult))
                link(V.tensor_tensor(KN, KN, both(ikb[:, bass.ds(l, 1), :]), ALU.add))
                for half in range(2):
                    h = IDX_DIM // 2
                    then(V.tensor_tensor(T2K[:, :, half, :], KN[:, :, (1 - half) * h:(2 - half) * h],
                                         sinI[:, :, half * h:(half + 1) * h], ALU.mult))
                chain.wait()
                link(V.tensor_tensor(KN, KN, cosI[:, :, :], ALU.mult))
                four = [128, NB, 4, IDX_DIM]
                V.tensor_tensor(RKI, KN.unsqueeze(2).broadcast_to(four),
                                T2K.rearrange("p b c d -> p b (c d)").unsqueeze(2).broadcast_to(four), ALU.add)
                dve.wait_ge(cos_part, 6 * l + 6)
                whole = T2.rearrange("p b h c d -> p b h (c d)")
                V.tensor_tensor(RQI, RQI, T2I.rearrange("p b h c d -> p b h (c d)"), ALU.add)
                for k, h in ((0, 8), (1, 9), (2, 18)):
                    V.tensor_tensor(RK[:, :, k, :, :], RK[:, :, k, :, :],
                                    whole[:, :, h:h + 1, :].broadcast_to([128, NB, 2, HD]), ALU.add)
                V.tensor_tensor(RQ[:, :, 0:8, :], RQ[:, :, 0:8, :], whole[:, :, 0:8, :], ALU.add)
                V.tensor_tensor(RQ[:, :, 8:16, :], RQ[:, :, 8:16, :], whole[:, :, 10:18, :], ALU.add).then_inc(rope_ready, 1)
                for i in range(1, 7, 2):
                    dve.wait_ge(qkT_psum, 7 * l + i + 1)
                    V.tensor_copy(TT[:, 2 * i:2 * i + 2, :].rearrange("p t n -> p (t n)"), ps[:, i, :]).then_inc(qkT_dve, 1)
                for b in range(NB):
                    nk = 128 * (b + 1)
                    causal = masks[:, 1, 256 - nk:256]

                    def per_head(ap):
                        return ap.rearrange("p (h k) -> p h k", h=Q_HEADS)

                    def bias(m):
                        return m.unsqueeze(1).broadcast_to([128, Q_HEADS, nk])

                    dve.wait_ge(swa_psum, 2 * l + b + 1)
                    S = per_head(Sswa[:, 0:8 * nk])
                    link(V.scalar_tensor_tensor(S, per_head(psf[:, 2048:2048 + 8 * nk]), HD ** -0.5,
                                                bias(masks[:, 0, 256 - nk:256]), ALU.mult, ALU.add))
                    link(V.tensor_reduce(swa_m, S, AX.X, ALU.max))
                    snk = sink[:, bass.ds(l, 1), :].rearrange("p o (a t) -> p (o t) a", t=2)

                    def by_place(ap):
                        return ap.rearrange("p (t a) -> p t a", t=2)

                    link(V.tensor_tensor(by_place(swa_m), by_place(swa_m), snk, ALU.max))
                    V.tensor_scalar(swa_nm, swa_m, -1.0, None, ALU.mult)
                    V.tensor_tensor(by_place(swa_es), snk, by_place(swa_m), ALU.subtract).then_inc(swa_scored, 1)
                    dve.wait_ge(relu_ready, 2 * l + b + 1)
                    sc = score[:, 0:nk]
                    for h in range(IDX_HEADS):
                        p = 2 * (h % 4) + h // 4
                        link(V.scalar_tensor_tensor(sc, RL[:, p * nk:(p + 1) * nk], wi[:, b, h:h + 1], sc if h else causal,
                                                    ALU.mult, ALU.add))
                    pause()
                    with dve.Fori(0, TOPK // 8) as r:
                        chain.enter(r, 2)
                        link(V.max(top8, sc))
                        pause()
                        link(V.match_replace(sc, top8, sc, TAKEN))
                    chain.leave(2, TOPK // 8)
                    db = dbias[:, 0:nk]
                    link(V.tensor_scalar(db, sc, TAKEN, NEG, ALU.not_equal, ALU.mult))
                    link(V.tensor_tensor(db, db, causal, ALU.min))
                    dve.wait_ge(dsa_psum, 2 * l + b + 1)
                    S = per_head(Sdsa[:, 0:8 * nk])
                    link(V.scalar_tensor_tensor(S, per_head(psf[:, 0:8 * nk]), HD ** -0.5, bias(db), ALU.mult, ALU.add))
                    link(V.tensor_reduce(dsa_m, S, AX.X, ALU.max))
                    V.tensor_scalar(dsa_nm, dsa_m, -1.0, None, ALU.mult).then_inc(dsa_scored, 1)
                    for kind, expd, den, rd in ((0, swa_exp, swa_den, swa_rd), (1, dsa_exp, dsa_den, dsa_rd)):
                        dve.wait_ge(expd, 8 * (2 * l + b + 1))
                        if kind == 0:
                            link(V.tensor_tensor(den, den, swa_es, ALU.add))
                        link(V.reciprocal(rd, den))
                        dve.wait_ge(pv_psum, 4 * l + 2 * b + kind + 1)
                        V.tensor_tensor(OM[:, b, 512 * kind:512 * kind + 512].rearrange("p (a t d) -> p t a d", t=2, d=HD),
                                        ps[:, 6 + kind, :].rearrange("p (t a d) -> p t a d", t=2, d=HD),
                                        by_place(rd).unsqueeze(3).broadcast_to([128, 2, Q_HEADS // 2, HD]),
                                        ALU.mult).then_inc(om_ready, 1)
                for i in range(2, 4):
                    dve.wait_ge(omT_psum, 4 * l + i + 1)
                    V.tensor_copy(MT2[:, 2 * i:2 * i + 2, :].rearrange("p t n -> p (t n)"), ps[:, i, :]).then_inc(mt2_dve, 1)
                for n in range(2):
                    dve.wait_ge(mix_psum, 2 * l + n + 5)
                    for b in range(NB):
                        x = X[:, b, 512 * n:512 * n + 512]
                        then(V.scalar_tensor_tensor(x, x, ALPHA, ps[:, 4 + 2 * b + n, :], ALU.mult, ALU.add))
                chain.wait()

                def lnrow(k):
                    return lnp[:, bass.ds(l, 1), k, :].rearrange("p o d -> p (o d)")

                layer_norm(2 * l + 1, lnrow(0), lnrow(1))
                features(2 * l + 5, None)
                xf = X[:, :, :].rearrange("p b n -> p (b n)")
                dve.wait_ge(sgp_ready, l + 1)
                dve.wait_ge(pp_psum, l + 1)
                V.tensor_tensor(PLEO, SGP, psf[:, 0:2048], ALU.mult).then_inc(ple_read, 1)
                dve.wait_ge(ple_read, l + 1)
                link(V.scalar_tensor_tensor(xf, xf, ALPHA, PLEO, ALU.mult, ALU.add))
                pause()
                feed_forward(B2_STEP0 + STEPS * l, STEPS)
                dve.wait_ge(down_done, B2_STEP0 + STEPS * l + STEPS)
                add_down(lambda b, ins: then(ins))
                chain.wait()
                layer_norm(2 * l + 2, lnrow(2), lnrow(3))
            chain.leave(PER_LAYER, DEPTH)


OUT_SHAPE = (1, SEQ, D)


def kernel(**inputs):
    import concourse.bacc as bacc
    from concourse.bass_utils import run_bass_kernel_spmd

    nc = bacc.Bacc("TRN2", target_bir_lowering=False, num_devices=1, dynamic_dma_scratch_size=1024)
    arrays = {n: np.ascontiguousarray(a) for n, a in inputs.items()}
    arrays.update(shape_constants())
    T = {n: nc.dram_tensor(f"in_{n}", a.shape, mybir.dt.from_np(a.dtype), kind="ExternalInput").ap()
         for n, a in arrays.items()}
    T["out"] = nc.dram_tensor("out", OUT_SHAPE, mybir.dt.float32, kind="ExternalOutput").ap()
    build_program(nc, {n: t[0] if n.startswith("moe_") and n != "moe_router" else t for n, t in T.items()})
    run = run_bass_kernel_spmd(nc, [{f"in_{n}": a for n, a in arrays.items()}], core_ids=[0])
    return run.results[0]["out"]
```

```python
from contextlib import ExitStack

import numpy as np

import concourse.bass as bass
from concourse import mybir


P128 = 128
SEQ, D = 256, 1024
NB = SEQ // P128
KT = D // P128
DEPTH = 2
D_POOL, D_GM, D_CONV = 256, 384, 384
WINDOWS = (2, 4, 8, 16)
GROUP = D_POOL // len(WINDOWS)
GM_HEADS = 4
GM_HD = D_GM // GM_HEADS
CHUNK = 64
TAPS = 31
D_IN = D_POOL + 2 * D_GM + 2 * D_CONV
U0, V0 = D_POOL, D_POOL + D_GM
CV0, CG0 = V0 + D_GM, V0 + D_GM + D_CONV
D_FF, D_FF_E, EXPERTS = 2816, 3584, 8
EPS, LN_EPS = 1e-6, 1e-5
HD, Q_HEADS = 64, 8
IDX_HEADS, IDX_DIM = 8, 32
PLE = 256
TOPK = 64
ALPHA = (2 * DEPTH) ** 0.25
NEG, TAKEN = -1e30, -3e38
QA, KA, VA = 0, 512, 640
QB, KB, VB = 768, 1280, 1344
QI, KI, WI = 1408, 1664, 1696
IN2 = 1704
C1, C2 = D_IN // 4, IN2 // 4
FN = 256
STEPS, STEPS_E = D_FF // FN, D_FF_E // FN
MOE_STEP0 = STEPS
B2_STEP0 = MOE_STEP0 + EXPERTS * STEPS_E
TOP_E = 2
MAX_OVER = (TOP_E * SEQ) // (P128 + 1)
R_N1, R_N2, R_DWB, R_LNG, R_LNB, R_PWB, R_PSC, R_DW = 0, 2, 4, 6, 8, 10, 12, 14
R_GMB = R_DW + DEPTH * TAPS
ROWS = R_GMB + DEPTH * GM_HEADS


def shape_constants():
    f32 = np.float32
    s = np.arange(SEQ)
    band = np.zeros((SEQ, len(WINDOWS), SEQ), f32)
    for g, w in enumerate(WINDOWS):
        inside = (s[:, None] <= s[None, :]) & (s[None, :] - s[:, None] < w)
        band[:, g] = inside / np.minimum(s + 1, w)[None, :].astype(f32) - np.eye(SEQ)
    i = np.arange(P128)
    causal = np.where(i[None, :] <= i[:, None], 0.0, NEG)
    older = np.where(i[None, :] > i[:, None], 0.0, NEG)
    masks = np.stack([np.concatenate([older, causal], 1),
                      np.concatenate([np.zeros_like(causal), causal], 1)], 1).astype(f32)
    freq = np.concatenate([
        f32(10000.0) ** (-np.arange(h, dtype=f32) / f32(h)) for h in (HD // 2, IDX_DIM // 2)]).astype(f32)
    e = np.arange(EXPERTS)
    lower = (e[None, :] < e[:, None]).astype(f32).reshape(1, -1)
    moe = np.stack([i[:, None] < i[None, :], np.ones((P128, P128)), np.broadcast_to(i[None, :], (P128, P128))], 1).astype(f32)
    return {"c_ident": np.eye(P128, dtype=f32), "c_band": band, "c_masks": masks,
            "c_freq": freq.reshape(1, -1), "c_lower": lower, "c_moe": moe}


def build_program(nc, T):
    f32 = mybir.dt.float32
    ALU = mybir.AluOpType
    ACT = mybir.ActivationFunctionType
    AX = mybir.AxisListType

    ctx = ExitStack()
    with ctx:
        def sb(name, shape, dt=f32):
            return ctx.enter_context(nc.sbuf_tensor(name, shape, dt))

        def sem(name):
            return ctx.enter_context(nc.semaphore(name))

        ident = sb("ident", [128, 128])
        band = sb("band", [128, NB, 4, SEQ])
        masks = sb("masks", [128, 2, 256])
        freq = sb("freq", [128, 48])
        lower = sb("lower", [128, EXPERTS, EXPERTS])
        parc = sb("parc", [128, KT, ROWS])
        router = sb("router", [128, KT, EXPERTS])
        poolw = sb("poolw", [128, DEPTH, 2, 128])
        wst = sb("wst", [128, DEPTH, GM_HEADS, 128])
        gmg = sb("gmg", [128, DEPTH, D_GM])
        sink = sb("sink", [128, DEPTH, Q_HEADS])
        ikg = sb("ikg", [128, DEPTH, IDX_DIM])
        ikb = sb("ikb", [128, DEPTH, IDX_DIM])
        pin = sb("pin", [128, NB, PLE])
        lnp = sb("lnp", [128, DEPTH, 4, D])
        lni = sb("lni", [128, 3, D])
        X = sb("X", [128, NB, D])
        hT = sb("hT", [128, KT, SEQ])
        XN = sb("XN", [128, NB, D])
        ringA = sb("ringA", [128, 2, 4096])
        ringD = sb("ringD", [128, 2, 2048])
        sil = sb("sil", [128, 2, NB, FN])
        am = sb("am", [128, 2, NB, FN])
        aT = sb("aT", [128, 2, 2, SEQ])
        gates = sb("gates", [128, NB, EXPERTS])
        cosA = sb("cosA", [128, NB, HD])
        sinA = sb("sinA", [128, NB, HD])
        cosI = sb("cosI", [128, NB, IDX_DIM])
        sinI = sb("sinI", [128, NB, IDX_DIM])
        small = sb("small", [128, 512])
        over_int = sb("over_int", [128, 1 + MAX_OVER], mybir.dt.int32)
        posi = sb("posi", [128, NB], mybir.dt.int32)
        SCR = sb("SCR", [128, 16600])
        ps = ctx.enter_context(nc.psum_tensor("ps", [128, 8, 512], f32))
        psf = ps[:, :, :].rearrange("p b n -> p (b n)")

        taken = [0]

        def col(n):
            taken[0] += n
            assert taken[0] <= 512
            return small[:, taken[0] - n:taken[0]]

        eps1, eps2, spare, spare2, spare3 = (col(1) for _ in range(5))
        ss, std, rstd = col(2), col(2), col(2)
        gm_ss, gm_std, gm_rstd = col(2), col(2), col(2)
        bst = col(2 * 2 * 6).rearrange("p (b c s) -> p b c s", b=2, c=2)
        mv = col(4).rearrange("p (b s) -> p b s", b=2)
        lstd, lrstd = col(2), col(2)
        posf = col(2)
        logit = col(16).rearrange("p (b e) -> p b e", b=2)
        gmax, gneg, gden, grec = col(2), col(2), col(2), col(2)
        gexp = col(16).rearrange("p (b e) -> p b e", b=2)
        rank = col(16).rearrange("p (b e) -> p b e", b=2)
        swa_m, swa_nm, swa_es, swa_den, swa_rd = (col(8) for _ in range(5))
        dsa_m, dsa_nm, dsa_den, dsa_rd = (col(8) for _ in range(4))
        top8 = col(8)
        wi = col(16).rearrange("p (b e) -> p b e", b=2)
        pos = col(16)
        over_flag, over_rank = col(EXPERTS), col(EXPERTS)
        over_pick = col(MAX_OVER * EXPERTS).rearrange("p (r e) -> p r e", r=MAX_OVER)
        over_list = col(1 + MAX_OVER)

        at = [0]

        def scr(n):
            at[0] += n
            assert at[0] <= 16600
            return SCR[:, at[0] - n:at[0]]

        Pm = scr(2 * D_IN).rearrange("p (b n) -> p b n", b=2)
        GH = scr(2 * D_CONV).rearrange("p (b n) -> p b n", b=2)
        CT = scr(3 * (SEQ + TAPS - 1)).rearrange("p (t n) -> p t n", t=3)
        ACC = scr(3 * SEQ).rearrange("p (t n) -> p t n", t=3)
        CN = scr(2 * D_CONV).rearrange("p (b n) -> p b n", b=2)
        HC = scr(3 * SEQ).rearrange("p (t n) -> p t n", t=3)
        GV = scr(2 * D_GM).rearrange("p (b n) -> p b n", b=2)
        YB = scr(2 * D_GM).rearrange("p (b n) -> p b n", b=2)
        YT = scr(2 * SEQ).rearrange("p (t n) -> p t n", t=2)
        MT = scr(KT * SEQ).rearrange("p (t n) -> p t n", t=KT)
        at[0] = 0
        par = scr(D)
        wsr = scr(DEPTH * GM_HEADS * 128).rearrange("p (l h n) -> p l h n", l=DEPTH, h=GM_HEADS)
        at[0] = 12000
        ang = scr(2 * 48).rearrange("p (b n) -> p b n", b=2)
        turn = scr(2 * 2 * 48).rearrange("p (c b n) -> p c b n", c=2, b=2)
        arg = scr(2 * 2 * 48).rearrange("p (c b n) -> p c b n", c=2, b=2)
        trig = scr(2 * 2 * 48).rearrange("p (c b n) -> p c b n", c=2, b=2)
        at[0] = 0
        XG = scr(KT * P128).rearrange("p (k n) -> p k n", k=KT)
        PG = scr(NB * P128).rearrange("p (b n) -> p b n", b=NB)
        GT = scr(SEQ)
        YE = scr(D)
        OP = scr(NB * P128).rearrange("p (b n) -> p b n", b=NB)
        OG = scr(NB * P128).rearrange("p (b n) -> p b n", b=NB)
        OA, OD = scr(4096), scr(2048)
        PL = hT[:, :, :].rearrange("p k n -> p (k n)").rearrange("p (b e n) -> p b e n", b=NB, e=EXPERTS)
        bandf = band[:, :, :, :].rearrange("p b w t -> p (b w t)")
        tri, ones, iota = (bandf[:, P128 * k:P128 * (k + 1)] for k in range(3))
        gain2 = bandf[:, 1024:2048]
        at[0] = 0
        P2 = scr(2 * IN2).rearrange("p (b n) -> p b n", b=2)
        region = at[0]
        RQ = scr(2 * 16 * HD).rearrange("p (b h d) -> p b h d", b=2, h=16)
        RK = scr(2 * 6 * HD).rearrange("p (b k u d) -> p b k u d", b=2, k=3, u=2)
        RQI = scr(2 * 256).rearrange("p (b h d) -> p b h d", b=2, h=8)
        RKI = scr(2 * 128).rearrange("p (b u d) -> p b u d", b=2, u=4)
        at[0] = region
        Sswa = scr(2048)
        Sdsa = scr(2048)
        TT = scr(14 * SEQ).rearrange("p (t n) -> p t n", t=14)
        pt_om = at[0]
        PT = scr(2048).rearrange("p (k h q) -> p k h q", k=2, h=8)
        OM = scr(2048).rearrange("p (b n) -> p b n", b=2)
        at[0] = pt_om
        T2 = scr(2 * 19 * HD).rearrange("p (b h c d) -> p b h c d", b=2, h=19, c=2)
        T2I = scr(2 * 8 * 32).rearrange("p (b h c d) -> p b h c d", b=2, h=8, c=2)
        T2K = scr(2 * 32).rearrange("p (b c d) -> p b c d", b=2, c=2)
        KN = scr(2 * 32).rearrange("p (b d) -> p b d", b=2)
        at[0] = pt_om + 4096
        score = scr(256)
        work = scr(256)
        dbias = scr(256)
        PPT = scr(2 * SEQ).rearrange("p (k n) -> p k n", k=2)
        MT2 = PT.rearrange("p k h q -> p (k h q)").rearrange("p (t n) -> p t n", t=KT)
        SGP = Sswa
        PLEO = Sdsa
        RL = XN[:, :, :].rearrange("p b n -> p (b n)")

        ident_loaded, x_loaded, par_loaded, mixer_loaded, attn_loaded, ln_loaded, pin_loaded = (
            sem(n) for n in ("ident_loaded", "x_loaded", "par_loaded", "mixer_loaded", "attn_loaded", "ln_loaded",
                             "pin_loaded"))
        zeroed = sem("zeroed")
        A_loaded = [sem("A_loaded0"), sem("A_loaded1")]
        D_loaded = [sem("D_loaded0"), sem("D_loaded1")]
        stored = sem("stored")
        pool_chain, act_chain, dve_chain = sem("pool_chain"), sem("act_chain"), sem("dve_chain")
        par_psum, parc_ready, wst_psum, wst_ready = sem("par_psum"), sem("parc_ready"), sem("wst_psum"), sem("wst_ready")
        args_ready, trig_ready, rope_tables = sem("args_ready"), sem("trig_ready"), sem("rope_tables")
        std_ready, xn_ready, hT_psum, hT_ready = sem("std_ready"), sem("xn_ready"), sem("hT_psum"), sem("hT_ready")
        proj_psum, proj_evac = sem("proj_psum"), sem("proj_evac")
        sg_ready, glu_ready, gluT_psum, ct_ready = sem("sg_ready"), sem("glu_ready"), sem("gluT_psum"), sem("ct_ready")
        gm_std_ready, gm_rstd_ready, gn_ready, gv_ready = sem("gm_std_ready"), sem("gm_rstd_ready"), sem("gn_ready"), sem("gv_ready")
        pool1_psum, yt_ready, pool2_psum, mt_ready = sem("pool1_psum"), sem("yt_ready"), sem("pool2_psum"), sem("mt_ready")
        z_psum, zb_ready, yb_ready, ybT_psum = sem("z_psum"), sem("zb_ready"), sem("yb_ready"), sem("ybT_psum")
        conv_ready, cl_psum, cl_var, cl_std, cn_ready, cnT_psum, hc_ready, pw_psum = (
            sem(n) for n in ("conv_ready", "cl_psum", "cl_var", "cl_std", "cn_ready", "cnT_psum", "hc_ready", "pw_psum"))
        mix_psum, x_ready = sem("mix_psum"), sem("x_ready")
        router_psum = sem("router_psum")
        gl_ready, ge_ready = sem("gl_ready"), sem("ge_ready")
        moe_loaded, xn_gained, sel_ready, pos_psum, pl_ready, over_ready = (
            sem(n) for n in ("moe_loaded", "xn_gained", "sel_ready", "pos_psum", "pl_ready", "over_ready"))
        xg_psum, xg_ready, pg_ready, gt_psum, gt_ready, ye_ready, scat_psum, moe_done = (
            sem(n) for n in ("xg_psum", "xg_ready", "pg_ready", "gt_psum", "gt_ready", "ye_ready", "scat_psum", "moe_done"))
        ov_free, ov_loaded, ov_places, ov_xg_psum, ov_xg, ov_gu, ov_silu, ov_act, ov_aT_psum, ov_aT, ov_sum, ov_scat, ov_chain = (
            sem(n) for n in ("ov_free", "ov_loaded", "ov_places", "ov_xg_psum", "ov_xg", "ov_gu", "ov_silu", "ov_act",
                             "ov_aT_psum", "ov_aT", "ov_sum", "ov_scat", "ov_chain"))
        gu_psum, silu_ready, act_ready, aT_psum, aT_ready, down_done, ffn_evac = (
            sem(n) for n in ("gu_psum", "silu_ready", "act_ready", "aT_psum", "aT_ready", "down_done", "ffn_evac"))
        ln_var, ln_std, xln_ready = sem("ln_var"), sem("ln_std"), sem("xln_ready")
        ik_var, ik_std, cos_part, rope_ready = sem("ik_var"), sem("ik_std"), sem("cos_part"), sem("rope_ready")
        qkT_psum, qkT_act, qkT_dve = sem("qkT_psum"), sem("qkT_act"), sem("qkT_dve")
        idx_psum, relu_ready, swa_psum, dsa_psum = sem("idx_psum"), sem("relu_ready"), sem("swa_psum"), sem("dsa_psum")
        swa_scored, dsa_scored = sem("swa_scored"), sem("dsa_scored")
        swa_exp, dsa_exp, pt_psum, pt_ready = sem("swa_exp"), sem("dsa_exp"), sem("pt_psum"), sem("pt_ready")
        pv_psum, om_ready, omT_psum, mt2_act, mt2_dve = (
            sem(n) for n in ("pv_psum", "om_ready", "omT_psum", "mt2_act", "mt2_dve"))
        pT_psum, pT_ready, pg_psum, pp_psum, sgp_ready, ple_read = (
            sem(n) for n in ("pT_psum", "pT_ready", "pg_psum", "pp_psum", "sgp_ready", "ple_read"))

        class Chain:

            def __init__(self, eng, s):
                self.eng, self.s, self.base, self.n, self.outer = eng, s, 0, 0, []

            def then(self, ins):
                self.n += 1
                ins.then_inc(self.s, 1)

            def wait(self, back=0):
                self.eng.wait_ge(self.s, self.base + self.n - back)

            def link(self, ins):
                self.then(ins)
                self.wait()

            def enter(self, turn, per):
                self.outer.append((self.base, self.n))
                self.base, self.n = (self.base + self.n) + turn * per, 0

            def leave(self, per, turns):
                assert self.n == per, (self.n, per)
                self.base, self.n = self.outer.pop()
                self.n += per * turns

        def place(h):
            return (h % 2) * 4 + h // 2

        def wait(eng, s, value):
            if not isinstance(value, int) or value > 0:
                eng.wait_ge(s, value)

        def overflowing(eng, body):
            eng.wait_ge(over_ready, 1)
            n = eng.value_load(over_int[0:1, 0:1], min_val=0, max_val=MAX_OVER)
            with eng.Fori(0, MAX_OVER) as r:
                with eng.If(r < n):
                    body(r, eng.value_load(over_int[0:1, bass.ds(r + 1, 1)], min_val=0, max_val=EXPERTS - 1))

        block = ctx.enter_context(nc.Block())

        @block.sync
        def _(sp):
            def cut(w, e, r0, rows, c0, n):
                return w[bass.ds(e, 1), bass.ds(r0, rows), bass.ds(c0, n)].rearrange("o (k p) n -> p (o k) n", p=128)

            def columns(slot, w, e, c0, n):
                dst = ringA[:, slot, 0:KT * n].rearrange("p (k n) -> p k n", k=KT)
                sp.dma_start(dst, cut(w, e, 0, D, c0, n)).then_inc(A_loaded[slot], 32)

            def gate_up(slot, wg, wu, e, cg, cu):
                dst = ringA[:, slot, :].rearrange("p (k u n) -> p k u n", k=KT, u=2)
                sp.dma_start(dst[:, :, 0, :], cut(wg, e, 0, D, cg, FN)).then_inc(A_loaded[slot], 16)
                sp.dma_start(dst[:, :, 1, :], cut(wu, e, 0, D, cu, FN)).then_inc(A_loaded[slot], 16)

            def rows(slot, w, e, r0):
                dst = ringD[:, slot, :].rearrange("p (k n) -> p k n", k=2)
                sp.dma_start(dst, cut(w, e, r0, FN, 0, D)).then_inc(D_loaded[slot], 16)

            def step_weights(wg, wu, wd, e, up0, s0, y, j):
                sp.wait_ge(gu_psum, s0 + y - 1)
                gate_up(j, wg, wu, e, y * FN, y * FN + up0)
                down_rows(wd, e, s0, y - 2, (j + 1) % 2)

            def down_rows(wd, e, s0, y, slot):
                wait(sp, down_done, s0 + y - 1)
                rows(slot, wd, e, y * FN)

            def feed_forward(wg, wu, wd, e, up0, s0, n):
                gate_up(1, wg, wu, e, FN, up0 + FN)
                step_weights(wg, wu, wd, e, up0, s0, 2, 0)
                step_weights(wg, wu, wd, e, up0, s0, 3, 1)
                with sp.Fori(2, n // 2) as i:
                    for j in range(2):
                        step_weights(wg, wu, wd, e, up0, s0, 2 * i + j, j)
                if n % 2:
                    step_weights(wg, wu, wd, e, up0, s0, n - 1, 0)
                down_rows(wd, e, s0, n - 2, (n - 1) % 2)
                down_rows(wd, e, s0, n - 1, n % 2)

            for l in range(DEPTH):
                for c in range(4):
                    if c >= 2:
                        sp.wait_ge(proj_psum, 4 * l + c - 1)
                    elif l:
                        sp.wait_ge(gu_psum, STEPS)
                    columns(c % 2, T["w_in"], l, D_IN - C1 * (c + 1), C1)
                if l:
                    sp.wait_ge(down_done, STEPS)
                sp.dma_start(ringD[:, 0, 0:3 * D_CONV].rearrange("p (k n) -> p k n", k=3),
                             cut(T["conv_pw_w"], l, 0, D_CONV, 0, D_CONV)).then_inc(D_loaded[0], 16)
                for n in range(2):
                    sp.wait_ge(proj_psum, 4 * l + n + 3)
                    columns(n, T["w_out"], l, 512 * n, 512)
                if l == 0:
                    sp.wait_ge(mix_psum, 1)
                    gate_up(0, T["ffn_wg"], T["ffn_wu"], 0, 0, 0)
                    sp.wait_ge(mix_psum, 2)
                    feed_forward(T["ffn_wg"], T["ffn_wu"], T["ffn_wd"], 0, 0, 0, STEPS)
            EG, EU, ED = T["moe_wg"], T["moe_wu"], T["moe_wd"]
            sp.wait_ge(mix_psum, 3)
            gate_up(0, EG, EU, 0, 0, 0)
            sp.wait_ge(mix_psum, 4)
            gate_up(1, EG, EU, 0, FN, FN)

            def further_steps(e, s0):
                with sp.Fori(0, STEPS_E // 2 - 1) as i:
                    for j in range(2):
                        step_weights(EG, EU, ED, e, 0, s0, 2 * i + 2 + j, j)

            further_steps(0, MOE_STEP0)
            with sp.Fori(1, EXPERTS) as e:
                s0 = MOE_STEP0 + STEPS_E * e
                for j in range(2):
                    sp.wait_ge(gu_psum, s0 + j - 1)
                    gate_up(j, EG, EU, e, j * FN, j * FN)
                    down_rows(ED, e - 1, s0 - STEPS_E, STEPS_E - 2 + j, (j + 1) % 2)
                further_steps(e, s0)
            for j in range(2):
                down_rows(ED, EXPERTS - 1, B2_STEP0 - STEPS_E, STEPS_E - 2 + j, (j + 1) % 2)
            def second_block(r, e):
                with sp.Fori(0, STEPS_E) as i:
                    sp.wait_ge(ov_free, STEPS_E * r + i + 1)
                    dst = OA.rearrange("p (k u n) -> p k u n", k=KT, u=2)
                    sp.dma_start(dst[:, :, 0, :], cut(EG, e, 0, D, i * FN, FN)).then_inc(ov_loaded, 16)
                    sp.dma_start(dst[:, :, 1, :], cut(EU, e, 0, D, i * FN, FN)).then_inc(ov_loaded, 16)
                    sp.dma_start(OD.rearrange("p (k n) -> p k n", k=2), cut(ED, e, i * FN, FN, 0, D)).then_inc(ov_loaded, 16)

            overflowing(sp, second_block)
            with sp.Fori(0, DEPTH) as l:
                q = l + 2
                s0 = B2_STEP0 + STEPS * l
                sp.wait_ge(gu_psum, s0)
                for c in range(4):
                    if c >= 2:
                        sp.wait_ge(proj_psum, 4 * q + c - 1)
                    columns(c % 2, T["w_in_2"], l, C2 * c, C2)
                sp.wait_ge(down_done, s0)
                rows(0, T["w_pp_2"], l, 0)
                sp.dma_start(pin[:, :, :], T["p_2"][bass.ds(l, 1), 0, :, :].rearrange("o (b p) n -> p (o b) n", p=128)
                             ).then_inc(pin_loaded, 16)
                for n in range(2):
                    sp.wait_ge(proj_psum, 4 * q + n + 3)
                    columns(n, T["w_o_2"], l, 512 * n, 512)
                for n in range(2):
                    sp.wait_ge(mix_psum, 2 * q + n + 1)
                    columns(n, T["w_pg_2"], l, 512 * n, 512)
                sp.wait_ge(pg_psum, 2 * l + 1)
                gate_up(0, T["w_gu_2"], T["w_gu_2"], l, 0, D_FF)
                sp.wait_ge(pp_psum, l + 1)
                feed_forward(T["w_gu_2"], T["w_gu_2"], T["w_down_2"], l, D_FF, s0, STEPS)
            sp.wait_ge(xln_ready, 1 + 2 * DEPTH)
            sp.dma_start(T["out"].rearrange("o (b p) d -> p (o b) d", p=128), X[:, :, :]).then_inc(stored, 16)
            sp.wait_ge(stored, 16)

        @block.tensor
        def _(pe):
            mm = nc.tensor.matmul

            def tr(out, in_, n=128):
                return nc.tensor.transpose(out, in_, ident[0:n, 0:n])

            def slotA(slot, n):
                return ringA[:, slot, 0:KT * n].rearrange("p (k n) -> p k n", k=KT)

            def to_features(t, src):
                for k in range(KT):
                    for b in range(NB):
                        c = (k % 2) * SEQ + b * 128
                        m = tr(ps[:, k // 2, c:c + 128], src[:, b, k * 128:(k + 1) * 128])
                    if k % 2:
                        m.then_inc(hT_psum, 1)
                pe.wait_ge(hT_ready, 8 * (t + 1))

            def project(q, c, n, use):
                pe.wait_ge(A_loaded[c % 2], 32 * use)
                if c >= 2:
                    pe.wait_ge(proj_evac, 4 * q + c - 1)
                w = slotA(c % 2, n)
                for k in range(KT):
                    for b in range(NB):
                        m = mm(ps[:, 4 + 2 * (c % 2) + b, 0:n], hT[:, k, b * 128:(b + 1) * 128], w[:, k, :],
                               start=(k == 0), stop=(k == KT - 1))
                m.then_inc(proj_psum, 1)

            def full_depth(lhs, slot, use, bank_of, done):
                pe.wait_ge(A_loaded[slot], 32 * use)
                w = slotA(slot, 512)
                for k in range(KT):
                    for b in range(NB):
                        m = mm(ps[:, bank_of(b), :], lhs[:, k, b * 128:(b + 1) * 128], w[:, k, :],
                               start=(k == 0), stop=(k == KT - 1))
                m.then_inc(done, 1)

            def up(s, par_, use, reused=True, x=hT, blocks=NB):
                pe.wait_ge(A_loaded[par_], 32 * use)
                if reused:
                    pe.wait_ge(aT_ready, s - 1)
                w = slotA(par_, 512)
                for k in range(KT):
                    for b in range(blocks):
                        m = mm(ps[:, 2 * par_ + b, :], x[:, k, b * 128:(b + 1) * 128], w[:, k, :],
                               start=(k == 0), stop=(k == KT - 1))
                m.then_inc(gu_psum, 1)

            def turn_act(s, par_, blocks=NB):
                pe.wait_ge(act_ready, s + 1)
                for f in range(2):
                    for b in range(blocks):
                        c = f * SEQ + b * 128
                        m = tr(ps[:, 2 * par_, c:c + 128], am[:, par_, b, f * 128:(f + 1) * 128])
                m.then_inc(aT_psum, 1)

            def down(s, par_, use, first=False, last=False, blocks=NB):
                slot = (par_ + 1) % 2
                pe.wait_ge(aT_ready, s + 1)
                pe.wait_ge(D_loaded[slot], 16 * use)
                w = ringD[:, slot, :].rearrange("p (k n) -> p k n", k=2)
                for f in range(2):
                    for n in range(2):
                        for b in range(blocks):
                            m = mm(ps[:, 4 + 2 * b + n, :], aT[:, par_, f, b * 128:(b + 1) * 128],
                                   w[:, f, n * 512:(n + 1) * 512],
                                   start=(first and f == 0), stop=(last and f == 1))
                m.then_inc(down_done, 1)

            pe.wait_ge(ident_loaded, 16)
            pe.wait_ge(par_loaded, 16 * 9)
            for k in range(KT):
                m = tr(ps[:, k // 4, (k % 4) * 128:(k % 4) * 128 + ROWS], par[0:ROWS, k * 128:(k + 1) * 128], ROWS)
            m.then_inc(par_psum, 1)
            pe.wait_ge(mixer_loaded, 16 * 5)
            for l in range(DEPTH):
                for h in range(GM_HEADS):
                    m = tr(ps[:, 2 + l, h * 128:(h + 1) * 128], wsr[:, l, h, :])
            m.then_inc(wst_psum, 1)
            pe.wait_ge(parc_ready, 2)
            pe.wait_ge(wst_ready, 2)

            def pipeline(s0, a0, a1, d0, d1, n, reused):
                up(s0, 0, a0 + 1, reused)
                up(s0 + 1, 1, a1 + 1, reused)
                turn_act(s0, 0)
                up(s0 + 2, 0, a0 + 2)
                turn_act(s0 + 1, 1)
                down(s0, 0, d1 + 1, first=True)
                with pe.Fori(0, (n - 3) // 2) as i:
                    s = s0 + 2 * i + 3
                    up(s, 1, a1 + 2 + i)
                    turn_act(s - 1, 0)
                    down(s - 2, 1, d0 + 1 + i)
                    up(s + 1, 0, a0 + 3 + i)
                    turn_act(s, 1)
                    down(s - 1, 0, d1 + 2 + i)
                s = s0 + n
                if n % 2:
                    turn_act(s - 1, 0)
                    down(s - 2, 1, d0 + n // 2)
                    down(s - 1, 0, d1 + n // 2 + 1, last=True)
                else:
                    up(s - 1, 1, a1 + n // 2)
                    turn_act(s - 2, 0)
                    down(s - 3, 1, d0 + n // 2 - 1)
                    turn_act(s - 1, 1)
                    down(s - 2, 0, d1 + n // 2)
                    down(s - 1, 1, d0 + n // 2, last=True)

            a_base = [(0, 0), (9, 8)]
            for l in range(DEPTH):
                pe.wait_ge(xn_ready, 2 * (2 * l + 1))
                to_features(2 * l, XN)
                a0, a1 = a_base[l]
                for c in range(3):
                    project(l, c, C1, (a0, a1)[c % 2] + c // 2 + 1)
                pe.wait_ge(glu_ready, l + 1)
                for t in range(3):
                    for b in range(NB):
                        c = (t % 2) * SEQ + b * 128
                        m = tr(ps[:, t // 2, c:c + 128], GH[:, b, t * 128:(t + 1) * 128])
                m.then_inc(gluT_psum, 1)
                project(l, 3, C1, a1 + 2)
                pe.wait_ge(proj_evac, 4 * l + 4)
                for g in range(2):
                    for b in range(NB):
                        m = mm(ps[:, 2 + g, :], Pm[:, b, g * 128:(g + 1) * 128],
                               band[:, b, 2 * g:2 * g + 2, :], start=(b == 0), stop=(b == NB - 1))
                m.then_inc(pool1_psum, 1)
                pe.wait_ge(gv_ready, l + 1)
                for b in range(NB):
                    for h in range(GM_HEADS):
                        m = mm(ps[:, 4 + b, h * GM_HD:(h + 1) * GM_HD], wst[:, l, h, :],
                               GV[:, b, h * GM_HD:(h + 1) * GM_HD], start=True, stop=True)
                m.then_inc(z_psum, 1)
                pe.wait_ge(yt_ready, 4 * (l + 1))
                for g in range(2):
                    m = mm(ps[:, 2, g * SEQ:(g + 1) * SEQ], poolw[:, l, g, :], YT[:, g, :], start=True, stop=True)
                m.then_inc(pool2_psum, 1)
                pe.wait_ge(yb_ready, l + 1)
                for t in range(3):
                    for b in range(NB):
                        c = (t % 2) * SEQ + b * 128
                        m = tr(ps[:, 6 + t // 2, c:c + 128], YB[:, b, t * 128:(t + 1) * 128])
                m.then_inc(ybT_psum, 1)
                pe.wait_ge(conv_ready, 3 * (l + 1))
                for b in range(NB):
                    for t in range(3):
                        m = tr(ps[:, b, t * 128:(t + 1) * 128], ACC[:, t, b * 128:(b + 1) * 128])
                m.then_inc(cl_psum, 1)
                pe.wait_ge(cn_ready, l + 1)
                pe.wait_ge(mt_ready, 7 * l + 4)
                for t in range(3):
                    for b in range(NB):
                        c = (t % 2) * SEQ + b * 128
                        m = tr(ps[:, 2 + t // 2, c:c + 128], CN[:, b, t * 128:(t + 1) * 128])
                m.then_inc(cnT_psum, 1)
                pe.wait_ge(hc_ready, 3 * (l + 1))
                pe.wait_ge(D_loaded[0], 16 * (6 * l + 1))
                pw = ringD[:, 0, 0:3 * D_CONV].rearrange("p (k n) -> p k n", k=3)
                for d in range(3):
                    for k in range(3):
                        m = mm(ps[:, d // 2, (d % 2) * SEQ:(d % 2 + 1) * SEQ], pw[:, k, d * 128:(d + 1) * 128],
                               HC[:, k, :], start=(k == 0), stop=(k == 2))
                m.then_inc(pw_psum, 1)
                pe.wait_ge(mt_ready, 7 * (l + 1))
                for n in range(2):
                    full_depth(MT, n, (a0, a1)[n] + 3, lambda b: 4 + 2 * b + n, mix_psum)
                pe.wait_ge(xn_ready, 2 * (2 * l + 2))
                to_features(2 * l + 1, XN)
                if l == 0:
                    pipeline(0, 3, 3, 1, 0, STEPS, False)
            pe.wait_ge(attn_loaded, 16 * 8)
            for b in range(NB):
                for k in range(KT):
                    m = mm(ps[:, 4, b * EXPERTS:(b + 1) * EXPERTS], hT[:, k, b * 128:(b + 1) * 128], router[:, k, :],
                           start=(k == 0), stop=(k == KT - 1))
            m.then_inc(router_psum, 1)
            pe.wait_ge(sel_ready, 1)
            pe.wait_ge(moe_loaded, 16 * 2)
            for b in range(NB):
                for c in range(b + 1):
                    mm(ps[:, 5, b * EXPERTS:(b + 1) * EXPERTS], tri if c == b else ones, rank[:, c, :],
                       start=(c == 0), stop=(c == b))
            for c in range(NB):
                m = mm(ps[:, 5, NB * EXPERTS:(NB + 1) * EXPERTS], ones, rank[:, c, :], start=(c == 0), stop=(c == NB - 1))
            m.then_inc(pos_psum, 1)

            def gather(places, done):
                for k in range(KT):
                    for b in range(NB):
                        m = mm(ps[:, 6 + k // 4, (k % 4) * 128:(k % 4 + 1) * 128], XN[:, b, k * 128:(k + 1) * 128], places(b),
                               start=(b == 0), stop=(b == NB - 1))
                m.then_inc(done, 1)

            def places_of(e):
                return lambda b: PL[:, b, bass.ds(e, 1), :].rearrange("p o n -> p (o n)")

            def turn_gates(src, done):
                for b in range(NB):
                    m = tr(ps[:, 1, b * 128:(b + 1) * 128], src[:, b, :])
                m.then_inc(done, 1)

            def scatter(done):
                for b in range(NB):
                    for n in range(2):
                        m = mm(ps[:, (1 + 2 * n, 6 + n)[b], :], GT[:, b * 128:(b + 1) * 128], YE[:, n * 512:(n + 1) * 512],
                               start=True, stop=True)
                m.then_inc(done, 1)

            def up_e(s, par_, use, reused=True):
                up(s, par_, use, reused, XG, 1)

            def expert(e, s, first=False, last=False):
                a, d = 12 + 7 * e, 7 + 7 * e
                pe.wait_ge(xg_ready, 2 * e + 2)
                up_e(s, 0, a + 1, not first)
                if not first:
                    turn_act(s - 1, 1, 1)
                    down(s - 2, 0, d - 1, blocks=1)
                up_e(s + 1, 1, a, not first)
                turn_act(s, 0, 1)
                if not first:
                    down(s - 1, 1, d, last=True, blocks=1)
                up_e(s + 2, 0, a + 2)
                turn_act(s + 1, 1, 1)
                if not first:
                    pe.wait_ge(gt_ready, e)
                    pe.wait_ge(ye_ready, e)
                    scatter(scat_psum)
                down(s, 0, d, first=True, blocks=1)
                up_e(s + 3, 1, a + 1)
                turn_act(s + 2, 0, 1)
                down(s + 1, 1, d + 1, blocks=1)
                pe.wait_ge(pg_ready, e + 1)
                if not first:
                    pe.wait_ge(ffn_evac, e)
                turn_gates(PG, gt_psum)
                if not last:
                    gather(places_of(e + 1), xg_psum)
                with pe.Fori(0, STEPS_E // 2 - 2) as i:
                    t = s + 2 * i + 4
                    up_e(t, 0, a + 3 + i)
                    turn_act(t - 1, 1, 1)
                    down(t - 2, 0, d + 1 + i, blocks=1)
                    up_e(t + 1, 1, a + 2 + i)
                    turn_act(t, 0, 1)
                    down(t - 1, 1, d + 2 + i, blocks=1)

            pe.wait_ge(xn_gained, 1)
            pe.wait_ge(pl_ready, 1)
            gather(places_of(0), xg_psum)
            expert(0, MOE_STEP0, first=True)
            with pe.Fori(1, EXPERTS - 1) as e:
                expert(e, MOE_STEP0 + STEPS_E * e)
            expert(EXPERTS - 1, B2_STEP0 - STEPS_E, last=True)
            s = B2_STEP0
            turn_act(s - 1, 1, 1)
            down(s - 2, 0, 62, blocks=1)
            down(s - 1, 1, 63, last=True, blocks=1)
            pe.wait_ge(gt_ready, EXPERTS)
            pe.wait_ge(ye_ready, EXPERTS)
            scatter(scat_psum)

            def second_block(r, e):
                pe.wait_ge(ov_places, r + 1)
                gather(lambda b: OP[:, b, :], ov_xg_psum)
                turn_gates(OG, ov_xg_psum)
                wa = OA.rearrange("p (k n) -> p k n", k=KT)
                wd = OD.rearrange("p (k n) -> p k n", k=2)
                with pe.Fori(0, STEPS_E) as i:
                    t = STEPS_E * r + i
                    pe.wait_ge(ov_xg, 2 * r + 2)
                    pe.wait_ge(ov_loaded, 48 * t + 48)
                    for k in range(KT):
                        m = mm(ps[:, 0, :], XG[:, k, :], wa[:, k, :], start=(k == 0), stop=(k == KT - 1))
                    m.then_inc(ov_gu, 1)
                    pe.wait_ge(ov_act, t + 1)
                    for f in range(2):
                        m = tr(ps[:, 2, f * 128:(f + 1) * 128], am[:, 0, 0, f * 128:(f + 1) * 128])
                    m.then_inc(ov_aT_psum, 1)
                    pe.wait_ge(ov_aT, t + 1)
                    for n in range(2):
                        for f in range(2):
                            m = mm(ps[:, 4 + n, :], aT[:, 0, f, 0:128], wd[:, f, n * 512:(n + 1) * 512],
                                   start=(f == 0), stop=(f == 1))
                    m.then_inc(ov_free, 1)
                pe.wait_ge(ov_sum, STEPS_E * r + STEPS_E)
                scatter(ov_scat)

            overflowing(pe, second_block)

            with pe.Fori(0, DEPTH) as l:
                q = l + 2
                a0, a1, d0, d1 = 68 + 10 * l, 67 + 9 * l, 63 + 6 * l, 62 + 6 * l
                pe.wait_ge(xln_ready, 2 * l + 1)
                to_features(2 * l + 4, X)
                for c in range(4):
                    project(q, c, C2, (a0, a1)[c % 2] + c // 2 + 1)
                pe.wait_ge(rope_ready, l + 1)
                flat = [RQI[:, :, 0:4, :], RQI[:, :, 4:8, :], RKI[:, :, :, :],
                        RK[:, :, 2, :, :], RK[:, :, 0, :, :], RK[:, :, 1, :, :]]
                flat += [RQ[:, :, 2 * t:2 * t + 2, :] for t in range(8)]
                for t in range(14):
                    for b in range(NB):
                        c = (t % 2) * SEQ + b * 128
                        m = tr(ps[:, t // 2, c:c + 128], flat[t][:, b].rearrange("p u d -> p (u d)"))
                    if t % 2:
                        m.then_inc(qkT_psum, 1)
                pe.wait_ge(qkT_act, 4 * (l + 1))
                pe.wait_ge(qkT_dve, 3 * (l + 1))
                for b in range(NB):
                    nk = 128 * (b + 1)
                    tok = slice(b * 128, (b + 1) * 128)
                    if b:
                        pe.wait_ge(dsa_scored, 2 * l + b)
                    for h in range(IDX_HEADS):
                        r = slice(32 * (h % 4), 32 * (h % 4) + 32)
                        m = mm(ps[:, h % 4, h // 4 * nk:(h // 4 + 1) * nk], TT[r, h // 4, tok], TT[r, 2, 0:nk],
                               start=True, stop=True)
                    m.then_inc(idx_psum, 1)
                    if b:
                        pe.wait_ge(om_ready, 4 * l + 2)
                    for h in range(Q_HEADS):
                        r = slice(64 * (h % 2), 64 * (h % 2) + 64)
                        c = 2048 + place(h) * nk
                        m = mm(psf[:, c:c + nk], TT[r, 6 + h // 2, tok], TT[r, 4 + h // 4, 0:nk], start=True, stop=True)
                    m.then_inc(swa_psum, 1)
                    pe.wait_ge(relu_ready, 2 * l + b + 1)
                    for h in range(Q_HEADS):
                        r = slice(64 * (h % 2), 64 * (h % 2) + 64)
                        c = place(h) * nk
                        m = mm(psf[:, c:c + nk], TT[r, 10 + h // 2, tok], TT[r, 3, 0:nk], start=True, stop=True)
                    m.then_inc(dsa_psum, 1)
                    for kind, S, expd, vcol in ((0, Sswa, swa_exp, lambda h: VA + HD * (h // 4)),
                                                (1, Sdsa, dsa_exp, lambda h: VB)):
                        pe.wait_ge(expd, 8 * (2 * l + b + 1))
                        g0 = 12 * l + 4 * b + 2 * (b + 1) * kind
                        for g in range(2 * (b + 1)):
                            if kind or g >= 2 or b:
                                pe.wait_ge(pt_ready, g0 + g - 1)
                            kt, h0 = g // 2, 4 * (g % 2)
                            for h in range(h0, h0 + 4):
                                m = tr(ps[:, 4 + g % 2, (h - h0) * 128:(h - h0 + 1) * 128],
                                       S[:, h * nk + kt * 128:h * nk + (kt + 1) * 128])
                            m.then_inc(pt_psum, 1)
                        pe.wait_ge(pt_ready, g0 + 2 * (b + 1))
                        for h in range(Q_HEADS):
                            p = place(h)
                            for kt in range(b + 1):
                                m = mm(ps[:, 6 + kind, p * HD:(p + 1) * HD], PT[:, kt, p, :],
                                       P2[:, kt, vcol(h):vcol(h) + HD], start=(kt == 0), stop=(kt == b))
                        m.then_inc(pv_psum, 1)
                pe.wait_ge(om_ready, 4 * (l + 1))
                for t in range(KT):
                    for b in range(NB):
                        c = (t % 2) * SEQ + b * 128
                        m = tr(ps[:, t // 2, c:c + 128], OM[:, b, t * 128:(t + 1) * 128])
                    if t % 2:
                        m.then_inc(omT_psum, 1)
                pe.wait_ge(mt2_act, 2 * (l + 1))
                pe.wait_ge(mt2_dve, 2 * (l + 1))
                for n in range(2):
                    full_depth(MT2, n, (a0, a1)[n] + 3, lambda b: 4 + 2 * b + n, mix_psum)
                pe.wait_ge(pin_loaded, 16 * (l + 1))
                for k in range(2):
                    for b in range(NB):
                        c = k * SEQ + b * 128
                        m = tr(ps[:, 0, c:c + 128], pin[:, b, k * 128:(k + 1) * 128])
                m.then_inc(pT_psum, 1)
                pe.wait_ge(pT_ready, l + 1)
                pe.wait_ge(xln_ready, 2 * l + 2)
                to_features(2 * l + 5, X)
                for n in range(2):
                    full_depth(hT, n, (a0, a1)[n] + 4, lambda b: 4 + 2 * b + n, pg_psum)
                pe.wait_ge(D_loaded[0], 16 * (d0 + 1))
                w = ringD[:, 0, :].rearrange("p (k n) -> p k n", k=2)
                for k in range(2):
                    for n in range(2):
                        for b in range(NB):
                            m = mm(ps[:, 2 * b + n, :], PPT[:, k, b * 128:(b + 1) * 128], w[:, k, n * 512:(n + 1) * 512],
                                   start=(k == 0), stop=(k == 1))
                m.then_inc(pp_psum, 1)
                pe.wait_ge(ple_read, l + 1)
                pipeline(B2_STEP0 + STEPS * l, a0 + 4, a1 + 4, d0 + 1, d1, STEPS, False)

        @block.gpsimd
        def _(pool):
            TTn = nc.gpsimd.tensor_tensor
            nc.gpsimd.memset(par, 0.0).then_inc(zeroed, 1)
            nc.gpsimd.memset(poolw[:, :, :, :], 0.0).then_inc(zeroed, 1)
            nc.gpsimd.memset(CT[:, :, 0:TAPS - 1], 0.0).then_inc(zeroed, 1)
            nc.gpsimd.memset(wst[:, :, :, 0:64], 0.0).then_inc(zeroed, 1)
            nc.gpsimd.memset(eps1, EPS).then_inc(zeroed, 1)
            nc.gpsimd.memset(eps2, LN_EPS).then_inc(zeroed, 1)
            pool.wait_ge(mixer_loaded, 16 * 5)
            for l in range(DEPTH):
                pool.wait_ge(gn_ready, 2 * (l + 1))
                TTn(GV, GV, gmg[:, l, :].unsqueeze(1).broadcast_to([128, NB, D_GM]), ALU.mult).then_inc(gv_ready, 1)
                pool.wait_ge(zb_ready, 8 * (l + 1))
                TTn(YB, YB, Pm[:, :, U0:U0 + D_GM], ALU.mult).then_inc(yb_ready, 1)
            pool.wait_ge(moe_loaded, 16 * 2)
            pool.wait_ge(hT_psum, 16)
            TTn(XN[:, :, :], XN[:, :, :], gain2.unsqueeze(1).broadcast_to([128, NB, D]), ALU.mult).then_inc(xn_gained, 1)
            pool.wait_ge(rope_tables, 8)
            with pool.Fori(0, DEPTH) as l:
                pool.wait_ge(proj_evac, 4 * l + 12)

                def heads(c0, n, d):
                    return P2[:, :, c0:c0 + n * d].rearrange("p b (h d) -> p b h d", d=d)

                def over(table, n, d):
                    return table[:, :, :].unsqueeze(2).broadcast_to([128, NB, n, d])

                TTn(RQI, heads(QI, 8, 32), over(cosI, 8, 32), ALU.mult).then_inc(cos_part, 1)
                TTn(RQ[:, :, 0:8, :], heads(QA, 8, HD), over(cosA, 8, HD), ALU.mult).then_inc(cos_part, 1)
                TTn(RQ[:, :, 8:16, :], heads(QB, 8, HD), over(cosA, 8, HD), ALU.mult).then_inc(cos_part, 1)
                for k, c0 in ((0, KA), (1, KA + HD), (2, KB)):
                    TTn(RK[:, :, k, :, :], P2[:, :, c0:c0 + HD].unsqueeze(2).broadcast_to([128, NB, 2, HD]),
                        over(cosA, 2, HD), ALU.mult).then_inc(cos_part, 1)

        @block.scalar
        def _(act):
            fn = nc.scalar.activation
            chain = Chain(act, act_chain)

            def load(dst, src, s):
                act.dma_start(dst, src).then_inc(s, 16)

            def rep(ap):
                return ap.partition_broadcast(128)

            load(ident[:, :], T["c_ident"], ident_loaded)
            load(X[:, :, :], T["x"].rearrange("o (b p) d -> p (o b) d", p=128), x_loaded)
            act.wait_ge(zeroed, 6)
            for r, n in ((R_N1, "norm1_g"), (R_N2, "norm2_g"), (R_DWB, "conv_dw_b"), (R_LNG, "conv_ln_g"),
                         (R_LNB, "conv_ln_b"), (R_PWB, "conv_pw_b"), (R_PSC, "pool_scale")):
                load(par[r:r + DEPTH, 0:T[n].shape[1]], T[n], par_loaded)
            load(par[R_DW:R_DW + DEPTH * TAPS, 0:D_CONV], T["conv_dw_w"].rearrange("l t c -> (l t) c"), par_loaded)
            load(par[R_GMB:ROWS, 0:128], T["gm_b"].rearrange("l h i -> (l h) i"), par_loaded)
            load(wsr, T["gm_ws"].rearrange("l h i j -> i l h j"), mixer_loaded)
            for g in range(2):
                load(poolw[64 * g:64 * g + 64, :, :, 64 * g:64 * g + 64],
                     T["pool_w"].rearrange("l (r g) c d -> g c l r d", g=2)[g], mixer_loaded)
            load(gmg[:, :, :], rep(T["gm_norm_g"]), mixer_loaded)
            load(band[:, :, :, :], T["c_band"].rearrange("(b p) w t -> p b w t", p=128), mixer_loaded)
            load(masks[:, :, :], T["c_masks"], attn_loaded)
            load(freq[:, :], rep(T["c_freq"][0]), attn_loaded)
            load(lower[:, :, :].rearrange("p a b -> p (a b)"), rep(T["c_lower"][0]), attn_loaded)
            with nc.allow_non_contiguous_dma(reason="256 positions, one per partition"):
                load(posi[:, :], T["positions_2"].rearrange("o (b p) -> p (o b)", p=128), attn_loaded)
            load(sink[:, :, :], rep(T["attn_sinks_2"]), attn_loaded)
            load(ikg[:, :, :], rep(T["idx_k_g_2"]), attn_loaded)
            load(ikb[:, :, :], rep(T["idx_k_b_2"]), attn_loaded)
            load(router[:, :, :], T["moe_router"][0].rearrange("(k p) e -> p k e", p=128), attn_loaded)
            for k, n in enumerate(("final_g", "ln_in_g_2", "ln_in_b_2")):
                load(lni[:, k, :], rep(T[n]), ln_loaded)
            for k, n in enumerate(("ln1_g_2", "ln1_b_2", "ln2_g_2", "ln2_b_2")):
                load(lnp[:, :, k, :], rep(T[n]), ln_loaded)

            def rms(t):
                for b in range(NB):
                    chain.then(fn(XN[:, b, :], X[:, b, :], ACT.Square, accum_out=ss[:, b:b + 1]))
                chain.wait()
                fn(std, ss, ACT.Sqrt, scale=1.0 / D, bias=eps1).then_inc(std_ready, 1)

            def features(t, gain):
                for k in range(4):
                    act.wait_ge(hT_psum, 4 * t + k // 2 + 1)
                    src = ps[:, k // 2, (k % 2) * SEQ:(k % 2 + 1) * SEQ]
                    fn(hT[:, k, :], src, ACT.Copy, scale=1.0 if gain is None else gain(k)).then_inc(hT_ready, 1)

            def silu(s, par_):
                act.wait_ge(gu_psum, s + 1)
                wait(act, act_ready, s - 1)
                fn(sil[:, par_, :, :], ps[:, 2 * par_:2 * par_ + 2, 0:FN], ACT.Silu).then_inc(silu_ready, 1)

            def act_out(s, par_):
                act.wait_ge(aT_psum, s + 1)
                wait(act, down_done, s - 1)
                fn(aT[:, par_, :, :].rearrange("p f n -> p (f n)"), ps[:, 2 * par_, :], ACT.Copy).then_inc(aT_ready, 1)

            def silu_e(s, par_):
                act.wait_ge(gu_psum, s + 1)
                act.wait_ge(act_ready, s - 1)
                fn(sil[:, par_, 0, :], ps[:, 2 * par_, 0:FN], ACT.Silu).then_inc(silu_ready, 1)

            def act_out_e(s, par_):
                act.wait_ge(aT_psum, s + 1)
                act.wait_ge(down_done, s - 1)
                fn(aT[:, par_, :, 0:128], ps[:, 2 * par_, :].rearrange("p (f n) -> p f n", f=2)[:, :, 0:128],
                   ACT.Copy).then_inc(aT_ready, 1)

            def tokens_out(e):
                act.wait_ge(xg_psum, e + 1)
                fn(XG[:, 0:4, :].rearrange("p k n -> p (k n)"), ps[:, 6, :], ACT.Copy).then_inc(xg_ready, 1)

            def output_out(s):
                act.wait_ge(down_done, s)
                fn(YE.rearrange("p (n c) -> p n c", n=2), ps[:, 4:6, :], ACT.Copy).then_inc(ye_ready, 1)

            def expert(e, s, first=False, last=False):
                silu_e(s, 0)
                if not first:
                    act_out_e(s - 1, 1)
                silu_e(s + 1, 1)
                act_out_e(s, 0)
                if not first:
                    output_out(s)
                silu_e(s + 2, 0)
                act_out_e(s + 1, 1)
                silu_e(s + 3, 1)
                act_out_e(s + 2, 0)
                act.wait_ge(gt_psum, e + 1)
                fn(GT, ps[:, 1, 0:SEQ], ACT.Copy).then_inc(gt_ready, 1)
                with act.Fori(0, STEPS_E // 2 - 2) as i:
                    t = s + 2 * i + 4
                    silu_e(t, 0)
                    act_out_e(t - 1, 1)
                    silu_e(t + 1, 1)
                    act_out_e(t, 0)
                if not last:
                    tokens_out(e + 1)

            def feed_forward(s0, n):
                silu(s0, 0)
                silu(s0 + 1, 1)
                act_out(s0, 0)

                def pair(s):
                    silu(s, 0)
                    act_out(s - 1, 1)
                    silu(s + 1, 1)
                    act_out(s, 0)

                pair(s0 + 2)
                with act.Fori(2, n // 2) as i:
                    pair(s0 + 2 * i)
                if n % 2:
                    silu(s0 + n - 1, 0)
                    act_out(s0 + n - 2, 1)
                act_out(s0 + n - 1, (n - 1) % 2)

            def evac_proj(q, c, dst):
                act.wait_ge(proj_psum, 4 * q + c + 1)
                fn(dst, ps[:, 4 + 2 * (c % 2):6 + 2 * (c % 2), 0:dst.shape[2]], ACT.Copy).then_inc(proj_evac, 1)

            act.wait_ge(x_loaded, 16)
            rms(0)
            act.wait_ge(par_psum, 1)
            for g in range(2):
                fn(parc[:, 4 * g:4 * g + 4, :], ps[:, g, :].rearrange("p (k n) -> p k n", k=4)[:, :, 0:ROWS],
                   ACT.Copy).then_inc(parc_ready, 1)
            act.wait_ge(wst_psum, 1)
            raw = ps[:, 2:4, :].rearrange("p l (h i) -> p (l h) i", h=GM_HEADS)
            wsf = wst[:, :, :, :].rearrange("p l h i -> p (l h) i")
            fn(wsf[0:64, :, :], raw[0:64, :, :], ACT.Copy).then_inc(wst_ready, 1)
            fn(wsf[64:128, :, 64:128], raw[64:128, :, 64:128], ACT.Copy).then_inc(wst_ready, 1)
            act.wait_ge(parc_ready, 2)
            for l in range(DEPTH):
                if l:
                    act.wait_ge(x_ready, 2)
                    rms(2)
                features(2 * l, lambda k: parc[:, k, R_N1 + l:R_N1 + l + 1])

                def cols(c):
                    c0 = D_IN - C1 * (c + 1)
                    return Pm[:, :, c0:c0 + C1]

                evac_proj(l, 0, cols(0))
                evac_proj(l, 1, cols(1))
                act.wait_ge(proj_evac, 4 * l + 2)
                fn(GH, Pm[:, :, CG0:CG0 + D_CONV], ACT.Sigmoid).then_inc(sg_ready, 1)
                evac_proj(l, 2, cols(2))
                act.wait_ge(proj_evac, 4 * l + 3)
                for b in range(NB):
                    chain.then(fn(GV[:, b, :], Pm[:, b, V0:V0 + D_GM], ACT.Square, accum_out=gm_ss[:, b:b + 1]))
                chain.wait()
                fn(gm_std, gm_ss, ACT.Sqrt, scale=1.0 / D_GM, bias=eps1).then_inc(gm_std_ready, 1)
                act.wait_ge(gluT_psum, l + 1)
                fn(CT[:, 0:2, TAPS - 1:], ps[:, 0, :].rearrange("p (t n) -> p t n", t=2), ACT.Copy).then_inc(ct_ready, 1)
                fn(CT[:, 2, TAPS - 1:], ps[:, 1, 0:SEQ], ACT.Copy).then_inc(ct_ready, 1)
                act.wait_ge(gm_rstd_ready, l + 1)
                for b in range(NB):
                    fn(GV[:, b, :], Pm[:, b, V0:V0 + D_GM], ACT.Copy, scale=gm_rstd[:, b:b + 1]).then_inc(gn_ready, 1)
                evac_proj(l, 3, cols(3))
                act.wait_ge(pool1_psum, l + 1)
                for g in range(2):
                    for h in range(2):
                        r = slice(64 * h, 64 * h + 64)
                        fn(YT[r, g, :], ps[r, 2 + g, h * SEQ:(h + 1) * SEQ], ACT.Copy).then_inc(yt_ready, 1)
                if l == DEPTH - 1:
                    load(bandf[:, 0:3 * P128].rearrange("p (k n) -> p k n", k=3), T["c_moe"], moe_loaded)
                    load(gain2, rep(T["norm2_g"][l]), moe_loaded)
                act.wait_ge(z_psum, l + 1)
                for b in range(NB):
                    for h in range(GM_HEADS):
                        c = slice(h * GM_HD, (h + 1) * GM_HD)
                        r = R_GMB + l * GM_HEADS + h
                        fn(YB[:, b, c], ps[:, 4 + b, c], ACT.Identity, bias=parc[:, 0, r:r + 1]).then_inc(zb_ready, 1)
                act.wait_ge(pool2_psum, l + 1)
                for g in range(2):
                    fn(MT[:, g, :], ps[:, 2, g * SEQ:(g + 1) * SEQ], ACT.Copy,
                       scale=parc[:, g, R_PSC + l:R_PSC + l + 1]).then_inc(mt_ready, 1)
                act.wait_ge(ybT_psum, l + 1)
                fn(MT[:, 2:4, :], ps[:, 6, :].rearrange("p (t n) -> p t n", t=2), ACT.Copy).then_inc(mt_ready, 1)
                fn(MT[:, 4, :], ps[:, 7, 0:SEQ], ACT.Copy).then_inc(mt_ready, 1)
                act.wait_ge(cl_var, l + 1)
                fn(lstd, mv[:, :, 1], ACT.Sqrt, bias=eps1).then_inc(cl_std, 1)
                act.wait_ge(cnT_psum, l + 1)
                for t in range(3):
                    fn(HC[:, t, :], ps[:, 2 + t // 2, (t % 2) * SEQ:(t % 2 + 1) * SEQ], ACT.Silu,
                       scale=parc[:, t, R_LNG + l:R_LNG + l + 1], bias=parc[:, t, R_LNB + l:R_LNB + l + 1]).then_inc(hc_ready, 1)
                act.wait_ge(pw_psum, l + 1)
                for d in range(3):
                    fn(MT[:, 5 + d, :], ps[:, d // 2, (d % 2) * SEQ:(d % 2 + 1) * SEQ], ACT.Identity,
                       bias=parc[:, d, R_PWB + l:R_PWB + l + 1]).then_inc(mt_ready, 1)
                act.wait_ge(x_ready, 2 * l + 1)
                rms(2 * l + 1)
                features(2 * l + 1, lambda k: parc[:, k, R_N2 + l:R_N2 + l + 1])
                if l == 0:
                    feed_forward(0, STEPS)
                    act.wait_ge(args_ready, 1)
                    fn(trig, arg, ACT.Sin).then_inc(trig_ready, 1)
            act.wait_ge(gl_ready, 1)
            for b in range(NB):
                fn(gexp[:, b, :], logit[:, b, :], ACT.Exp, bias=gneg[:, b:b + 1]).then_inc(ge_ready, 1)
            tokens_out(0)
            expert(0, MOE_STEP0, first=True)
            with act.Fori(1, EXPERTS - 1) as e:
                expert(e, MOE_STEP0 + STEPS_E * e)
            expert(EXPERTS - 1, B2_STEP0 - STEPS_E, last=True)
            act_out_e(B2_STEP0 - 1, 1)
            output_out(B2_STEP0)

            def second_block(r, e):
                act.wait_ge(ov_xg_psum, 2 * r + 2)
                fn(XG.rearrange("p (c k) n -> p c (k n)", c=2), ps[:, 6:8, :], ACT.Copy).then_inc(ov_xg, 1)
                fn(GT, ps[:, 1, 0:SEQ], ACT.Copy).then_inc(ov_xg, 1)
                with act.Fori(0, STEPS_E) as i:
                    t = STEPS_E * r + i
                    act.wait_ge(ov_gu, t + 1)
                    fn(sil[:, 0, 0, :], ps[:, 0, 0:FN], ACT.Silu).then_inc(ov_silu, 1)
                    act.wait_ge(ov_aT_psum, t + 1)
                    fn(aT[:, 0, :, 0:128], ps[:, 2, 0:256].rearrange("p (f n) -> p f n", f=2), ACT.Copy).then_inc(ov_aT, 1)

            overflowing(act, second_block)
            act.wait_ge(moe_done, 1)
            rms(4)

            def ln_std_of(i):
                act.wait_ge(ln_var, i + 1)
                fn(lstd, mv[:, :, 1], ACT.Sqrt, bias=eps2).then_inc(ln_std, 1)

            ln_std_of(0)
            with act.Fori(0, DEPTH) as l:
                features(2 * l + 4, None)
                for c in range(4):
                    evac_proj(l + 2, c, P2[:, :, c * C2:(c + 1) * C2])
                act.wait_ge(ik_var, l + 1)
                fn(lstd, mv[:, :, 1], ACT.Sqrt, bias=eps2).then_inc(ik_std, 1)
                for i in range(0, 7, 2):
                    act.wait_ge(qkT_psum, 7 * l + i + 1)
                    fn(TT[:, 2 * i:2 * i + 2, :].rearrange("p t n -> p (t n)"), ps[:, i, :], ACT.Copy).then_inc(qkT_act, 1)
                for b in range(NB):
                    nk = 128 * (b + 1)
                    act.wait_ge(idx_psum, 2 * l + b + 1)
                    fn(RL[:, 0:8 * nk].rearrange("p (r n) -> p r n", r=4), ps[:, 0:4, 0:2 * nk], ACT.Relu).then_inc(relu_ready, 1)
                    for kind, S, scored, nm, den, done in ((0, Sswa, swa_scored, swa_nm, swa_den, swa_exp),
                                                           (1, Sdsa, dsa_scored, dsa_nm, dsa_den, dsa_exp)):
                        act.wait_ge(scored, 2 * l + b + 1)
                        if kind == 0:
                            fn(swa_es, swa_es, ACT.Exp)
                        for h in range(Q_HEADS):
                            fn(S[:, h * nk:(h + 1) * nk], S[:, h * nk:(h + 1) * nk], ACT.Exp, bias=nm[:, h:h + 1],
                               accum_out=den[:, h:h + 1]).then_inc(done, 1)
                        g0 = 12 * l + 4 * b + 2 * (b + 1) * kind
                        for g in range(2 * (b + 1)):
                            act.wait_ge(pt_psum, g0 + g + 1)
                            h0 = 4 * (g % 2)
                            fn(PT[:, g // 2, h0:h0 + 4, :].rearrange("p h q -> p (h q)"), ps[:, 4 + g % 2, :],
                               ACT.Copy).then_inc(pt_ready, 1)
                for i in range(2):
                    act.wait_ge(omT_psum, 4 * l + i + 1)
                    fn(MT2[:, 2 * i:2 * i + 2, :].rearrange("p t n -> p (t n)"), ps[:, i, :], ACT.Copy).then_inc(mt2_act, 1)
                act.wait_ge(pT_psum, l + 1)
                fn(PPT.rearrange("p k n -> p (k n)"), ps[:, 0, :], ACT.Copy).then_inc(pT_ready, 1)
                ln_std_of(2 * l + 1)
                features(2 * l + 5, None)
                act.wait_ge(pg_psum, 2 * l + 2)
                fn(SGP, psf[:, 2048:4096], ACT.Sigmoid).then_inc(sgp_ready, 1)
                feed_forward(B2_STEP0 + STEPS * l, STEPS)
                ln_std_of(2 * l + 2)

        @block.vector
        def _(dve):
            V = nc.vector
            chain = Chain(dve, dve_chain)
            link, then = chain.link, chain.then

            def pause():
                V.memset(spare, 0.0)

            MAGIC, TURN = 1.5 * 2.0 ** 23, 2.0 * np.pi
            T1_ = 6.28125
            T2_ = float(np.round((TURN - T1_) * 2.0 ** 21) / 2.0 ** 21)
            T3_ = float(TURN - T1_ - T2_)
            PI = 3.1415925
            dve.wait_ge(attn_loaded, 16 * 8)
            link(V.tensor_copy(posf, posi[:, :]))
            for b in range(NB):
                then(V.tensor_scalar(ang[:, b, :], freq[:, :], posf[:, b:b + 1], None, ALU.mult))
            chain.wait()
            for c in range(2):
                then(V.tensor_scalar(turn[:, c], ang, 1.0 / TURN, 0.25 * c, ALU.mult, ALU.add))
            chain.wait()
            link(V.tensor_scalar(turn, turn, MAGIC, MAGIC, ALU.add, ALU.subtract))
            for c in range(2):
                then(V.scalar_tensor_tensor(arg[:, c], turn[:, c], -T1_, ang, ALU.mult, ALU.add))
            chain.wait()
            for part in (T2_, T3_):
                link(V.scalar_tensor_tensor(arg, turn, -part, arg, ALU.mult, ALU.add))
            link(V.tensor_scalar(arg[:, 1], arg[:, 1], np.pi / 2, None, ALU.add))
            V.tensor_scalar(arg, arg, PI, -PI, ALU.min, ALU.max).then_inc(args_ready, 1)

            def normed(t):
                dve.wait_ge(std_ready, t + 1)
                link(V.reciprocal(rstd, std))
                for b in range(NB):
                    V.tensor_scalar(XN[:, b, :], X[:, b, :], rstd[:, b:b + 1], None, ALU.mult).then_inc(xn_ready, 1)

            def features(t, gain):
                for k in range(4, KT):
                    dve.wait_ge(hT_psum, 4 * t + k // 2 + 1)
                    src = ps[:, k // 2, (k % 2) * SEQ:(k % 2 + 1) * SEQ]
                    if gain is None:
                        ins = V.tensor_copy(hT[:, k, :], src)
                    else:
                        ins = V.tensor_scalar(hT[:, k, :], src, gain(k), None, ALU.mult)
                    ins.then_inc(hT_ready, 1)

            def act_mul(s, par_):
                dve.wait_ge(silu_ready, s + 1)
                wait(dve, aT_psum, s - 1)
                V.tensor_tensor(am[:, par_, :, :], sil[:, par_, :, :], ps[:, 2 * par_:2 * par_ + 2, FN:2 * FN],
                                ALU.mult).then_inc(act_ready, 1)

            def feed_forward(s0, n):
                act_mul(s0, 0)
                act_mul(s0 + 1, 1)
                with dve.Fori(1, n // 2) as i:
                    act_mul(s0 + 2 * i, 0)
                    act_mul(s0 + 2 * i + 1, 1)
                if n % 2:
                    act_mul(s0 + n - 1, 0)

            def add_down(done, gate=None):
                for b in range(NB):
                    src = psf[:, 2048 + 1024 * b:3072 + 1024 * b]
                    if gate is None:
                        ins = V.tensor_tensor(X[:, b, :], X[:, b, :], src, ALU.add)
                    else:
                        ins = V.scalar_tensor_tensor(X[:, b, :], src, gate(b), X[:, b, :], ALU.mult, ALU.add)
                    done(b, ins)

            for l in range(DEPTH):
                normed(2 * l)
                if l == 0:
                    dve.wait_ge(parc_ready, 2)
                features(2 * l, lambda k: parc[:, k, R_N1 + l:R_N1 + l + 1])
                dve.wait_ge(sg_ready, l + 1)
                V.tensor_tensor(GH, GH, Pm[:, :, CV0:CV0 + D_CONV], ALU.mult).then_inc(glu_ready, 1)
                dve.wait_ge(gm_std_ready, l + 1)
                V.reciprocal(gm_rstd, gm_std).then_inc(gm_rstd_ready, 1)
                dve.wait_ge(ct_ready, 2 * (l + 1))
                for t in range(3):
                    then(V.tensor_scalar(ACC[:, t, :], CT[:, t, 0:SEQ], parc[:, t, R_DW + TAPS * l:R_DW + TAPS * l + 1],
                                         parc[:, t, R_DWB + l:R_DWB + l + 1], ALU.mult, ALU.add))
                with dve.Fori(0, TAPS - 2) as i:
                    chain.enter(i, 3)
                    for t in range(3):
                        chain.wait(back=2)
                        then(V.scalar_tensor_tensor(ACC[:, t, :], CT[:, t, bass.ds(i + 1, SEQ)],
                                                    parc[:, t, bass.ds(i + R_DW + TAPS * l + 1, 1)], ACC[:, t, :],
                                                    ALU.mult, ALU.add))
                chain.leave(3, TAPS - 2)
                for t in range(3):
                    chain.wait(back=2 - t)
                    V.scalar_tensor_tensor(ACC[:, t, :], CT[:, t, TAPS - 1:TAPS - 1 + SEQ],
                                           parc[:, t, R_DW + TAPS * l + TAPS - 1:R_DW + TAPS * l + TAPS], ACC[:, t, :],
                                           ALU.mult, ALU.add).then_inc(conv_ready, 1)
                dve.wait_ge(cl_psum, l + 1)
                for b in range(NB):
                    then(V.bn_stats(bst[:, b, 0, :], ps[:, b, 0:D_CONV]))
                chain.wait()
                for b in range(NB):
                    ins = V.bn_aggr(mv[:, b, :], bst[:, b, 0, :])
                ins.then_inc(cl_var, 1)
                dve.wait_ge(cl_std, l + 1)
                link(V.reciprocal(lrstd, lstd))
                for b in range(NB):
                    ins = V.tensor_scalar(CN[:, b, :], ps[:, b, 0:D_CONV], mv[:, b, 0:1], lrstd[:, b:b + 1],
                                          ALU.subtract, ALU.mult)
                ins.then_inc(cn_ready, 1)
                for n in range(2):
                    dve.wait_ge(mix_psum, 2 * l + n + 1)
                    for b in range(NB):
                        x = X[:, b, 512 * n:512 * n + 512]
                        ins = V.tensor_tensor(x, x, ps[:, 4 + 2 * b + n, :], ALU.add)
                ins.then_inc(x_ready, 1)
                dve.wait_ge(x_ready, 2 * l + 1)
                normed(2 * l + 1)
                features(2 * l + 1, lambda k: parc[:, k, R_N2 + l:R_N2 + l + 1])
                if l == 0:
                    feed_forward(0, STEPS)
                    dve.wait_ge(down_done, STEPS)
                    add_down(lambda b, ins: ins.then_inc(x_ready, 1) if b else None)
                    dve.wait_ge(trig_ready, 1)
                    for tc, tsn, h, f in ((cosA, sinA, HD // 2, slice(0, 32)), (cosI, sinI, IDX_DIM // 2, slice(32, 48))):
                        for half in range(2):
                            V.tensor_copy(tc[:, :, half * h:(half + 1) * h], trig[:, 1, :, f]).then_inc(rope_tables, 1)
                            V.tensor_scalar(tsn[:, :, half * h:(half + 1) * h], trig[:, 0, :, f], 2.0 * half - 1.0, None,
                                            ALU.mult).then_inc(rope_tables, 1)
                    dve.wait_ge(x_ready, 2)
            dve.wait_ge(router_psum, 1)
            link(V.tensor_copy(logit, ps[:, 4, 0:NB * EXPERTS].rearrange("p (b e) -> p b e", b=NB)))
            then(V.tensor_reduce(gmax, logit, AX.X, ALU.max))
            for b in range(NB):
                other = logit[:, b, :].unsqueeze(1).broadcast_to([128, EXPERTS, EXPERTS])
                own = logit[:, b, :].unsqueeze(2).broadcast_to([128, EXPERTS, EXPERTS])
                beats = score[:, 64 * b:64 * b + 64].rearrange("p (e f) -> p e f", e=EXPERTS)
                ties = work[:, 64 * b:64 * b + 64].rearrange("p (e f) -> p e f", e=EXPERTS)
                then(V.tensor_tensor(beats, other, own, ALU.is_gt))
                link(V.tensor_tensor(ties, other, own, ALU.is_equal))
                link(V.tensor_tensor(ties, ties, lower[:, :, :], ALU.mult))
                link(V.tensor_tensor(beats, beats, ties, ALU.add))
                link(V.tensor_reduce(rank[:, b, :], beats, AX.X, ALU.add))
            V.tensor_scalar(gneg, gmax, -1.0, None, ALU.mult).then_inc(gl_ready, 1)
            V.tensor_scalar(rank, rank, float(TOP_E), None, ALU.is_lt).then_inc(sel_ready, 1)
            dve.wait_ge(sel_ready, 1)
            dve.wait_ge(ge_ready, NB)
            link(V.tensor_tensor(gexp, gexp, rank, ALU.mult))
            link(V.tensor_reduce(gden, gexp, AX.X, ALU.add))
            link(V.reciprocal(grec, gden))
            for b in range(NB):
                then(V.tensor_scalar(gates[:, b, :], gexp[:, b, :], grec[:, b:b + 1], None, ALU.mult))
            dve.wait_ge(pos_psum, 1)
            link(V.scalar_tensor_tensor(pos, ps[:, 5, 0:NB * EXPERTS], 1.0, rank.rearrange("p b e -> p (b e)"), ALU.add, ALU.mult))
            link(V.tensor_scalar(pos, pos, -1.0, None, ALU.add))
            every = [128, NB * EXPERTS, P128]
            V.tensor_tensor(PL.rearrange("p b e n -> p (b e) n"), iota.unsqueeze(1).broadcast_to(every),
                            pos.unsqueeze(2).broadcast_to(every), ALU.is_equal).then_inc(pl_ready, 1)
            link(V.tensor_scalar(over_flag, ps[:, 5, NB * EXPERTS:(NB + 1) * EXPERTS], float(P128), None, ALU.is_gt))
            over_pairs = score[:, 0:64].rearrange("p (e f) -> p e f", e=EXPERTS)
            then(V.tensor_reduce(over_list[:, 0:1], over_flag, AX.X, ALU.add))
            link(V.tensor_tensor(over_pairs, lower[:, :, :], over_flag.unsqueeze(1).broadcast_to([128, EXPERTS, EXPERTS]), ALU.mult))
            link(V.tensor_reduce(over_rank, over_pairs, AX.X, ALU.add))
            some = [128, MAX_OVER, EXPERTS]
            link(V.tensor_tensor(over_pick, over_rank.unsqueeze(1).broadcast_to(some),
                                 iota[:, 0:MAX_OVER].unsqueeze(2).broadcast_to(some), ALU.is_equal))
            link(V.tensor_tensor(over_pick, over_pick, over_flag.unsqueeze(1).broadcast_to(some), ALU.mult))
            link(V.tensor_tensor(over_pick, over_pick, iota[:, 0:EXPERTS].unsqueeze(1).broadcast_to(some), ALU.mult))
            link(V.tensor_reduce(over_list[:, 1:], over_pick, AX.X, ALU.add))
            V.tensor_copy(over_int[:, :], over_list).then_inc(over_ready, 1)

            def tokens_out(e):
                dve.wait_ge(xg_psum, e + 1)
                V.tensor_copy(XG[:, 4:8, :].rearrange("p k n -> p (k n)"), ps[:, 7, :]).then_inc(xg_ready, 1)

            def act_mul_e(s, par_):
                dve.wait_ge(silu_ready, s + 1)
                dve.wait_ge(aT_psum, s - 1)
                V.tensor_tensor(am[:, par_, 0, :], sil[:, par_, 0, :], ps[:, 2 * par_, FN:2 * FN], ALU.mult).then_inc(act_ready, 1)

            def add_scattered():
                for b, n, bank in ((0, 0, 1), (0, 1, 3), (1, 0, 6), (1, 1, 7)):
                    x = X[:, b, n * 512:(n + 1) * 512]
                    ins = V.tensor_tensor(x, x, ps[:, bank, :], ALU.add)
                return ins

            def expert(e, s, first=False, last=False):
                for j in range(3):
                    act_mul_e(s + j, j % 2)
                if not first:
                    dve.wait_ge(scat_psum, e)
                    add_scattered().then_inc(ffn_evac, 1)
                    dve.wait_ge(gt_psum, e)
                for b in range(NB):
                    ins = V.tensor_scalar(PG[:, b, :], PL[:, b, bass.ds(e, 1), :].rearrange("p o n -> p (o n)"),
                                          gates[:, b, bass.ds(e, 1)], None, ALU.mult)
                ins.then_inc(pg_ready, 1)
                act_mul_e(s + 3, 1)
                if not first:
                    dve.wait_ge(ffn_evac, e)
                    pause()
                with dve.Fori(0, STEPS_E // 2 - 2) as i:
                    act_mul_e(s + 2 * i + 4, 0)
                    act_mul_e(s + 2 * i + 5, 1)
                if not last:
                    tokens_out(e + 1)

            tokens_out(0)
            chain.wait()
            dve.wait_ge(pl_ready, 1)
            expert(0, MOE_STEP0, first=True)
            with dve.Fori(1, EXPERTS - 1) as e:
                expert(e, MOE_STEP0 + STEPS_E * e)
            expert(EXPERTS - 1, B2_STEP0 - STEPS_E, last=True)
            dve.wait_ge(scat_psum, EXPERTS)
            add_scattered().then_inc(ffn_evac, 1)
            dve.wait_ge(ffn_evac, EXPERTS)
            V.memset(spare3, 0.0).then_inc(ov_free, 1)

            def second_block(r, e):
                PER = 4
                ov = Chain(dve, ov_chain)
                ov.enter(r, PER)
                for b in range(NB):
                    ov.then(V.tensor_scalar(OP[:, b, :], iota, float(P128), pos[:, bass.ds(e + b * EXPERTS, 1)],
                                            ALU.add, ALU.is_equal))
                ov.wait()
                for b in range(NB):
                    ins = V.tensor_scalar(OG[:, b, :], OP[:, b, :], gates[:, b, bass.ds(e, 1)], None, ALU.mult)
                ins.then_inc(ov_places, 1)
                ov.link(V.memset(YE, 0.0))
                pause()
                with dve.Fori(0, STEPS_E) as i:
                    t = STEPS_E * r + i
                    dve.wait_ge(ov_silu, t + 1)
                    V.tensor_tensor(am[:, 0, 0, :], sil[:, 0, 0, :], ps[:, 0, FN:2 * FN], ALU.mult).then_inc(ov_act, 1)
                    dve.wait_ge(ov_free, t + 2)
                    y = YE.rearrange("p (n c) -> p n c", n=2)
                    V.tensor_tensor(y, y, ps[:, 4:6, :], ALU.add).then_inc(ov_sum, 1)
                    dve.wait_ge(ov_sum, t + 1)
                    pause()
                dve.wait_ge(ov_scat, r + 1)
                ov.link(add_scattered())
                pause()

            overflowing(dve, second_block)
            V.memset(spare2, 0.0).then_inc(moe_done, 1)

            def layer_norm(i, g, b_):
                for b in range(NB):
                    for c in range(2):
                        then(V.bn_stats(bst[:, b, c, :], X[:, b, 512 * c:512 * c + 512]))
                chain.wait()
                pause()
                for b in range(NB):
                    ins = V.bn_aggr(mv[:, b, :], bst[:, b, :, :].rearrange("p c s -> p (c s)"))
                ins.then_inc(ln_var, 1)
                dve.wait_ge(ln_std, i + 1)
                link(V.reciprocal(lrstd, lstd))
                for b in range(NB):
                    then(V.scalar_tensor_tensor(X[:, b, :], X[:, b, :], mv[:, b, 0:1], g, ALU.subtract, ALU.mult))
                chain.wait()
                for b in range(NB):
                    ins = V.scalar_tensor_tensor(X[:, b, :], X[:, b, :], lrstd[:, b:b + 1], b_, ALU.mult, ALU.add)
                ins.then_inc(xln_ready, 1)

            dve.wait_ge(std_ready, 5)
            dve.wait_ge(ln_loaded, 16 * 7)
            link(V.reciprocal(rstd, std))
            for b in range(NB):
                then(V.scalar_tensor_tensor(X[:, b, :], X[:, b, :], rstd[:, b:b + 1], lni[:, 0, :], ALU.mult, ALU.mult))
            chain.wait()
            layer_norm(0, lni[:, 1, :], lni[:, 2, :])

            PER_LAYER = 106
            with dve.Fori(0, DEPTH) as l:
                chain.enter(l, PER_LAYER)
                features(2 * l + 4, None)
                dve.wait_ge(proj_evac, 4 * l + 12)

                def halves(c0, n, d):
                    return P2[:, :, c0:c0 + n * d].rearrange("p b (h c d) -> p b h c d", c=2, d=d // 2)

                def over(table, half, n, d):
                    return table[:, :, half * d // 2:(half + 1) * d // 2].unsqueeze(2).broadcast_to([128, NB, n, d // 2])

                for b in range(NB):
                    then(V.bn_stats(bst[:, b, 0, :], P2[:, b, KI:KI + IDX_DIM]))
                chain.wait()
                pause()
                for b in range(NB):
                    ins = V.bn_aggr(mv[:, b, :], bst[:, b, 0, :])
                ins.then_inc(ik_var, 1)
                for c0, h0, n in ((QA, 0, 10), (QB, 10, 9)):
                    for half in range(2):
                        then(V.tensor_tensor(T2[:, :, h0:h0 + n, half, :], halves(c0, n, HD)[:, :, :, 1 - half, :],
                                             over(sinA, half, n, HD), ALU.mult))
                for half in range(2):
                    then(V.tensor_tensor(T2I[:, :, :, half, :], halves(QI, 8, IDX_DIM)[:, :, :, 1 - half, :],
                                         over(sinI, half, 8, IDX_DIM), ALU.mult))
                then(V.tensor_scalar(wi, P2[:, :, WI:WI + IDX_HEADS], IDX_HEADS ** -0.5 * IDX_DIM ** -0.5, None, ALU.mult))
                dve.wait_ge(ik_std, l + 1)
                link(V.reciprocal(lrstd, lstd))
                for b in range(NB):
                    then(V.tensor_scalar(KN[:, b, :], P2[:, b, KI:KI + IDX_DIM], mv[:, b, 0:1], lrstd[:, b:b + 1],
                                         ALU.subtract, ALU.mult))
                chain.wait()

                def both(row):
                    return row.broadcast_to([128, NB, IDX_DIM])

                link(V.tensor_tensor(KN, KN, both(ikg[:, bass.ds(l, 1), :]), ALU.mult))
                link(V.tensor_tensor(KN, KN, both(ikb[:, bass.ds(l, 1), :]), ALU.add))
                for half in range(2):
                    h = IDX_DIM // 2
                    then(V.tensor_tensor(T2K[:, :, half, :], KN[:, :, (1 - half) * h:(2 - half) * h],
                                         sinI[:, :, half * h:(half + 1) * h], ALU.mult))
                chain.wait()
                link(V.tensor_tensor(KN, KN, cosI[:, :, :], ALU.mult))
                four = [128, NB, 4, IDX_DIM]
                V.tensor_tensor(RKI, KN.unsqueeze(2).broadcast_to(four),
                                T2K.rearrange("p b c d -> p b (c d)").unsqueeze(2).broadcast_to(four), ALU.add)
                dve.wait_ge(cos_part, 6 * l + 6)
                whole = T2.rearrange("p b h c d -> p b h (c d)")
                V.tensor_tensor(RQI, RQI, T2I.rearrange("p b h c d -> p b h (c d)"), ALU.add)
                for k, h in ((0, 8), (1, 9), (2, 18)):
                    V.tensor_tensor(RK[:, :, k, :, :], RK[:, :, k, :, :],
                                    whole[:, :, h:h + 1, :].broadcast_to([128, NB, 2, HD]), ALU.add)
                V.tensor_tensor(RQ[:, :, 0:8, :], RQ[:, :, 0:8, :], whole[:, :, 0:8, :], ALU.add)
                V.tensor_tensor(RQ[:, :, 8:16, :], RQ[:, :, 8:16, :], whole[:, :, 10:18, :], ALU.add).then_inc(rope_ready, 1)
                for i in range(1, 7, 2):
                    dve.wait_ge(qkT_psum, 7 * l + i + 1)
                    V.tensor_copy(TT[:, 2 * i:2 * i + 2, :].rearrange("p t n -> p (t n)"), ps[:, i, :]).then_inc(qkT_dve, 1)
                for b in range(NB):
                    nk = 128 * (b + 1)
                    causal = masks[:, 1, 256 - nk:256]

                    def per_head(ap):
                        return ap.rearrange("p (h k) -> p h k", h=Q_HEADS)

                    def bias(m):
                        return m.unsqueeze(1).broadcast_to([128, Q_HEADS, nk])

                    dve.wait_ge(swa_psum, 2 * l + b + 1)
                    S = per_head(Sswa[:, 0:8 * nk])
                    link(V.scalar_tensor_tensor(S, per_head(psf[:, 2048:2048 + 8 * nk]), HD ** -0.5,
                                                bias(masks[:, 0, 256 - nk:256]), ALU.mult, ALU.add))
                    link(V.tensor_reduce(swa_m, S, AX.X, ALU.max))
                    snk = sink[:, bass.ds(l, 1), :].rearrange("p o (a t) -> p (o t) a", t=2)

                    def by_place(ap):
                        return ap.rearrange("p (t a) -> p t a", t=2)

                    link(V.tensor_tensor(by_place(swa_m), by_place(swa_m), snk, ALU.max))
                    V.tensor_scalar(swa_nm, swa_m, -1.0, None, ALU.mult)
                    V.tensor_tensor(by_place(swa_es), snk, by_place(swa_m), ALU.subtract).then_inc(swa_scored, 1)
                    dve.wait_ge(relu_ready, 2 * l + b + 1)
                    sc = score[:, 0:nk]
                    for h in range(IDX_HEADS):
                        p = 2 * (h % 4) + h // 4
                        link(V.scalar_tensor_tensor(sc, RL[:, p * nk:(p + 1) * nk], wi[:, b, h:h + 1], sc if h else causal,
                                                    ALU.mult, ALU.add))
                    pause()
                    with dve.Fori(0, TOPK // 8) as r:
                        chain.enter(r, 2)
                        link(V.max(top8, sc))
                        pause()
                        link(V.match_replace(sc, top8, sc, TAKEN))
                    chain.leave(2, TOPK // 8)
                    db = dbias[:, 0:nk]
                    link(V.tensor_scalar(db, sc, TAKEN, NEG, ALU.not_equal, ALU.mult))
                    link(V.tensor_tensor(db, db, causal, ALU.min))
                    dve.wait_ge(dsa_psum, 2 * l + b + 1)
                    S = per_head(Sdsa[:, 0:8 * nk])
                    link(V.scalar_tensor_tensor(S, per_head(psf[:, 0:8 * nk]), HD ** -0.5, bias(db), ALU.mult, ALU.add))
                    link(V.tensor_reduce(dsa_m, S, AX.X, ALU.max))
                    V.tensor_scalar(dsa_nm, dsa_m, -1.0, None, ALU.mult).then_inc(dsa_scored, 1)
                    for kind, expd, den, rd in ((0, swa_exp, swa_den, swa_rd), (1, dsa_exp, dsa_den, dsa_rd)):
                        dve.wait_ge(expd, 8 * (2 * l + b + 1))
                        if kind == 0:
                            link(V.tensor_tensor(den, den, swa_es, ALU.add))
                        link(V.reciprocal(rd, den))
                        dve.wait_ge(pv_psum, 4 * l + 2 * b + kind + 1)
                        V.tensor_tensor(OM[:, b, 512 * kind:512 * kind + 512].rearrange("p (a t d) -> p t a d", t=2, d=HD),
                                        ps[:, 6 + kind, :].rearrange("p (t a d) -> p t a d", t=2, d=HD),
                                        by_place(rd).unsqueeze(3).broadcast_to([128, 2, Q_HEADS // 2, HD]),
                                        ALU.mult).then_inc(om_ready, 1)
                for i in range(2, 4):
                    dve.wait_ge(omT_psum, 4 * l + i + 1)
                    V.tensor_copy(MT2[:, 2 * i:2 * i + 2, :].rearrange("p t n -> p (t n)"), ps[:, i, :]).then_inc(mt2_dve, 1)
                for n in range(2):
                    dve.wait_ge(mix_psum, 2 * l + n + 5)
                    for b in range(NB):
                        x = X[:, b, 512 * n:512 * n + 512]
                        then(V.scalar_tensor_tensor(x, x, ALPHA, ps[:, 4 + 2 * b + n, :], ALU.mult, ALU.add))
                chain.wait()

                def lnrow(k):
                    return lnp[:, bass.ds(l, 1), k, :].rearrange("p o d -> p (o d)")

                layer_norm(2 * l + 1, lnrow(0), lnrow(1))
                features(2 * l + 5, None)
                xf = X[:, :, :].rearrange("p b n -> p (b n)")
                dve.wait_ge(sgp_ready, l + 1)
                dve.wait_ge(pp_psum, l + 1)
                V.tensor_tensor(PLEO, SGP, psf[:, 0:2048], ALU.mult).then_inc(ple_read, 1)
                dve.wait_ge(ple_read, l + 1)
                link(V.scalar_tensor_tensor(xf, xf, ALPHA, PLEO, ALU.mult, ALU.add))
                pause()
                feed_forward(B2_STEP0 + STEPS * l, STEPS)
                dve.wait_ge(down_done, B2_STEP0 + STEPS * l + STEPS)
                add_down(lambda b, ins: then(ins))
                chain.wait()
                layer_norm(2 * l + 2, lnrow(2), lnrow(3))
            chain.leave(PER_LAYER, DEPTH)


OUT_SHAPE = (1, SEQ, D)


def kernel(**inputs):
    import concourse.bacc as bacc
    from concourse.bass_utils import run_bass_kernel_spmd

    nc = bacc.Bacc("TRN2", target_bir_lowering=False, num_devices=1, dynamic_dma_scratch_size=1024)
    arrays = {n: np.ascontiguousarray(a) for n, a in inputs.items()}
    arrays.update(shape_constants())
    T = {n: nc.dram_tensor(f"in_{n}", a.shape, mybir.dt.from_np(a.dtype), kind="ExternalInput").ap()
         for n, a in arrays.items()}
    T["out"] = nc.dram_tensor("out", OUT_SHAPE, mybir.dt.float32, kind="ExternalOutput").ap()
    build_program(nc, {n: t[0] if n.startswith("moe_") and n != "moe_router" else t for n, t in T.items()})
    run = run_bass_kernel_spmd(nc, [{f"in_{n}": a for n, a in arrays.items()}], core_ids=[0])
    return run.results[0]["out"]
```

```python
from contextlib import ExitStack

import numpy as np

import concourse.bass as bass
from concourse import mybir


P128 = 128
SEQ, D = 256, 1024
NB = SEQ // P128
KT = D // P128
DEPTH = 2
D_POOL, D_GM, D_CONV = 256, 384, 384
WINDOWS = (2, 4, 8, 16)
GROUP = D_POOL // len(WINDOWS)
GM_HEADS = 4
GM_HD = D_GM // GM_HEADS
CHUNK = 64
TAPS = 31
D_IN = D_POOL + 2 * D_GM + 2 * D_CONV
U0, V0 = D_POOL, D_POOL + D_GM
CV0, CG0 = V0 + D_GM, V0 + D_GM + D_CONV
D_FF, D_FF_E, EXPERTS = 2816, 3584, 8
EPS, LN_EPS = 1e-6, 1e-5
HD, Q_HEADS = 64, 8
IDX_HEADS, IDX_DIM = 8, 32
PLE = 256
TOPK = 64
ALPHA = (2 * DEPTH) ** 0.25
NEG, TAKEN = -1e30, -3e38
QA, KA, VA = 0, 512, 640
QB, KB, VB = 768, 1280, 1344
QI, KI, WI = 1408, 1664, 1696
IN2 = 1704
C1, C2 = D_IN // 4, IN2 // 4
FN = 256
STEPS, STEPS_E = D_FF // FN, D_FF_E // FN
MOE_STEP0 = STEPS
B2_STEP0 = MOE_STEP0 + EXPERTS * STEPS_E
TOP_E = 2
MAX_OVER = (TOP_E * SEQ) // (P128 + 1)
R_N1, R_N2, R_DWB, R_LNG, R_LNB, R_PWB, R_PSC, R_DW = 0, 2, 4, 6, 8, 10, 12, 14
R_GMB = R_DW + DEPTH * TAPS
ROWS = R_GMB + DEPTH * GM_HEADS


def shape_constants():
    f32 = np.float32
    s = np.arange(SEQ)
    band = np.zeros((SEQ, len(WINDOWS), SEQ), f32)
    for g, w in enumerate(WINDOWS):
        inside = (s[:, None] <= s[None, :]) & (s[None, :] - s[:, None] < w)
        band[:, g] = inside / np.minimum(s + 1, w)[None, :].astype(f32) - np.eye(SEQ)
    i = np.arange(P128)
    causal = np.where(i[None, :] <= i[:, None], 0.0, NEG)
    older = np.where(i[None, :] > i[:, None], 0.0, NEG)
    masks = np.stack([np.concatenate([older, causal], 1),
                      np.concatenate([np.zeros_like(causal), causal], 1)], 1).astype(f32)
    freq = np.concatenate([
        f32(10000.0) ** (-np.arange(h, dtype=f32) / f32(h)) for h in (HD // 2, IDX_DIM // 2)]).astype(f32)
    e = np.arange(EXPERTS)
    lower = (e[None, :] < e[:, None]).astype(f32).reshape(1, -1)
    moe = np.stack([i[:, None] < i[None, :], np.ones((P128, P128)), np.broadcast_to(i[None, :], (P128, P128))], 1).astype(f32)
    return {"c_ident": np.eye(P128, dtype=f32), "c_band": band, "c_masks": masks,
            "c_freq": freq.reshape(1, -1), "c_lower": lower, "c_moe": moe}


def build_program(nc, T):
    f32, f32r = mybir.dt.float32, mybir.dt.float32r
    ALU = mybir.AluOpType
    ACT = mybir.ActivationFunctionType
    AX = mybir.AxisListType

    ctx = ExitStack()
    with ctx:
        def sb(name, shape, dt=f32):
            return ctx.enter_context(nc.sbuf_tensor(name, shape, dt))

        def sem(name):
            return ctx.enter_context(nc.semaphore(name))

        def sb_rounded(name, shape):
            start = -(-nc.sbuf_base // 32) * 32
            wide = sb(name, shape)
            return wide, nc.alloc_sbuf_tensor_at(name + "_rounded", shape, f32r, offset=start)

        ident = sb("ident", [128, 128])
        band = sb("band", [128, NB, 4, SEQ])
        masks = sb("masks", [128, 2, 256])
        freq = sb("freq", [128, 48])
        lower = sb("lower", [128, EXPERTS, EXPERTS])
        parc = sb("parc", [128, KT, ROWS])
        router = sb("router", [128, KT, EXPERTS])
        poolw = sb("poolw", [128, DEPTH, 2, 128])
        wst = sb("wst", [128, DEPTH, GM_HEADS, 128])
        gmg = sb("gmg", [128, DEPTH, D_GM])
        sink = sb("sink", [128, DEPTH, Q_HEADS])
        ikg = sb("ikg", [128, DEPTH, IDX_DIM])
        ikb = sb("ikb", [128, DEPTH, IDX_DIM])
        pin = sb("pin", [128, NB, PLE])
        lnp = sb("lnp", [128, DEPTH, 4, D])
        lni = sb("lni", [128, 3, D])
        X = sb("X", [128, NB, D])
        hT, hTr = sb_rounded("hT", [128, KT, SEQ])
        XN, XNr = sb_rounded("XN", [128, NB, D])
        ringA = sb("ringA", [128, 2, 4096])
        ringD = sb("ringD", [128, 2, 2048])
        sil = sb("sil", [128, 2, NB, FN])
        am = sb("am", [128, 2, NB, FN])
        aT = sb("aT", [128, 2, 2, SEQ], f32r)
        gates = sb("gates", [128, NB, EXPERTS])
        cosA = sb("cosA", [128, NB, HD])
        sinA = sb("sinA", [128, NB, HD])
        cosI = sb("cosI", [128, NB, IDX_DIM])
        sinI = sb("sinI", [128, NB, IDX_DIM])
        small = sb("small", [128, 512])
        over_int = sb("over_int", [128, 1 + MAX_OVER], mybir.dt.int32)
        posi = sb("posi", [128, NB], mybir.dt.int32)
        SCR, SCRr = sb_rounded("SCR", [128, 16600])
        ps = ctx.enter_context(nc.psum_tensor("ps", [128, 8, 512], f32))
        psf = ps[:, :, :].rearrange("p b n -> p (b n)")

        taken = [0]

        def col(n):
            taken[0] += n
            assert taken[0] <= 512
            return small[:, taken[0] - n:taken[0]]

        eps1, eps2, spare, spare2, spare3 = (col(1) for _ in range(5))
        ss, std, rstd = col(2), col(2), col(2)
        gm_ss, gm_std, gm_rstd = col(2), col(2), col(2)
        bst = col(2 * 2 * 6).rearrange("p (b c s) -> p b c s", b=2, c=2)
        mv = col(4).rearrange("p (b s) -> p b s", b=2)
        lstd, lrstd = col(2), col(2)
        posf = col(2)
        logit = col(16).rearrange("p (b e) -> p b e", b=2)
        gmax, gneg, gden, grec = col(2), col(2), col(2), col(2)
        gexp = col(16).rearrange("p (b e) -> p b e", b=2)
        rank = col(16).rearrange("p (b e) -> p b e", b=2)
        swa_m, swa_nm, swa_es, swa_den, swa_rd = (col(8) for _ in range(5))
        dsa_m, dsa_nm, dsa_den, dsa_rd = (col(8) for _ in range(4))
        top8 = col(8)
        wi = col(16).rearrange("p (b e) -> p b e", b=2)
        pos = col(16)
        over_flag, over_rank = col(EXPERTS), col(EXPERTS)
        over_pick = col(MAX_OVER * EXPERTS).rearrange("p (r e) -> p r e", r=MAX_OVER)
        over_list = col(1 + MAX_OVER)

        at = [0]

        def scr(n):
            at[0] += n
            assert at[0] <= 16600
            return SCR[:, at[0] - n:at[0]]

        def scr_r(n):
            at[0] += n
            return SCRr[:, at[0] - n:at[0]]

        Pm = scr(2 * D_IN).rearrange("p (b n) -> p b n", b=2)
        GH = scr(2 * D_CONV).rearrange("p (b n) -> p b n", b=2)
        CT = scr(3 * (SEQ + TAPS - 1)).rearrange("p (t n) -> p t n", t=3)
        ACC = scr(3 * SEQ).rearrange("p (t n) -> p t n", t=3)
        CN = scr(2 * D_CONV).rearrange("p (b n) -> p b n", b=2)
        HC = scr(3 * SEQ).rearrange("p (t n) -> p t n", t=3)
        GV = scr(2 * D_GM).rearrange("p (b n) -> p b n", b=2)
        YB = scr(2 * D_GM).rearrange("p (b n) -> p b n", b=2)
        YT = scr(2 * SEQ).rearrange("p (t n) -> p t n", t=2)
        MT = scr(KT * SEQ).rearrange("p (t n) -> p t n", t=KT)
        at[0] = 12000
        par = scr(D)
        wsr = scr(DEPTH * GM_HEADS * 128).rearrange("p (l h n) -> p l h n", l=DEPTH, h=GM_HEADS)
        at[0] = 15360
        ang = scr(2 * 48).rearrange("p (b n) -> p b n", b=2)
        turn = scr(2 * 2 * 48).rearrange("p (c b n) -> p c b n", c=2, b=2)
        arg = scr(2 * 2 * 48).rearrange("p (c b n) -> p c b n", c=2, b=2)
        trig = scr(2 * 2 * 48).rearrange("p (c b n) -> p c b n", c=2, b=2)
        at[0] = 0
        UH, UL = [None, None], [None, None]
        for h in range(2):
            UH[h], UL[h] = scr_r(2048), scr_r(2048)
        DH, DL = scr_r(2048), scr_r(2048)
        XGH, XGL = (scr_r(KT * P128).rearrange("p (k n) -> p k n", k=KT) for _ in range(2))
        aTl = scr_r(2 * 2 * SEQ).rearrange("p (c f n) -> p c f n", c=2, f=2)
        xh = XNr[:, :, :].rearrange("p b n -> p (b n)").rearrange("p (k n) -> p k n", k=KT)
        xl = hTr[:, :, :]
        at[0] = 0
        OA, OD = scr(4096), scr(2048)
        OP = scr(NB * P128).rearrange("p (b n) -> p b n", b=NB)
        OG = scr(NB * P128).rearrange("p (b n) -> p b n", b=NB)
        OX = scr(KT * P128).rearrange("p (k n) -> p k n", k=KT)
        OT = scr(2 * P128).rearrange("p (f n) -> p f n", f=2)
        PL = hT[:, :, :].rearrange("p k n -> p (k n)").rearrange("p (b e n) -> p b e n", b=NB, e=EXPERTS)
        bandf = band[:, :, :, :].rearrange("p b w t -> p (b w t)")
        tri, ones, iota = (bandf[:, P128 * k:P128 * (k + 1)] for k in range(3))
        gain2 = bandf[:, 1024:2048]
        PG = bandf[:, 384:640].rearrange("p (b n) -> p b n", b=NB)
        GT = bandf[:, 640:896]
        YE = gain2
        at[0] = 0
        P2 = scr(2 * IN2).rearrange("p (b n) -> p b n", b=2)
        region = at[0]
        RQ = scr(2 * 16 * HD).rearrange("p (b h d) -> p b h d", b=2, h=16)
        RK = scr(2 * 6 * HD).rearrange("p (b k u d) -> p b k u d", b=2, k=3, u=2)
        RQI = scr(2 * 256).rearrange("p (b h d) -> p b h d", b=2, h=8)
        RKI = scr(2 * 128).rearrange("p (b u d) -> p b u d", b=2, u=4)
        at[0] = region
        Sswa = scr(2048)
        Sdsa = scr(2048)
        TT = scr(14 * SEQ).rearrange("p (t n) -> p t n", t=14)
        pt_om = at[0]
        PT = scr(2048).rearrange("p (k h q) -> p k h q", k=2, h=8)
        OM = scr(2048).rearrange("p (b n) -> p b n", b=2)
        at[0] = pt_om
        T2 = scr(2 * 19 * HD).rearrange("p (b h c d) -> p b h c d", b=2, h=19, c=2)
        T2I = scr(2 * 8 * 32).rearrange("p (b h c d) -> p b h c d", b=2, h=8, c=2)
        T2K = scr(2 * 32).rearrange("p (b c d) -> p b c d", b=2, c=2)
        KN = scr(2 * 32).rearrange("p (b d) -> p b d", b=2)
        at[0] = pt_om + 4096
        score = scr(256)
        work = scr(256)
        dbias = scr(256)
        PPT = scr(2 * SEQ).rearrange("p (k n) -> p k n", k=2)
        MT2 = PT.rearrange("p k h q -> p (k h q)").rearrange("p (t n) -> p t n", t=KT)
        at[0] = 12288
        SGP, PLEO = scr(2048), scr(2048)
        RL = XN[:, :, :].rearrange("p b n -> p (b n)")

        ident_loaded, x_loaded, par_loaded, mixer_loaded, attn_loaded, ln_loaded, pin_loaded = (
            sem(n) for n in ("ident_loaded", "x_loaded", "par_loaded", "mixer_loaded", "attn_loaded", "ln_loaded",
                             "pin_loaded"))
        zeroed = sem("zeroed")
        A_loaded = [sem("A_loaded0"), sem("A_loaded1")]
        D_loaded = [sem("D_loaded0"), sem("D_loaded1")]
        stored = sem("stored")
        act_chain, dve_chain = sem("act_chain"), sem("dve_chain")
        par_psum, parc_ready, wst_psum, wst_ready = sem("par_psum"), sem("parc_ready"), sem("wst_psum"), sem("wst_ready")
        args_ready, trig_ready, rope_tables = sem("args_ready"), sem("trig_ready"), sem("rope_tables")
        std_ready, xn_ready, hT_psum, hT_ready = sem("std_ready"), sem("xn_ready"), sem("hT_psum"), sem("hT_ready")
        proj_psum, proj_evac = sem("proj_psum"), sem("proj_evac")
        sg_ready, glu_ready, gluT_psum, ct_ready = sem("sg_ready"), sem("glu_ready"), sem("gluT_psum"), sem("ct_ready")
        gm_std_ready, gm_rstd_ready, gn_ready, gv_ready = sem("gm_std_ready"), sem("gm_rstd_ready"), sem("gn_ready"), sem("gv_ready")
        pool1_psum, yt_ready, pool2_psum, mt_ready = sem("pool1_psum"), sem("yt_ready"), sem("pool2_psum"), sem("mt_ready")
        z_psum, zb_ready, yb_ready, ybT_psum = sem("z_psum"), sem("zb_ready"), sem("yb_ready"), sem("ybT_psum")
        conv_ready, cl_psum, cl_var, cl_std, cn_ready, cnT_psum, hc_ready, pw_psum = (
            sem(n) for n in ("conv_ready", "cl_psum", "cl_var", "cl_std", "cn_ready", "cnT_psum", "hc_ready", "pw_psum"))
        mix_psum, x_ready = sem("mix_psum"), sem("x_ready")
        router_psum = sem("router_psum")
        gl_ready, ge_ready = sem("gl_ready"), sem("ge_ready")
        moe_loaded, xn_gained, sel_ready, pos_psum, pl_ready, over_ready = (
            sem(n) for n in ("moe_loaded", "xn_gained", "sel_ready", "pos_psum", "pl_ready", "over_ready"))
        xg_psum, xg_ready, pg_ready, gt_psum, gt_ready, ye_ready, scat_psum, moe_done = (
            sem(n) for n in ("xg_psum", "xg_ready", "pg_ready", "gt_psum", "gt_ready", "ye_ready", "scat_psum", "moe_done"))
        ov_free, ov_loaded, ov_places, ov_xg_psum, ov_xg, ov_gu, ov_silu, ov_act, ov_aT_psum, ov_aT, ov_sum, ov_scat, ov_chain = (
            sem(n) for n in ("ov_free", "ov_loaded", "ov_places", "ov_xg_psum", "ov_xg", "ov_gu", "ov_silu", "ov_act",
                             "ov_aT_psum", "ov_aT", "ov_sum", "ov_scat", "ov_chain"))
        gu_psum, silu_ready, act_ready, aT_psum, aT_ready, down_done, ffn_evac = (
            sem(n) for n in ("gu_psum", "silu_ready", "act_ready", "aT_psum", "aT_ready", "down_done", "ffn_evac"))
        u_hi, u_ready = [sem("u_hi0"), sem("u_hi1")], [sem("u_ready0"), sem("u_ready1")]
        u0_used, d_hi, d_ready, aT_hi, xs_hi, xs_ready, xg_hi = (
            sem(n) for n in ("u0_used", "d_hi", "d_ready", "aT_hi", "xs_hi", "xs_ready", "xg_hi"))
        ln_var, ln_std, xln_ready = sem("ln_var"), sem("ln_std"), sem("xln_ready")
        ik_var, ik_std, cos_part, rope_ready = sem("ik_var"), sem("ik_std"), sem("cos_part"), sem("rope_ready")
        qkT_psum, qkT_act, qkT_dve = sem("qkT_psum"), sem("qkT_act"), sem("qkT_dve")
        idx_psum, relu_ready, swa_psum, dsa_psum = sem("idx_psum"), sem("relu_ready"), sem("swa_psum"), sem("dsa_psum")
        swa_scored, dsa_scored = sem("swa_scored"), sem("dsa_scored")
        swa_exp, dsa_exp, pt_psum, pt_ready = sem("swa_exp"), sem("dsa_exp"), sem("pt_psum"), sem("pt_ready")
        pv_psum, om_ready, omT_psum, mt2_act, mt2_dve = (
            sem(n) for n in ("pv_psum", "om_ready", "omT_psum", "mt2_act", "mt2_dve"))
        pT_psum, pT_ready, pg_psum, pp_psum, pp_ready, sgp_ready = (
            sem(n) for n in ("pT_psum", "pT_ready", "pg_psum", "pp_psum", "pp_ready", "sgp_ready"))

        class Chain:

            def __init__(self, eng, s):
                self.eng, self.s, self.base, self.n, self.outer = eng, s, 0, 0, []

            def then(self, ins):
                self.n += 1
                ins.then_inc(self.s, 1)

            def wait(self, back=0):
                self.eng.wait_ge(self.s, self.base + self.n - back)

            def link(self, ins):
                self.then(ins)
                self.wait()

            def enter(self, turn, per):
                self.outer.append((self.base, self.n))
                self.base, self.n = (self.base + self.n) + turn * per, 0

            def leave(self, per, turns):
                assert self.n == per, (self.n, per)
                self.base, self.n = self.outer.pop()
                self.n += per * turns

        def place(h):
            return (h % 2) * 4 + h // 2

        def wait(eng, s, value):
            if not isinstance(value, int) or value > 0:
                eng.wait_ge(s, value)

        def overflowing(eng, body):
            eng.wait_ge(over_ready, 1)
            n = eng.value_load(over_int[0:1, 0:1], min_val=0, max_val=MAX_OVER)
            with eng.Fori(0, MAX_OVER) as r:
                with eng.If(r < n):
                    body(r, eng.value_load(over_int[0:1, bass.ds(r + 1, 1)], min_val=0, max_val=EXPERTS - 1))

        block = ctx.enter_context(nc.Block())

        @block.sync
        def _(sp):
            def cut(w, e, r0, rows, c0, n):
                return w[bass.ds(e, 1), bass.ds(r0, rows), bass.ds(c0, n)].rearrange("o (k p) n -> p (o k) n", p=128)

            def columns(slot, w, e, c0, n):
                dst = ringA[:, slot, 0:KT * n].rearrange("p (k n) -> p k n", k=KT)
                sp.dma_start(dst, cut(w, e, 0, D, c0, n)).then_inc(A_loaded[slot], 32)

            def gate_up(slot, wg, wu, e, cg, cu):
                dst = ringA[:, slot, :].rearrange("p (k u n) -> p k u n", k=KT, u=2)
                sp.dma_start(dst[:, :, 0, :], cut(wg, e, 0, D, cg, FN)).then_inc(A_loaded[slot], 16)
                sp.dma_start(dst[:, :, 1, :], cut(wu, e, 0, D, cu, FN)).then_inc(A_loaded[slot], 16)

            def rows(slot, w, e, r0):
                dst = ringD[:, slot, :].rearrange("p (k n) -> p k n", k=2)
                sp.dma_start(dst, cut(w, e, r0, FN, 0, D)).then_inc(D_loaded[slot], 16)

            def step_weights(wg, wu, wd, e, up0, s0, y, j):
                sp.wait_ge(u_ready[1], s0 + y - 1)
                gate_up(j, wg, wu, e, y * FN, y * FN + up0)
                down_rows(wd, e, s0, y - 2, (j + 1) % 2)

            def down_rows(wd, e, s0, y, slot):
                wait(sp, d_ready, s0 + y - 1)
                rows(slot, wd, e, y * FN)

            def feed_forward(wg, wu, wd, e, up0, s0, n):
                gate_up(1, wg, wu, e, FN, up0 + FN)
                step_weights(wg, wu, wd, e, up0, s0, 2, 0)
                step_weights(wg, wu, wd, e, up0, s0, 3, 1)
                with sp.Fori(2, n // 2) as i:
                    for j in range(2):
                        step_weights(wg, wu, wd, e, up0, s0, 2 * i + j, j)
                if n % 2:
                    step_weights(wg, wu, wd, e, up0, s0, n - 1, 0)
                down_rows(wd, e, s0, n - 2, (n - 1) % 2)
                down_rows(wd, e, s0, n - 1, n % 2)

            def load(dst, src, s):
                sp.dma_start(dst, src).then_inc(s, 16)

            load(X[:, :, :], T["x"].rearrange("o (b p) d -> p (o b) d", p=128), x_loaded)
            sp.wait_ge(zeroed, 6)
            for r, n in ((R_N1, "norm1_g"), (R_N2, "norm2_g"), (R_DWB, "conv_dw_b"), (R_LNG, "conv_ln_g"),
                         (R_LNB, "conv_ln_b"), (R_PWB, "conv_pw_b"), (R_PSC, "pool_scale")):
                load(par[r:r + DEPTH, 0:T[n].shape[1]], T[n], par_loaded)
            load(par[R_DW:R_DW + DEPTH * TAPS, 0:D_CONV], T["conv_dw_w"].rearrange("l t c -> (l t) c"), par_loaded)
            load(par[R_GMB:ROWS, 0:128], T["gm_b"].rearrange("l h i -> (l h) i"), par_loaded)
            for l in range(DEPTH):
                for c in range(4):
                    if c >= 2:
                        sp.wait_ge(proj_psum, 4 * l + c - 1)
                    elif l:
                        sp.wait_ge(u_ready[1], STEPS)
                    columns(c % 2, T["w_in"], l, D_IN - C1 * (c + 1), C1)
                if l:
                    sp.wait_ge(d_ready, STEPS)
                sp.dma_start(ringD[:, 0, 0:3 * D_CONV].rearrange("p (k n) -> p k n", k=3),
                             cut(T["conv_pw_w"], l, 0, D_CONV, 0, D_CONV)).then_inc(D_loaded[0], 16)
                for n in range(2):
                    sp.wait_ge(proj_psum, 4 * l + n + 3)
                    columns(n, T["w_out"], l, 512 * n, 512)
                if l == 0:
                    sp.wait_ge(mix_psum, 1)
                    gate_up(0, T["ffn_wg"], T["ffn_wu"], 0, 0, 0)
                    sp.wait_ge(mix_psum, 2)
                    feed_forward(T["ffn_wg"], T["ffn_wu"], T["ffn_wd"], 0, 0, 0, STEPS)
            EG, EU, ED = T["moe_wg"], T["moe_wu"], T["moe_wd"]
            sp.wait_ge(mix_psum, 3)
            gate_up(0, EG, EU, 0, 0, 0)
            sp.wait_ge(mix_psum, 4)
            gate_up(1, EG, EU, 0, FN, FN)

            def further_steps(e, s0):
                with sp.Fori(0, STEPS_E // 2 - 1) as i:
                    for j in range(2):
                        step_weights(EG, EU, ED, e, 0, s0, 2 * i + 2 + j, j)

            further_steps(0, MOE_STEP0)
            with sp.Fori(1, EXPERTS) as e:
                s0 = MOE_STEP0 + STEPS_E * e
                for j in range(2):
                    sp.wait_ge(u_ready[1], s0 + j - 1)
                    gate_up(j, EG, EU, e, j * FN, j * FN)
                    down_rows(ED, e - 1, s0 - STEPS_E, STEPS_E - 2 + j, (j + 1) % 2)
                further_steps(e, s0)
            for j in range(2):
                down_rows(ED, EXPERTS - 1, B2_STEP0 - STEPS_E, STEPS_E - 2 + j, (j + 1) % 2)

            def second_block(r, e):
                with sp.Fori(0, STEPS_E) as i:
                    sp.wait_ge(ov_free, STEPS_E * r + i + 1)
                    dst = OA.rearrange("p (k u n) -> p k u n", k=KT, u=2)
                    sp.dma_start(dst[:, :, 0, :], cut(EG, e, 0, D, i * FN, FN)).then_inc(ov_loaded, 16)
                    sp.dma_start(dst[:, :, 1, :], cut(EU, e, 0, D, i * FN, FN)).then_inc(ov_loaded, 16)
                    sp.dma_start(OD.rearrange("p (k n) -> p k n", k=2), cut(ED, e, i * FN, FN, 0, D)).then_inc(ov_loaded, 16)

            overflowing(sp, second_block)
            with sp.Fori(0, DEPTH) as l:
                q = l + 2
                s0 = B2_STEP0 + STEPS * l
                sp.wait_ge(u_ready[1], s0)
                for c in range(4):
                    if c >= 2:
                        sp.wait_ge(proj_psum, 4 * q + c - 1)
                    if c == 3:
                        sp.dma_start(pin[:, :, :], T["p_2"][bass.ds(l, 1), 0, :, :].rearrange("o (b p) n -> p (o b) n", p=128)
                                     ).then_inc(pin_loaded, 16)
                    columns(c % 2, T["w_in_2"], l, IN2 - C2 * (c + 1), C2)
                sp.wait_ge(d_ready, s0)
                rows(0, T["w_pp_2"], l, 0)
                for n in range(2):
                    sp.wait_ge(proj_psum, 4 * q + n + 3)
                    columns(n, T["w_o_2"], l, 512 * n, 512)
                for n in range(2):
                    sp.wait_ge(mix_psum, 2 * q + n + 1)
                    columns(n, T["w_pg_2"], l, 512 * n, 512)
                sp.wait_ge(pg_psum, 2 * l + 1)
                gate_up(0, T["w_gu_2"], T["w_gu_2"], l, 0, D_FF)
                sp.wait_ge(sgp_ready, l + 1)
                feed_forward(T["w_gu_2"], T["w_gu_2"], T["w_down_2"], l, D_FF, s0, STEPS)
            sp.wait_ge(xln_ready, 1 + 2 * DEPTH)
            sp.dma_start(T["out"].rearrange("o (b p) d -> p (o b) d", p=128), X[:, :, :]).then_inc(stored, 16)
            sp.wait_ge(stored, 16)

        @block.tensor
        def _(pe):
            mm = nc.tensor.matmul

            def tr(out, in_, n=128):
                return nc.tensor.transpose(out, in_, ident[0:n, 0:n])

            def slotA(slot, n):
                return ringA[:, slot, 0:KT * n].rearrange("p (k n) -> p k n", k=KT)

            def to_features(t, src):
                for k in range(KT):
                    for b in range(NB):
                        c = (k % 2) * SEQ + b * 128
                        m = tr(ps[:, k // 2, c:c + 128], src[:, b, k * 128:(k + 1) * 128])
                    if k % 2:
                        m.then_inc(hT_psum, 1)
                pe.wait_ge(hT_ready, 8 * (t + 1))

            def project(q, c, n, use):
                pe.wait_ge(A_loaded[c % 2], 32 * use)
                if c >= 2:
                    pe.wait_ge(proj_evac, 4 * q + c - 1)
                w = slotA(c % 2, n)
                for k in range(KT):
                    for b in range(NB):
                        m = mm(ps[:, 4 + 2 * (c % 2) + b, 0:n], hT[:, k, b * 128:(b + 1) * 128], w[:, k, :],
                               start=(k == 0), stop=(k == KT - 1))
                m.then_inc(proj_psum, 1)

            def full_depth(lhs, slot, use, bank_of, done, k0=0, k1=KT):
                pe.wait_ge(A_loaded[slot], 32 * use)
                w = slotA(slot, 512)
                for k in range(k0, k1):
                    for b in range(NB):
                        m = mm(ps[:, bank_of(b), :], lhs[:, k, b * 128:(b + 1) * 128], w[:, k, :],
                               start=(k == 0), stop=(k == KT - 1))
                if k1 == KT:
                    m.then_inc(done, 1)

            def parts(out, wide, x, w, start, stop):
                (x0, x1), (w0, w1) = x, w
                mm(out, x0, w0[:, wide], start=start, stop=False)
                mm(out, x0, w1[:, wide], start=False, stop=False)
                return mm(out, x1, w0[:, wide], start=False, stop=stop)

            def up(s, par_, reused=True, x=(xh, xl), blocks=NB):
                if reused:
                    pe.wait_ge(aT_ready, s - 1)
                for h in range(2):
                    pe.wait_ge(u_ready[h], s + 1)
                    for k in range(4):
                        for b in range(blocks):
                            lhs = [part[:, 4 * h + k, b * 128:(b + 1) * 128] for part in x]
                            m = parts(ps[:, 2 * par_ + b, :], slice(512 * k, 512 * k + 512), lhs,
                                      (UH[h], UL[h]), 4 * h + k == 0, 4 * h + k == KT - 1)
                    m.then_inc((u0_used, gu_psum)[h], 1)

            def turn_act(s, par_, blocks=NB):
                pe.wait_ge(act_ready, s + 1)
                for f in range(2):
                    for b in range(blocks):
                        c = f * SEQ + b * 128
                        m = tr(ps[:, 2 * par_, c:c + 128], am[:, par_, b, f * 128:(f + 1) * 128])
                m.then_inc(aT_psum, 1)

            def down(s, par_, first=False, last=False, blocks=NB, unit=(DH, DL)):
                pe.wait_ge(aT_ready, s + 1)
                pe.wait_ge(d_ready, s + 1)
                for f in range(2):
                    for n in range(2):
                        for b in range(blocks):
                            lhs = [part[:, par_, f, b * 128:(b + 1) * 128] for part in (aT, aTl)]
                            m = parts(ps[:, 4 + 2 * b + n, :], slice(1024 * f + 512 * n, 1024 * f + 512 * n + 512), lhs,
                                      unit, first and f == 0, last and f == 1)
                m.then_inc(down_done, 1)

            pe.wait_ge(ident_loaded, 16)
            pe.wait_ge(par_loaded, 16 * 9)
            for k in range(KT):
                m = tr(ps[:, k // 4, (k % 4) * 128:(k % 4) * 128 + ROWS], par[0:ROWS, k * 128:(k + 1) * 128], ROWS)
            m.then_inc(par_psum, 1)
            pe.wait_ge(parc_ready, 2)

            def pipeline(s0, turn):
                n = STEPS
                pe.wait_ge(xs_ready, 2 * turn + 2)
                up(s0, 0, False)
                up(s0 + 1, 1, False)
                turn_act(s0, 0)
                up(s0 + 2, 0)
                turn_act(s0 + 1, 1)
                wait(pe, sgp_ready, turn)
                down(s0, 0, first=True)
                with pe.Fori(0, (n - 3) // 2) as i:
                    s = s0 + 2 * i + 3
                    up(s, 1)
                    turn_act(s - 1, 0)
                    down(s - 2, 1)
                    up(s + 1, 0)
                    turn_act(s, 1)
                    down(s - 1, 0)
                s = s0 + n
                turn_act(s - 1, 0)
                down(s - 2, 1, unit=(UH[0], UL[0]))
                down(s - 1, 0, last=True, unit=(UH[1], UL[1]))

            a_base = [(0, 0), (9, 8)]
            for l in range(DEPTH):
                pe.wait_ge(xn_ready, 2 * (2 * l + 1))
                to_features(2 * l, XN)
                a0, a1 = a_base[l]
                for c in range(3):
                    project(l, c, C1, (a0, a1)[c % 2] + c // 2 + 1)
                    if l + c == 0:
                        pe.wait_ge(mixer_loaded, 16 * 5)
                        for d in range(DEPTH):
                            for h in range(GM_HEADS):
                                m = tr(ps[:, 2 + d, h * 128:(h + 1) * 128], wsr[:, d, h, :])
                        m.then_inc(wst_psum, 1)
                pe.wait_ge(glu_ready, l + 1)
                for t in range(3):
                    for b in range(NB):
                        c = (t % 2) * SEQ + b * 128
                        m = tr(ps[:, t // 2, c:c + 128], GH[:, b, t * 128:(t + 1) * 128])
                m.then_inc(gluT_psum, 1)
                project(l, 3, C1, a1 + 2)
                pe.wait_ge(proj_evac, 4 * l + 4)
                pe.wait_ge(wst_ready, 2)
                for g in range(2):
                    for b in range(NB):
                        m = mm(ps[:, 2 + g, :], Pm[:, b, g * 128:(g + 1) * 128],
                               band[:, b, 2 * g:2 * g + 2, :], start=(b == 0), stop=(b == NB - 1))
                m.then_inc(pool1_psum, 1)
                pe.wait_ge(gv_ready, l + 1)
                for b in range(NB):
                    for h in range(GM_HEADS):
                        m = mm(ps[:, 4 + b, h * GM_HD:(h + 1) * GM_HD], wst[:, l, h, :],
                               GV[:, b, h * GM_HD:(h + 1) * GM_HD], start=True, stop=True)
                m.then_inc(z_psum, 1)
                pe.wait_ge(yt_ready, 4 * (l + 1))
                for g in range(2):
                    m = mm(ps[:, 2, g * SEQ:(g + 1) * SEQ], poolw[:, l, g, :], YT[:, g, :], start=True, stop=True)
                m.then_inc(pool2_psum, 1)
                pe.wait_ge(yb_ready, l + 1)
                for t in range(3):
                    for b in range(NB):
                        c = (t % 2) * SEQ + b * 128
                        m = tr(ps[:, 6 + t // 2, c:c + 128], YB[:, b, t * 128:(t + 1) * 128])
                m.then_inc(ybT_psum, 1)
                pe.wait_ge(mt_ready, 7 * l + 4)
                for n in range(2):
                    full_depth(MT, n, (a0, a1)[n] + 3, lambda b: 4 + 2 * b + n, mix_psum, k1=5)
                pe.wait_ge(conv_ready, 3 * (l + 1))
                for b in range(NB):
                    for t in range(3):
                        m = tr(ps[:, b, t * 128:(t + 1) * 128], ACC[:, t, b * 128:(b + 1) * 128])
                m.then_inc(cl_psum, 1)
                pe.wait_ge(cn_ready, l + 1)
                for t in range(3):
                    for b in range(NB):
                        c = (t % 2) * SEQ + b * 128
                        m = tr(ps[:, 2 + t // 2, c:c + 128], CN[:, b, t * 128:(t + 1) * 128])
                m.then_inc(cnT_psum, 1)
                pe.wait_ge(hc_ready, 3 * (l + 1))
                pe.wait_ge(D_loaded[0], 16 * (6 * l + 1))
                pw = ringD[:, 0, 0:3 * D_CONV].rearrange("p (k n) -> p k n", k=3)
                for d in range(3):
                    for k in range(3):
                        m = mm(ps[:, d // 2, (d % 2) * SEQ:(d % 2 + 1) * SEQ], pw[:, k, d * 128:(d + 1) * 128],
                               HC[:, k, :], start=(k == 0), stop=(k == 2))
                m.then_inc(pw_psum, 1)
                pe.wait_ge(mt_ready, 7 * (l + 1))
                for n in range(2):
                    full_depth(MT, n, (a0, a1)[n] + 3, lambda b: 4 + 2 * b + n, mix_psum, k0=5)
                pe.wait_ge(xn_ready, 2 * (2 * l + 2))
                to_features(2 * l + 1, XN)
                if l == 0:
                    pipeline(0, 0)
            pe.wait_ge(attn_loaded, 16 * 8)
            for b in range(NB):
                for k in range(KT):
                    m = mm(ps[:, 4, b * EXPERTS:(b + 1) * EXPERTS], hT[:, k, b * 128:(b + 1) * 128], router[:, k, :],
                           start=(k == 0), stop=(k == KT - 1))
            m.then_inc(router_psum, 1)
            pe.wait_ge(sel_ready, 1)
            pe.wait_ge(moe_loaded, 16 * 2)
            for b in range(NB):
                for c in range(b + 1):
                    mm(ps[:, 5, b * EXPERTS:(b + 1) * EXPERTS], tri if c == b else ones, rank[:, c, :],
                       start=(c == 0), stop=(c == b))
            for c in range(NB):
                m = mm(ps[:, 5, NB * EXPERTS:(NB + 1) * EXPERTS], ones, rank[:, c, :], start=(c == 0), stop=(c == NB - 1))
            m.then_inc(pos_psum, 1)

            def gather(places, done):
                for k in range(KT):
                    for b in range(NB):
                        m = mm(ps[:, 6 + k // 4, (k % 4) * 128:(k % 4 + 1) * 128], XN[:, b, k * 128:(k + 1) * 128], places(b),
                               start=(b == 0), stop=(b == NB - 1))
                m.then_inc(done, 1)

            def places_of(e):
                return lambda b: PL[:, b, bass.ds(e, 1), :].rearrange("p o n -> p (o n)")

            def turn_gates(src, done):
                for b in range(NB):
                    m = tr(ps[:, 1, b * 128:(b + 1) * 128], src[:, b, :])
                m.then_inc(done, 1)

            def scatter(done):
                for b in range(NB):
                    for n in range(2):
                        m = mm(ps[:, (1 + 2 * n, 6 + n)[b], :], GT[:, b * 128:(b + 1) * 128], YE[:, n * 512:(n + 1) * 512],
                               start=True, stop=True)
                m.then_inc(done, 1)

            def up_e(s, par_, reused=True):
                up(s, par_, reused, (XGH, XGL), 1)

            def expert(e, s, first=False, last=False):
                pe.wait_ge(xg_ready, 2 * e + 2)
                up_e(s, 0, not first)
                if not first:
                    turn_act(s - 1, 1, 1)
                    down(s - 2, 0, blocks=1)
                up_e(s + 1, 1, not first)
                turn_act(s, 0, 1)
                if not first:
                    down(s - 1, 1, last=True, blocks=1)
                up_e(s + 2, 0)
                turn_act(s + 1, 1, 1)
                if not first:
                    pe.wait_ge(gt_ready, e)
                    pe.wait_ge(ye_ready, e)
                    scatter(scat_psum)
                down(s, 0, first=True, blocks=1)
                up_e(s + 3, 1)
                turn_act(s + 2, 0, 1)
                down(s + 1, 1, blocks=1)
                pe.wait_ge(pg_ready, e + 1)
                if not first:
                    pe.wait_ge(ffn_evac, e)
                turn_gates(PG, gt_psum)
                if not last:
                    gather(places_of(e + 1), xg_psum)
                with pe.Fori(0, STEPS_E // 2 - 2) as i:
                    t = s + 2 * i + 4
                    up_e(t, 0)
                    turn_act(t - 1, 1, 1)
                    down(t - 2, 0, blocks=1)
                    up_e(t + 1, 1)
                    turn_act(t, 0, 1)
                    down(t - 1, 1, blocks=1)

            pe.wait_ge(xn_gained, 1)
            pe.wait_ge(pl_ready, 1)
            gather(places_of(0), xg_psum)
            expert(0, MOE_STEP0, first=True)
            with pe.Fori(1, EXPERTS - 1) as e:
                expert(e, MOE_STEP0 + STEPS_E * e)
            expert(EXPERTS - 1, B2_STEP0 - STEPS_E, last=True)
            s = B2_STEP0
            turn_act(s - 1, 1, 1)
            down(s - 2, 0, blocks=1, unit=(UH[0], UL[0]))
            down(s - 1, 1, last=True, blocks=1, unit=(UH[1], UL[1]))
            pe.wait_ge(gt_ready, EXPERTS)
            pe.wait_ge(ye_ready, EXPERTS)
            scatter(scat_psum)

            def second_block(r, e):
                pe.wait_ge(ov_places, r + 1)
                gather(lambda b: OP[:, b, :], ov_xg_psum)
                turn_gates(OG, ov_xg_psum)
                wa = OA.rearrange("p (k n) -> p k n", k=KT)
                wd = OD.rearrange("p (k n) -> p k n", k=2)
                with pe.Fori(0, STEPS_E) as i:
                    t = STEPS_E * r + i
                    pe.wait_ge(ov_xg, 2 * r + 2)
                    pe.wait_ge(ov_loaded, 48 * t + 48)
                    for k in range(KT):
                        m = mm(ps[:, 0, :], OX[:, k, :], wa[:, k, :], start=(k == 0), stop=(k == KT - 1))
                    m.then_inc(ov_gu, 1)
                    pe.wait_ge(ov_act, t + 1)
                    for f in range(2):
                        m = tr(ps[:, 2, f * 128:(f + 1) * 128], am[:, 0, 0, f * 128:(f + 1) * 128])
                    m.then_inc(ov_aT_psum, 1)
                    pe.wait_ge(ov_aT, t + 1)
                    for n in range(2):
                        for f in range(2):
                            m = mm(ps[:, 4 + n, :], OT[:, f, :], wd[:, f, n * 512:(n + 1) * 512],
                                   start=(f == 0), stop=(f == 1))
                    m.then_inc(ov_free, 1)
                pe.wait_ge(ov_sum, STEPS_E * r + STEPS_E)
                scatter(ov_scat)

            overflowing(pe, second_block)

            with pe.Fori(0, DEPTH) as l:
                q = l + 2
                a0, a1, d0 = 68 + 10 * l, 67 + 9 * l, 63 + 6 * l
                pe.wait_ge(xln_ready, 2 * l + 1)
                to_features(2 * l + 4, X)
                for c in range(4):
                    project(q, c, C2, (a0, a1)[c % 2] + c // 2 + 1)
                pe.wait_ge(rope_ready, l + 1)
                flat = [RQI[:, :, 0:4, :], RQI[:, :, 4:8, :], RKI[:, :, :, :],
                        RK[:, :, 2, :, :], RK[:, :, 0, :, :], RK[:, :, 1, :, :]]
                flat += [RQ[:, :, 2 * t:2 * t + 2, :] for t in range(8)]
                for t in range(14):
                    for b in range(NB):
                        c = (t % 2) * SEQ + b * 128
                        m = tr(ps[:, t // 2, c:c + 128], flat[t][:, b].rearrange("p u d -> p (u d)"))
                    if t % 2:
                        m.then_inc(qkT_psum, 1)
                pe.wait_ge(qkT_act, 4 * (l + 1))
                pe.wait_ge(qkT_dve, 3 * (l + 1))
                for b in range(NB):
                    nk = 128 * (b + 1)
                    tok = slice(b * 128, (b + 1) * 128)
                    if b:
                        pe.wait_ge(dsa_scored, 2 * l + b)
                    for h in range(IDX_HEADS):
                        r = slice(32 * (h % 4), 32 * (h % 4) + 32)
                        m = mm(ps[:, h % 4, h // 4 * nk:(h // 4 + 1) * nk], TT[r, h // 4, tok], TT[r, 2, 0:nk],
                               start=True, stop=True)
                    m.then_inc(idx_psum, 1)
                    if b:
                        pe.wait_ge(om_ready, 4 * l + 2)
                    for h in range(Q_HEADS):
                        r = slice(64 * (h % 2), 64 * (h % 2) + 64)
                        c = 2048 + place(h) * nk
                        m = mm(psf[:, c:c + nk], TT[r, 6 + h // 2, tok], TT[r, 4 + h // 4, 0:nk], start=True, stop=True)
                    m.then_inc(swa_psum, 1)
                    pe.wait_ge(relu_ready, 2 * l + b + 1)
                    for h in range(Q_HEADS):
                        r = slice(64 * (h % 2), 64 * (h % 2) + 64)
                        c = place(h) * nk
                        m = mm(psf[:, c:c + nk], TT[r, 10 + h // 2, tok], TT[r, 3, 0:nk], start=True, stop=True)
                    m.then_inc(dsa_psum, 1)
                    for kind, S, expd, vcol in ((0, Sswa, swa_exp, lambda h: VA + HD * (h // 4)),
                                                (1, Sdsa, dsa_exp, lambda h: VB)):
                        pe.wait_ge(expd, 8 * (2 * l + b + 1))
                        g0 = 12 * l + 4 * b + 2 * (b + 1) * kind
                        for g in range(2 * (b + 1)):
                            if kind or g >= 2 or b:
                                pe.wait_ge(pt_ready, g0 + g - 1)
                            kt, h0 = g // 2, 4 * (g % 2)
                            for h in range(h0, h0 + 4):
                                m = tr(ps[:, 4 + g % 2, (h - h0) * 128:(h - h0 + 1) * 128],
                                       S[:, h * nk + kt * 128:h * nk + (kt + 1) * 128])
                            m.then_inc(pt_psum, 1)
                        pe.wait_ge(pt_ready, g0 + 2 * (b + 1))
                        for h in range(Q_HEADS):
                            p = place(h)
                            for kt in range(b + 1):
                                m = mm(ps[:, 6 + kind, p * HD:(p + 1) * HD], PT[:, kt, p, :],
                                       P2[:, kt, vcol(h):vcol(h) + HD], start=(kt == 0), stop=(kt == b))
                        m.then_inc(pv_psum, 1)
                pe.wait_ge(om_ready, 4 * (l + 1))
                for t in range(KT):
                    for b in range(NB):
                        c = (t % 2) * SEQ + b * 128
                        m = tr(ps[:, t // 2, c:c + 128], OM[:, b, t * 128:(t + 1) * 128])
                    if t % 2:
                        m.then_inc(omT_psum, 1)
                pe.wait_ge(mt2_act, 2 * (l + 1))
                pe.wait_ge(mt2_dve, 2 * (l + 1))
                for n in range(2):
                    full_depth(MT2, n, (a0, a1)[n] + 3, lambda b: 4 + 2 * b + n, mix_psum)
                pe.wait_ge(pin_loaded, 16 * (l + 1))
                for k in range(2):
                    for b in range(NB):
                        c = k * SEQ + b * 128
                        m = tr(ps[:, 0, c:c + 128], pin[:, b, k * 128:(k + 1) * 128])
                m.then_inc(pT_psum, 1)
                pe.wait_ge(pT_ready, l + 1)
                pe.wait_ge(D_loaded[0], 16 * (d0 + 1))
                w = ringD[:, 0, :].rearrange("p (k n) -> p k n", k=2)
                for k in range(2):
                    for n in range(2):
                        for b in range(NB):
                            m = mm(ps[:, 2 * b + n, :], PPT[:, k, b * 128:(b + 1) * 128], w[:, k, n * 512:(n + 1) * 512],
                                   start=(k == 0), stop=(k == 1))
                m.then_inc(pp_psum, 1)
                pe.wait_ge(pp_ready, l + 1)
                pe.wait_ge(xln_ready, 2 * l + 2)
                to_features(2 * l + 5, X)
                for n in range(2):
                    full_depth(hT, n, (a0, a1)[n] + 4, lambda b: 4 + 2 * b + n, pg_psum)
                pipeline(B2_STEP0 + STEPS * l, l + 1)

        @block.gpsimd
        def _(pool):
            TTn = nc.gpsimd.tensor_tensor
            nc.gpsimd.memset(par, 0.0).then_inc(zeroed, 1)
            nc.gpsimd.memset(poolw[:, :, :, :], 0.0).then_inc(zeroed, 1)
            nc.gpsimd.memset(CT[:, :, 0:TAPS - 1], 0.0).then_inc(zeroed, 1)
            nc.gpsimd.memset(wst[:, :, :, 0:64], 0.0).then_inc(zeroed, 1)
            nc.gpsimd.memset(eps1, EPS).then_inc(zeroed, 1)
            nc.gpsimd.memset(eps2, LN_EPS).then_inc(zeroed, 1)
            pool.wait_ge(mixer_loaded, 16 * 5)
            for l in range(DEPTH):
                if l:
                    pool.wait_ge(x_ready, 2 * l)
                    nc.gpsimd.memset(CT[:, :, 0:TAPS - 1], 0.0).then_inc(zeroed, 1)
                pool.wait_ge(gn_ready, 2 * (l + 1))
                TTn(GV, GV, gmg[:, l, :].unsqueeze(1).broadcast_to([128, NB, D_GM]), ALU.mult).then_inc(gv_ready, 1)
                pool.wait_ge(zb_ready, 8 * (l + 1))
                TTn(YB, YB, Pm[:, :, U0:U0 + D_GM], ALU.mult).then_inc(yb_ready, 1)
            pool.wait_ge(moe_loaded, 16 * 2)
            pool.wait_ge(hT_psum, 16)
            TTn(XN[:, :, :], XN[:, :, :], gain2.unsqueeze(1).broadcast_to([128, NB, D]), ALU.mult).then_inc(xn_gained, 1)
            pool.wait_ge(rope_tables, 8)
            with pool.Fori(0, DEPTH) as l:

                def heads(c0, n, d):
                    return P2[:, :, c0:c0 + n * d].rearrange("p b (h d) -> p b h d", d=d)

                def over(table, n, d):
                    return table[:, :, :].unsqueeze(2).broadcast_to([128, NB, n, d])

                def key(k, c0):
                    TTn(RK[:, :, k, :, :], P2[:, :, c0:c0 + HD].unsqueeze(2).broadcast_to([128, NB, 2, HD]),
                        over(cosA, 2, HD), ALU.mult).then_inc(cos_part, 1)

                pool.wait_ge(proj_evac, 4 * l + 9)
                TTn(RQI, heads(QI, 8, 32), over(cosI, 8, 32), ALU.mult).then_inc(cos_part, 1)
                key(2, KB)
                pool.wait_ge(proj_evac, 4 * l + 11)
                TTn(RQ[:, :, 8:16, :], heads(QB, 8, HD), over(cosA, 8, HD), ALU.mult).then_inc(cos_part, 1)
                key(0, KA)
                key(1, KA + HD)
                pool.wait_ge(proj_evac, 4 * l + 12)
                TTn(RQ[:, :, 0:8, :], heads(QA, 8, HD), over(cosA, 8, HD), ALU.mult).then_inc(cos_part, 1)

        @block.scalar
        def _(act):
            fn = nc.scalar.activation
            chain = Chain(act, act_chain)

            def load(dst, src, s):
                act.dma_start(dst, src).then_inc(s, 16)

            def rep(ap):
                return ap.partition_broadcast(128)

            load(ident[:, :], T["c_ident"], ident_loaded)

            def rms(t):
                for b in range(NB):
                    chain.then(fn(XN[:, b, :], X[:, b, :], ACT.Square, accum_out=ss[:, b:b + 1]))
                chain.wait()
                fn(std, ss, ACT.Sqrt, scale=1.0 / D, bias=eps1).then_inc(std_ready, 1)

            def features(t, gain):
                for k in range(4):
                    act.wait_ge(hT_psum, 4 * t + k // 2 + 1)
                    src = ps[:, k // 2, (k % 2) * SEQ:(k % 2 + 1) * SEQ]
                    fn(hT[:, k, :], src, ACT.Copy, scale=1.0 if gain is None else gain(k)).then_inc(hT_ready, 1)

            def silu(s, par_, blocks):
                act.wait_ge(gu_psum, s + 1)
                wait(act, act_ready, s - 1)
                fn(sil[:, par_, 0:blocks, :], ps[:, 2 * par_:2 * par_ + blocks, 0:FN], ACT.Silu).then_inc(silu_ready, 1)

            def split_up(s, par_, use, h):
                if h == 0:
                    act.wait_ge(A_loaded[par_], 32 * use)
                wait(act, (u0_used, gu_psum)[h], s)
                fn(UH[h], ringA[:, par_, 2048 * h:2048 * h + 2048], ACT.Copy).then_inc(u_hi[h], 1)

            def split_down(s, par_, use, unit=None):
                slot = (par_ + 1) % 2
                act.wait_ge(D_loaded[slot], 16 * use)
                if unit is None:
                    wait(act, down_done, s)
                else:
                    act.wait_ge((u0_used, gu_psum)[unit], s + 2 - unit)
                fn(DH if unit is None else UH[unit], ringD[:, slot, :], ACT.Copy).then_inc(d_hi, 1)

            def split_act(s, par_, blocks=NB):
                act.wait_ge(aT_psum, s + 1)
                wait(act, down_done, s - 1)
                fn(aT[:, par_, :, 0:128 * blocks],
                   ps[:, 2 * par_, :].rearrange("p (f n) -> p f n", f=2)[:, :, 0:128 * blocks], ACT.Copy).then_inc(aT_hi, 1)

            def step(s, par_, a_use=None, d_use=None, blocks=NB, between=None, unit=None):
                if a_use is not None:
                    split_up(s + 1, 1 - par_, a_use, 0)
                silu(s, par_, blocks)
                if between:
                    between()
                if d_use is not None:
                    split_act(s - 1, 1 - par_, blocks)
                if a_use is not None:
                    split_up(s + 1, 1 - par_, a_use, 1)
                if d_use is not None:
                    split_down(s - 1, 1 - par_, d_use, unit)

            def split_stream(t, turn):
                for h in range(2):
                    act.wait_ge(hT_ready, 8 * t + 8)
                    fn(xh[:, 4 * h:4 * h + 4, :], hT[:, 4 * h:4 * h + 4, :], ACT.Copy).then_inc(xs_hi, 1)

            def feed_forward(s0, a0, a1, d0, d1):
                step(s0, 0, a1 + 1)
                step(s0 + 1, 1, a0 + 2, d1 + 1)

                def pair(i):
                    step(s0 + 2 * i, 0, a1 + i + 1, d0 + i)
                    step(s0 + 2 * i + 1, 1, a0 + i + 2, d1 + i + 1)

                pair(1)
                with act.Fori(2, STEPS // 2) as i:
                    pair(i)
                s = s0 + STEPS
                step(s - 1, 0, None, d0 + STEPS // 2, unit=0)
                split_act(s - 1, 0)
                split_down(s - 1, 0, d1 + STEPS // 2 + 1, unit=1)

            def tokens_out(e):
                act.wait_ge(xg_psum, e + 1)
                for h in range(2):
                    fn(XGH[:, 4 * h:4 * h + 4, :].rearrange("p k n -> p (k n)"), ps[:, 6 + h, :],
                       ACT.Copy).then_inc(xg_hi, 1)

            def output_out(s):
                act.wait_ge(down_done, s)
                fn(YE.rearrange("p (n c) -> p n c", n=2), ps[:, 4:6, :], ACT.Copy).then_inc(ye_ready, 1)

            def expert(e, s, first=False, last=False):
                a0, a1, d0, d1 = 12 + 7 * e, 11 + 7 * e, 7 + 7 * e, 6 + 7 * e

                def pair(i):
                    step(s + 2 * i, 0, a1 + i + 1, d0 + i, 1)
                    step(s + 2 * i + 1, 1, a0 + i + 2, d1 + i + 1, 1)

                step(s, 0, a1 + 1, None if first else d0, 1)
                step(s + 1, 1, a0 + 2, d1 + 1, 1)
                if not first:
                    output_out(s)
                pair(1)
                act.wait_ge(gt_psum, e + 1)
                fn(GT, ps[:, 1, 0:SEQ], ACT.Copy).then_inc(gt_ready, 1)
                with act.Fori(2, STEPS_E // 2 - 1) as i:
                    pair(i)
                i = STEPS_E // 2 - 1
                step(s + 2 * i, 0, a1 + i + 1, d0 + i, 1)
                step(s + 2 * i + 1, 1, None if last else a0 + i + 2, d1 + i + 1, 1, None if last else lambda: tokens_out(e + 1),
                     0 if last else None)

            def evac_proj(q, c, dst):
                act.wait_ge(proj_psum, 4 * q + c + 1)
                fn(dst, ps[:, 4 + 2 * (c % 2):6 + 2 * (c % 2), 0:dst.shape[2]], ACT.Copy).then_inc(proj_evac, 1)

            act.wait_ge(zeroed, 6)
            act.wait_ge(x_loaded, 16)
            rms(0)
            load(wsr, T["gm_ws"].rearrange("l h i j -> i l h j"), mixer_loaded)
            for g in range(2):
                load(poolw[64 * g:64 * g + 64, :, :, 64 * g:64 * g + 64],
                     T["pool_w"].rearrange("l (r g) c d -> g c l r d", g=2)[g], mixer_loaded)
            load(gmg[:, :, :], rep(T["gm_norm_g"]), mixer_loaded)
            load(band[:, :, :, :], T["c_band"].rearrange("(b p) w t -> p b w t", p=128), mixer_loaded)
            act.wait_ge(par_psum, 1)
            for g in range(2):
                fn(parc[:, 4 * g:4 * g + 4, :], ps[:, g, :].rearrange("p (k n) -> p k n", k=4)[:, :, 0:ROWS],
                   ACT.Copy).then_inc(parc_ready, 1)
            act.wait_ge(parc_ready, 2)
            for l in range(DEPTH):
                if l:
                    act.wait_ge(x_ready, 2)
                    rms(2)
                features(2 * l, lambda k: parc[:, k, R_N1 + l:R_N1 + l + 1])

                def cols(c):
                    c0 = D_IN - C1 * (c + 1)
                    return Pm[:, :, c0:c0 + C1]

                evac_proj(l, 0, cols(0))
                if l == 0:
                    act.wait_ge(wst_psum, 1)
                    raw = ps[:, 2:4, :].rearrange("p l (h i) -> p (l h) i", h=GM_HEADS)
                    wsf = wst[:, :, :, :].rearrange("p l h i -> p (l h) i")
                    fn(wsf[0:64, :, :], raw[0:64, :, :], ACT.Copy).then_inc(wst_ready, 1)
                    fn(wsf[64:128, :, 64:128], raw[64:128, :, 64:128], ACT.Copy).then_inc(wst_ready, 1)
                evac_proj(l, 1, cols(1))
                act.wait_ge(proj_evac, 4 * l + 2)
                fn(GH, Pm[:, :, CG0:CG0 + D_CONV], ACT.Sigmoid).then_inc(sg_ready, 1)
                evac_proj(l, 2, cols(2))
                act.wait_ge(proj_evac, 4 * l + 3)
                for b in range(NB):
                    chain.then(fn(GV[:, b, :], Pm[:, b, V0:V0 + D_GM], ACT.Square, accum_out=gm_ss[:, b:b + 1]))
                chain.wait()
                fn(gm_std, gm_ss, ACT.Sqrt, scale=1.0 / D_GM, bias=eps1).then_inc(gm_std_ready, 1)
                act.wait_ge(gluT_psum, l + 1)
                fn(CT[:, 0:2, TAPS - 1:], ps[:, 0, :].rearrange("p (t n) -> p t n", t=2), ACT.Copy).then_inc(ct_ready, 1)
                fn(CT[:, 2, TAPS - 1:], ps[:, 1, 0:SEQ], ACT.Copy).then_inc(ct_ready, 1)
                act.wait_ge(gm_rstd_ready, l + 1)
                for b in range(NB):
                    fn(GV[:, b, :], Pm[:, b, V0:V0 + D_GM], ACT.Copy, scale=gm_rstd[:, b:b + 1]).then_inc(gn_ready, 1)
                evac_proj(l, 3, cols(3))
                act.wait_ge(pool1_psum, l + 1)
                for g in range(2):
                    for h in range(2):
                        r = slice(64 * h, 64 * h + 64)
                        fn(YT[r, g, :], ps[r, 2 + g, h * SEQ:(h + 1) * SEQ], ACT.Copy).then_inc(yt_ready, 1)
                act.wait_ge(z_psum, l + 1)
                for b in range(NB):
                    for h in range(GM_HEADS):
                        c = slice(h * GM_HD, (h + 1) * GM_HD)
                        r = R_GMB + l * GM_HEADS + h
                        fn(YB[:, b, c], ps[:, 4 + b, c], ACT.Identity, bias=parc[:, 0, r:r + 1]).then_inc(zb_ready, 1)
                act.wait_ge(pool2_psum, l + 1)
                for g in range(2):
                    fn(MT[:, g, :], ps[:, 2, g * SEQ:(g + 1) * SEQ], ACT.Copy,
                       scale=parc[:, g, R_PSC + l:R_PSC + l + 1]).then_inc(mt_ready, 1)
                act.wait_ge(ybT_psum, l + 1)
                fn(MT[:, 2:4, :], ps[:, 6, :].rearrange("p (t n) -> p t n", t=2), ACT.Copy).then_inc(mt_ready, 1)
                fn(MT[:, 4, :], ps[:, 7, 0:SEQ], ACT.Copy).then_inc(mt_ready, 1)
                if l == 0:
                    load(masks[:, :, :], T["c_masks"], attn_loaded)
                    load(freq[:, :], rep(T["c_freq"][0]), attn_loaded)
                    load(lower[:, :, :].rearrange("p a b -> p (a b)"), rep(T["c_lower"][0]), attn_loaded)
                    with nc.allow_non_contiguous_dma(reason="256 positions, one per partition"):
                        load(posi[:, :], T["positions_2"].rearrange("o (b p) -> p (o b)", p=128), attn_loaded)
                    load(sink[:, :, :], rep(T["attn_sinks_2"]), attn_loaded)
                    load(ikg[:, :, :], rep(T["idx_k_g_2"]), attn_loaded)
                    load(ikb[:, :, :], rep(T["idx_k_b_2"]), attn_loaded)
                    load(router[:, :, :], T["moe_router"][0].rearrange("(k p) e -> p k e", p=128), attn_loaded)
                    for k, n in enumerate(("final_g", "ln_in_g_2", "ln_in_b_2")):
                        load(lni[:, k, :], rep(T[n]), ln_loaded)
                    for k, n in enumerate(("ln1_g_2", "ln1_b_2", "ln2_g_2", "ln2_b_2")):
                        load(lnp[:, :, k, :], rep(T[n]), ln_loaded)
                else:
                    load(bandf[:, 0:3 * P128].rearrange("p (k n) -> p k n", k=3), T["c_moe"], moe_loaded)
                    load(gain2, rep(T["norm2_g"][l]), moe_loaded)
                act.wait_ge(cl_var, l + 1)
                fn(lstd, mv[:, :, 1], ACT.Sqrt, bias=eps1).then_inc(cl_std, 1)
                act.wait_ge(cnT_psum, l + 1)
                for t in range(3):
                    fn(HC[:, t, :], ps[:, 2 + t // 2, (t % 2) * SEQ:(t % 2 + 1) * SEQ], ACT.Silu,
                       scale=parc[:, t, R_LNG + l:R_LNG + l + 1], bias=parc[:, t, R_LNB + l:R_LNB + l + 1]).then_inc(hc_ready, 1)
                act.wait_ge(pw_psum, l + 1)
                for d in range(3):
                    fn(MT[:, 5 + d, :], ps[:, d // 2, (d % 2) * SEQ:(d % 2 + 1) * SEQ], ACT.Identity,
                       bias=parc[:, d, R_PWB + l:R_PWB + l + 1]).then_inc(mt_ready, 1)
                act.wait_ge(x_ready, 2 * l + 1)
                rms(2 * l + 1)
                s0, a0 = (0, 3) if l == 0 else (MOE_STEP0, 12)
                split_up(s0, 0, a0 + 1, 0)
                split_up(s0, 0, a0 + 1, 1)
                features(2 * l + 1, lambda k: parc[:, k, R_N2 + l:R_N2 + l + 1])
                if l == 0:
                    split_stream(1, 0)
                    feed_forward(0, 3, 3, 1, 0)
                    act.wait_ge(args_ready, 1)
                    fn(trig, arg, ACT.Sin).then_inc(trig_ready, 1)
            act.wait_ge(gl_ready, 1)
            for b in range(NB):
                fn(gexp[:, b, :], logit[:, b, :], ACT.Exp, bias=gneg[:, b:b + 1]).then_inc(ge_ready, 1)
            tokens_out(0)
            expert(0, MOE_STEP0, first=True)
            with act.Fori(1, EXPERTS - 1) as e:
                expert(e, MOE_STEP0 + STEPS_E * e)
            expert(EXPERTS - 1, B2_STEP0 - STEPS_E, last=True)
            split_act(B2_STEP0 - 1, 1, 1)
            split_down(B2_STEP0 - 1, 1, 63, unit=1)
            output_out(B2_STEP0)

            def second_block(r, e):
                act.wait_ge(ov_xg_psum, 2 * r + 2)
                fn(OX.rearrange("p (c k) n -> p c (k n)", c=2), ps[:, 6:8, :], ACT.Copy).then_inc(ov_xg, 1)
                fn(GT, ps[:, 1, 0:SEQ], ACT.Copy).then_inc(ov_xg, 1)
                with act.Fori(0, STEPS_E) as i:
                    t = STEPS_E * r + i
                    act.wait_ge(ov_gu, t + 1)
                    fn(sil[:, 0, 0, :], ps[:, 0, 0:FN], ACT.Silu).then_inc(ov_silu, 1)
                    act.wait_ge(ov_aT_psum, t + 1)
                    fn(OT, ps[:, 2, 0:256].rearrange("p (f n) -> p f n", f=2), ACT.Copy).then_inc(ov_aT, 1)

            overflowing(act, second_block)
            act.wait_ge(moe_done, 1)
            rms(4)

            def ln_std_of(i):
                act.wait_ge(ln_var, i + 1)
                fn(lstd, mv[:, :, 1], ACT.Sqrt, bias=eps2).then_inc(ln_std, 1)

            ln_std_of(0)
            with act.Fori(0, DEPTH) as l:
                features(2 * l + 4, None)
                for c in range(4):
                    evac_proj(l + 2, c, P2[:, :, (3 - c) * C2:(4 - c) * C2])
                    if c == 1:
                        act.wait_ge(ik_var, l + 1)
                        fn(lstd, mv[:, :, 1], ACT.Sqrt, bias=eps2).then_inc(ik_std, 1)
                for i in range(0, 7, 2):
                    act.wait_ge(qkT_psum, 7 * l + i + 1)
                    fn(TT[:, 2 * i:2 * i + 2, :].rearrange("p t n -> p (t n)"), ps[:, i, :], ACT.Copy).then_inc(qkT_act, 1)
                for b in range(NB):
                    nk = 128 * (b + 1)
                    act.wait_ge(idx_psum, 2 * l + b + 1)
                    fn(RL[:, 0:8 * nk].rearrange("p (r n) -> p r n", r=4), ps[:, 0:4, 0:2 * nk], ACT.Relu).then_inc(relu_ready, 1)
                    for kind, S, scored, nm, den, done in ((0, Sswa, swa_scored, swa_nm, swa_den, swa_exp),
                                                           (1, Sdsa, dsa_scored, dsa_nm, dsa_den, dsa_exp)):
                        act.wait_ge(scored, 2 * l + b + 1)
                        if kind == 0:
                            fn(swa_es, swa_es, ACT.Exp)
                        for h in range(Q_HEADS):
                            fn(S[:, h * nk:(h + 1) * nk], S[:, h * nk:(h + 1) * nk], ACT.Exp, bias=nm[:, h:h + 1],
                               accum_out=den[:, h:h + 1]).then_inc(done, 1)
                        g0 = 12 * l + 4 * b + 2 * (b + 1) * kind
                        for g in range(2 * (b + 1)):
                            act.wait_ge(pt_psum, g0 + g + 1)
                            h0 = 4 * (g % 2)
                            fn(PT[:, g // 2, h0:h0 + 4, :].rearrange("p h q -> p (h q)"), ps[:, 4 + g % 2, :],
                               ACT.Copy).then_inc(pt_ready, 1)
                for i in range(2):
                    act.wait_ge(omT_psum, 4 * l + i + 1)
                    fn(MT2[:, 2 * i:2 * i + 2, :].rearrange("p t n -> p (t n)"), ps[:, i, :], ACT.Copy).then_inc(mt2_act, 1)
                act.wait_ge(pT_psum, l + 1)
                fn(PPT.rearrange("p k n -> p (k n)"), ps[:, 0, :], ACT.Copy).then_inc(pT_ready, 1)
                ln_std_of(2 * l + 1)
                act.wait_ge(pp_psum, l + 1)
                fn(PLEO, psf[:, 0:2048], ACT.Copy).then_inc(pp_ready, 1)
                features(2 * l + 5, None)
                split_stream(2 * l + 5, l + 1)
                s0, a0, a1, d0, d1 = B2_STEP0 + STEPS * l, 72 + 10 * l, 71 + 9 * l, 64 + 6 * l, 62 + 6 * l
                split_up(s0, 0, a0 + 1, 0)
                split_up(s0, 0, a0 + 1, 1)
                act.wait_ge(pg_psum, 2 * l + 2)
                fn(SGP, psf[:, 2048:4096], ACT.Sigmoid).then_inc(sgp_ready, 1)
                feed_forward(s0, a0, a1, d0, d1)
                ln_std_of(2 * l + 2)

        @block.vector
        def _(dve):
            V = nc.vector
            chain = Chain(dve, dve_chain)
            link, then = chain.link, chain.then

            def pause():
                V.memset(spare, 0.0)

            MAGIC, TURN = 1.5 * 2.0 ** 23, 2.0 * np.pi
            T1_ = 6.28125
            T2_ = float(np.round((TURN - T1_) * 2.0 ** 21) / 2.0 ** 21)
            T3_ = float(TURN - T1_ - T2_)
            PI = 3.1415925
            def rope_angles():
                dve.wait_ge(attn_loaded, 16 * 8)
                link(V.tensor_copy(posf, posi[:, :]))
                for b in range(NB):
                    then(V.tensor_scalar(ang[:, b, :], freq[:, :], posf[:, b:b + 1], None, ALU.mult))
                chain.wait()
                for c in range(2):
                    then(V.tensor_scalar(turn[:, c], ang, 1.0 / TURN, 0.25 * c, ALU.mult, ALU.add))
                chain.wait()
                link(V.tensor_scalar(turn, turn, MAGIC, MAGIC, ALU.add, ALU.subtract))
                for c in range(2):
                    then(V.scalar_tensor_tensor(arg[:, c], turn[:, c], -T1_, ang, ALU.mult, ALU.add))
                chain.wait()
                for part in (T2_, T3_):
                    link(V.scalar_tensor_tensor(arg, turn, -part, arg, ALU.mult, ALU.add))
                link(V.tensor_scalar(arg[:, 1], arg[:, 1], np.pi / 2, None, ALU.add))
                V.tensor_scalar(arg, arg, PI, -PI, ALU.min, ALU.max).then_inc(args_ready, 1)

            def normed(t):
                dve.wait_ge(std_ready, t + 1)
                link(V.reciprocal(rstd, std))
                for b in range(NB):
                    V.tensor_scalar(XN[:, b, :], X[:, b, :], rstd[:, b:b + 1], None, ALU.mult).then_inc(xn_ready, 1)

            def features(t, gain):
                for k in range(4, KT):
                    dve.wait_ge(hT_psum, 4 * t + k // 2 + 1)
                    src = ps[:, k // 2, (k % 2) * SEQ:(k % 2 + 1) * SEQ]
                    if gain is None:
                        ins = V.tensor_copy(hT[:, k, :], src)
                    else:
                        ins = V.tensor_scalar(hT[:, k, :], src, gain(k), None, ALU.mult)
                    ins.then_inc(hT_ready, 1)

            def act_mul(s, par_, blocks):
                dve.wait_ge(silu_ready, s + 1)
                wait(dve, aT_psum, s - 1)
                V.tensor_tensor(am[:, par_, 0:blocks, :], sil[:, par_, 0:blocks, :], ps[:, 2 * par_:2 * par_ + blocks, FN:2 * FN],
                                ALU.mult).then_inc(act_ready, 1)

            def split_up(s, par_, h):
                dve.wait_ge(u_hi[h], s + 1)
                V.tensor_tensor(UL[h], ringA[:, par_, 2048 * h:2048 * h + 2048], UH[h].bitcast(f32),
                                ALU.subtract).then_inc(u_ready[h], 1)

            def split_down(s, par_, unit=None):
                hi, lo = (DH, DL) if unit is None else (UH[unit], UL[unit])
                dve.wait_ge(d_hi, s + 1)
                V.tensor_tensor(lo, ringD[:, (par_ + 1) % 2, :], hi.bitcast(f32), ALU.subtract).then_inc(d_ready, 1)

            def split_act(s, par_, blocks=NB):
                dve.wait_ge(aT_hi, s + 1)
                V.tensor_tensor(aTl[:, par_, :, 0:128 * blocks],
                                ps[:, 2 * par_, :].rearrange("p (f n) -> p f n", f=2)[:, :, 0:128 * blocks],
                                aT[:, par_, :, 0:128 * blocks].bitcast(f32), ALU.subtract).then_inc(aT_ready, 1)

            def step(s, par_, ahead=True, behind=True, blocks=NB, between=None, joined=None, unit=None):
                if ahead:
                    split_up(s + 1, 1 - par_, 0)
                act_mul(s, par_, blocks)
                if between:
                    between()
                if behind:
                    split_act(s - 1, 1 - par_, blocks)
                if ahead:
                    split_up(s + 1, 1 - par_, 1)
                if behind:
                    if joined:
                        joined()
                    split_down(s - 1, 1 - par_, unit)

            def split_stream(turn):
                for h in range(2):
                    dve.wait_ge(xs_hi, 2 * turn + h + 1)
                    V.tensor_tensor(xl[:, 4 * h:4 * h + 4, :], hT[:, 4 * h:4 * h + 4, :], xh[:, 4 * h:4 * h + 4, :].bitcast(f32),
                                    ALU.subtract).then_inc(xs_ready, 1)

            def feed_forward(s0):
                step(s0, 0, behind=False)
                step(s0 + 1, 1)
                with dve.Fori(1, STEPS // 2) as i:
                    step(s0 + 2 * i, 0)
                    step(s0 + 2 * i + 1, 1)
                step(s0 + STEPS - 1, 0, ahead=False, unit=0)
                split_act(s0 + STEPS - 1, 0)
                split_down(s0 + STEPS - 1, 0, 1)

            def add_down(done, gate=None):
                for b in range(NB):
                    src = psf[:, 2048 + 1024 * b:3072 + 1024 * b]
                    if gate is None:
                        ins = V.tensor_tensor(X[:, b, :], X[:, b, :], src, ALU.add)
                    else:
                        ins = V.scalar_tensor_tensor(X[:, b, :], src, gate(b), X[:, b, :], ALU.mult, ALU.add)
                    done(b, ins)

            for l in range(DEPTH):
                normed(2 * l)
                if l == 0:
                    dve.wait_ge(parc_ready, 2)
                features(2 * l, lambda k: parc[:, k, R_N1 + l:R_N1 + l + 1])
                dve.wait_ge(sg_ready, l + 1)
                V.tensor_tensor(GH, GH, Pm[:, :, CV0:CV0 + D_CONV], ALU.mult).then_inc(glu_ready, 1)
                dve.wait_ge(gm_std_ready, l + 1)
                V.reciprocal(gm_rstd, gm_std).then_inc(gm_rstd_ready, 1)
                dve.wait_ge(ct_ready, 2 * (l + 1))
                dve.wait_ge(zeroed, 6 + l)
                for t in range(3):
                    then(V.tensor_scalar(ACC[:, t, :], CT[:, t, 0:SEQ], parc[:, t, R_DW + TAPS * l:R_DW + TAPS * l + 1],
                                         parc[:, t, R_DWB + l:R_DWB + l + 1], ALU.mult, ALU.add))
                with dve.Fori(0, TAPS - 2) as i:
                    chain.enter(i, 3)
                    for t in range(3):
                        chain.wait(back=2)
                        then(V.scalar_tensor_tensor(ACC[:, t, :], CT[:, t, bass.ds(i + 1, SEQ)],
                                                    parc[:, t, bass.ds(i + R_DW + TAPS * l + 1, 1)], ACC[:, t, :],
                                                    ALU.mult, ALU.add))
                chain.leave(3, TAPS - 2)
                for t in range(3):
                    chain.wait(back=2 - t)
                    V.scalar_tensor_tensor(ACC[:, t, :], CT[:, t, TAPS - 1:TAPS - 1 + SEQ],
                                           parc[:, t, R_DW + TAPS * l + TAPS - 1:R_DW + TAPS * l + TAPS], ACC[:, t, :],
                                           ALU.mult, ALU.add).then_inc(conv_ready, 1)
                dve.wait_ge(cl_psum, l + 1)
                for b in range(NB):
                    then(V.bn_stats(bst[:, b, 0, :], ps[:, b, 0:D_CONV]))
                chain.wait()
                for b in range(NB):
                    ins = V.bn_aggr(mv[:, b, :], bst[:, b, 0, :])
                ins.then_inc(cl_var, 1)
                dve.wait_ge(cl_std, l + 1)
                link(V.reciprocal(lrstd, lstd))
                for b in range(NB):
                    ins = V.tensor_scalar(CN[:, b, :], ps[:, b, 0:D_CONV], mv[:, b, 0:1], lrstd[:, b:b + 1],
                                          ALU.subtract, ALU.mult)
                ins.then_inc(cn_ready, 1)
                if l == 0:
                    rope_angles()
                for n in range(2):
                    dve.wait_ge(mix_psum, 2 * l + n + 1)
                    for b in range(NB):
                        x = X[:, b, 512 * n:512 * n + 512]
                        ins = V.tensor_tensor(x, x, ps[:, 4 + 2 * b + n, :], ALU.add)
                ins.then_inc(x_ready, 1)
                dve.wait_ge(x_ready, 2 * l + 1)
                normed(2 * l + 1)
                for h in range(2):
                    split_up((0, MOE_STEP0)[l], 0, h)
                features(2 * l + 1, lambda k: parc[:, k, R_N2 + l:R_N2 + l + 1])
                if l == 0:
                    split_stream(0)
                    feed_forward(0)
                    dve.wait_ge(down_done, STEPS)
                    add_down(lambda b, ins: ins.then_inc(x_ready, 1) if b else None)
                    dve.wait_ge(trig_ready, 1)
                    for tc, tsn, h, f in ((cosA, sinA, HD // 2, slice(0, 32)), (cosI, sinI, IDX_DIM // 2, slice(32, 48))):
                        for half in range(2):
                            V.tensor_copy(tc[:, :, half * h:(half + 1) * h], trig[:, 1, :, f]).then_inc(rope_tables, 1)
                            V.tensor_scalar(tsn[:, :, half * h:(half + 1) * h], trig[:, 0, :, f], 2.0 * half - 1.0, None,
                                            ALU.mult).then_inc(rope_tables, 1)
                    dve.wait_ge(x_ready, 2)
            dve.wait_ge(router_psum, 1)
            link(V.tensor_copy(logit, ps[:, 4, 0:NB * EXPERTS].rearrange("p (b e) -> p b e", b=NB)))
            then(V.tensor_reduce(gmax, logit, AX.X, ALU.max))
            for b in range(NB):
                other = logit[:, b, :].unsqueeze(1).broadcast_to([128, EXPERTS, EXPERTS])
                own = logit[:, b, :].unsqueeze(2).broadcast_to([128, EXPERTS, EXPERTS])
                beats = score[:, 64 * b:64 * b + 64].rearrange("p (e f) -> p e f", e=EXPERTS)
                ties = work[:, 64 * b:64 * b + 64].rearrange("p (e f) -> p e f", e=EXPERTS)
                then(V.tensor_tensor(beats, other, own, ALU.is_gt))
                link(V.tensor_tensor(ties, other, own, ALU.is_equal))
                link(V.tensor_tensor(ties, ties, lower[:, :, :], ALU.mult))
                link(V.tensor_tensor(beats, beats, ties, ALU.add))
                link(V.tensor_reduce(rank[:, b, :], beats, AX.X, ALU.add))
            V.tensor_scalar(gneg, gmax, -1.0, None, ALU.mult).then_inc(gl_ready, 1)
            V.tensor_scalar(rank, rank, float(TOP_E), None, ALU.is_lt).then_inc(sel_ready, 1)
            dve.wait_ge(sel_ready, 1)
            dve.wait_ge(ge_ready, NB)
            link(V.tensor_tensor(gexp, gexp, rank, ALU.mult))
            link(V.tensor_reduce(gden, gexp, AX.X, ALU.add))
            link(V.reciprocal(grec, gden))
            for b in range(NB):
                then(V.tensor_scalar(gates[:, b, :], gexp[:, b, :], grec[:, b:b + 1], None, ALU.mult))
            dve.wait_ge(pos_psum, 1)
            link(V.scalar_tensor_tensor(pos, ps[:, 5, 0:NB * EXPERTS], 1.0, rank.rearrange("p b e -> p (b e)"), ALU.add, ALU.mult))
            link(V.tensor_scalar(pos, pos, -1.0, None, ALU.add))
            every = [128, NB * EXPERTS, P128]
            V.tensor_tensor(PL.rearrange("p b e n -> p (b e) n"), iota.unsqueeze(1).broadcast_to(every),
                            pos.unsqueeze(2).broadcast_to(every), ALU.is_equal).then_inc(pl_ready, 1)
            link(V.tensor_scalar(over_flag, ps[:, 5, NB * EXPERTS:(NB + 1) * EXPERTS], float(P128), None, ALU.is_gt))
            over_pairs = score[:, 0:64].rearrange("p (e f) -> p e f", e=EXPERTS)
            then(V.tensor_reduce(over_list[:, 0:1], over_flag, AX.X, ALU.add))
            link(V.tensor_tensor(over_pairs, lower[:, :, :], over_flag.unsqueeze(1).broadcast_to([128, EXPERTS, EXPERTS]), ALU.mult))
            link(V.tensor_reduce(over_rank, over_pairs, AX.X, ALU.add))
            some = [128, MAX_OVER, EXPERTS]
            link(V.tensor_tensor(over_pick, over_rank.unsqueeze(1).broadcast_to(some),
                                 iota[:, 0:MAX_OVER].unsqueeze(2).broadcast_to(some), ALU.is_equal))
            link(V.tensor_tensor(over_pick, over_pick, over_flag.unsqueeze(1).broadcast_to(some), ALU.mult))
            link(V.tensor_tensor(over_pick, over_pick, iota[:, 0:EXPERTS].unsqueeze(1).broadcast_to(some), ALU.mult))
            link(V.tensor_reduce(over_list[:, 1:], over_pick, AX.X, ALU.add))
            V.tensor_copy(over_int[:, :], over_list).then_inc(over_ready, 1)

            def tokens_out(e):
                for h in range(2):
                    dve.wait_ge(xg_hi, 2 * e + h + 1)
                    V.tensor_tensor(XGL[:, 4 * h:4 * h + 4, :].rearrange("p k n -> p (k n)"), ps[:, 6 + h, :],
                                    XGH[:, 4 * h:4 * h + 4, :].rearrange("p k n -> p (k n)").bitcast(f32), ALU.subtract).then_inc(xg_ready, 1)

            def add_scattered():
                for b, n, bank in ((0, 0, 1), (0, 1, 3), (1, 0, 6), (1, 1, 7)):
                    x = X[:, b, n * 512:(n + 1) * 512]
                    ins = V.tensor_tensor(x, x, ps[:, bank, :], ALU.add)
                return ins

            def expert(e, s, first=False, last=False):
                def joined():
                    if not first:
                        dve.wait_ge(scat_psum, e)
                        add_scattered().then_inc(ffn_evac, 1)
                        dve.wait_ge(gt_psum, e)
                    for b in range(NB):
                        ins = V.tensor_scalar(PG[:, b, :], PL[:, b, bass.ds(e, 1), :].rearrange("p o n -> p (o n)"),
                                              gates[:, b, bass.ds(e, 1)], None, ALU.mult)
                    ins.then_inc(pg_ready, 1)

                step(s, 0, behind=not first, blocks=1)
                step(s + 1, 1, blocks=1)
                step(s + 2, 0, blocks=1, joined=joined)
                step(s + 3, 1, blocks=1)
                if not first:
                    dve.wait_ge(ffn_evac, e)
                    pause()
                with dve.Fori(2, STEPS_E // 2 - 1) as i:
                    step(s + 2 * i, 0, blocks=1)
                    step(s + 2 * i + 1, 1, blocks=1)
                step(s + STEPS_E - 2, 0, blocks=1)
                step(s + STEPS_E - 1, 1, not last, blocks=1, between=None if last else lambda: tokens_out(e + 1),
                     unit=0 if last else None)

            tokens_out(0)
            chain.wait()
            dve.wait_ge(pl_ready, 1)
            expert(0, MOE_STEP0, first=True)
            with dve.Fori(1, EXPERTS - 1) as e:
                expert(e, MOE_STEP0 + STEPS_E * e)
            expert(EXPERTS - 1, B2_STEP0 - STEPS_E, last=True)
            split_act(B2_STEP0 - 1, 1, 1)
            split_down(B2_STEP0 - 1, 1, 1)
            dve.wait_ge(scat_psum, EXPERTS)
            add_scattered().then_inc(ffn_evac, 1)
            dve.wait_ge(ffn_evac, EXPERTS)
            V.memset(spare3, 0.0).then_inc(ov_free, 1)

            def second_block(r, e):
                PER = 4
                ov = Chain(dve, ov_chain)
                ov.enter(r, PER)
                for b in range(NB):
                    ov.then(V.tensor_scalar(OP[:, b, :], iota, float(P128), pos[:, bass.ds(e + b * EXPERTS, 1)],
                                            ALU.add, ALU.is_equal))
                ov.wait()
                for b in range(NB):
                    ins = V.tensor_scalar(OG[:, b, :], OP[:, b, :], gates[:, b, bass.ds(e, 1)], None, ALU.mult)
                ins.then_inc(ov_places, 1)
                ov.link(V.memset(YE, 0.0))
                pause()
                with dve.Fori(0, STEPS_E) as i:
                    t = STEPS_E * r + i
                    dve.wait_ge(ov_silu, t + 1)
                    V.tensor_tensor(am[:, 0, 0, :], sil[:, 0, 0, :], ps[:, 0, FN:2 * FN], ALU.mult).then_inc(ov_act, 1)
                    dve.wait_ge(ov_free, t + 2)
                    y = YE.rearrange("p (n c) -> p n c", n=2)
                    V.tensor_tensor(y, y, ps[:, 4:6, :], ALU.add).then_inc(ov_sum, 1)
                    dve.wait_ge(ov_sum, t + 1)
                    pause()
                dve.wait_ge(ov_scat, r + 1)
                ov.link(add_scattered())
                pause()

            overflowing(dve, second_block)
            V.memset(spare2, 0.0).then_inc(moe_done, 1)

            def layer_norm(i, g, b_):
                for b in range(NB):
                    for c in range(2):
                        then(V.bn_stats(bst[:, b, c, :], X[:, b, 512 * c:512 * c + 512]))
                chain.wait()
                pause()
                for b in range(NB):
                    ins = V.bn_aggr(mv[:, b, :], bst[:, b, :, :].rearrange("p c s -> p (c s)"))
                ins.then_inc(ln_var, 1)
                dve.wait_ge(ln_std, i + 1)
                link(V.reciprocal(lrstd, lstd))
                for b in range(NB):
                    then(V.scalar_tensor_tensor(X[:, b, :], X[:, b, :], mv[:, b, 0:1], g, ALU.subtract, ALU.mult))
                chain.wait()
                for b in range(NB):
                    ins = V.scalar_tensor_tensor(X[:, b, :], X[:, b, :], lrstd[:, b:b + 1], b_, ALU.mult, ALU.add)
                ins.then_inc(xln_ready, 1)

            dve.wait_ge(std_ready, 5)
            dve.wait_ge(ln_loaded, 16 * 7)
            link(V.reciprocal(rstd, std))
            for b in range(NB):
                then(V.scalar_tensor_tensor(X[:, b, :], X[:, b, :], rstd[:, b:b + 1], lni[:, 0, :], ALU.mult, ALU.mult))
            chain.wait()
            layer_norm(0, lni[:, 1, :], lni[:, 2, :])

            PER_LAYER = 111
            with dve.Fori(0, DEPTH) as l:
                chain.enter(l, PER_LAYER)
                features(2 * l + 4, None)

                def halves(c0, n, d):
                    return P2[:, :, c0:c0 + n * d].rearrange("p b (h c d) -> p b h c d", c=2, d=d // 2)

                def over(table, half, n, d):
                    return table[:, :, half * d // 2:(half + 1) * d // 2].unsqueeze(2).broadcast_to([128, NB, n, d // 2])

                def turned(c0, h0, n):
                    for half in range(2):
                        then(V.tensor_tensor(T2[:, :, h0:h0 + n, half, :], halves(c0, n, HD)[:, :, :, 1 - half, :],
                                             over(sinA, half, n, HD), ALU.mult))

                dve.wait_ge(proj_evac, 4 * l + 9)
                for b in range(NB):
                    then(V.bn_stats(bst[:, b, 0, :], P2[:, b, KI:KI + IDX_DIM]))
                chain.wait()
                pause()
                for b in range(NB):
                    ins = V.bn_aggr(mv[:, b, :], bst[:, b, 0, :])
                ins.then_inc(ik_var, 1)
                for half in range(2):
                    then(V.tensor_tensor(T2I[:, :, :, half, :], halves(QI, 8, IDX_DIM)[:, :, :, 1 - half, :],
                                         over(sinI, half, 8, IDX_DIM), ALU.mult))
                turned(KB, 18, 1)
                then(V.tensor_scalar(wi, P2[:, :, WI:WI + IDX_HEADS], IDX_HEADS ** -0.5 * IDX_DIM ** -0.5, None, ALU.mult))
                dve.wait_ge(ik_std, l + 1)
                link(V.reciprocal(lrstd, lstd))
                for b in range(NB):
                    then(V.tensor_scalar(KN[:, b, :], P2[:, b, KI:KI + IDX_DIM], mv[:, b, 0:1], lrstd[:, b:b + 1],
                                         ALU.subtract, ALU.mult))
                chain.wait()

                def both(row):
                    return row.broadcast_to([128, NB, IDX_DIM])

                link(V.tensor_tensor(KN, KN, both(ikg[:, bass.ds(l, 1), :]), ALU.mult))
                link(V.tensor_tensor(KN, KN, both(ikb[:, bass.ds(l, 1), :]), ALU.add))
                for half in range(2):
                    h = IDX_DIM // 2
                    then(V.tensor_tensor(T2K[:, :, half, :], KN[:, :, (1 - half) * h:(2 - half) * h],
                                         sinI[:, :, half * h:(half + 1) * h], ALU.mult))
                chain.wait()
                link(V.tensor_tensor(KN, KN, cosI[:, :, :], ALU.mult))
                four = [128, NB, 4, IDX_DIM]
                V.tensor_tensor(RKI, KN.unsqueeze(2).broadcast_to(four),
                                T2K.rearrange("p b c d -> p b (c d)").unsqueeze(2).broadcast_to(four), ALU.add)
                whole = T2.rearrange("p b h c d -> p b h (c d)")

                def key(k, h):
                    V.tensor_tensor(RK[:, :, k, :, :], RK[:, :, k, :, :],
                                    whole[:, :, h:h + 1, :].broadcast_to([128, NB, 2, HD]), ALU.add)

                dve.wait_ge(cos_part, 6 * l + 2)
                V.tensor_tensor(RQI, RQI, T2I.rearrange("p b h c d -> p b h (c d)"), ALU.add)
                key(2, 18)
                dve.wait_ge(proj_evac, 4 * l + 11)
                turned(QB, 10, 8)
                turned(KA, 8, 2)
                dve.wait_ge(cos_part, 6 * l + 5)
                chain.wait()
                V.tensor_tensor(RQ[:, :, 8:16, :], RQ[:, :, 8:16, :], whole[:, :, 10:18, :], ALU.add)
                key(0, 8)
                key(1, 9)
                dve.wait_ge(proj_evac, 4 * l + 12)
                turned(QA, 0, 8)
                dve.wait_ge(cos_part, 6 * l + 6)
                chain.wait()
                V.tensor_tensor(RQ[:, :, 0:8, :], RQ[:, :, 0:8, :], whole[:, :, 0:8, :], ALU.add).then_inc(rope_ready, 1)
                for i in range(1, 7, 2):
                    dve.wait_ge(qkT_psum, 7 * l + i + 1)
                    V.tensor_copy(TT[:, 2 * i:2 * i + 2, :].rearrange("p t n -> p (t n)"), ps[:, i, :]).then_inc(qkT_dve, 1)
                for b in range(NB):
                    nk = 128 * (b + 1)
                    causal = masks[:, 1, 256 - nk:256]

                    def per_head(ap):
                        return ap.rearrange("p (h k) -> p h k", h=Q_HEADS)

                    def bias(m):
                        return m.unsqueeze(1).broadcast_to([128, Q_HEADS, nk])

                    dve.wait_ge(relu_ready, 2 * l + b + 1)
                    sc = score[:, 0:nk]
                    for h in range(IDX_HEADS):
                        p = 2 * (h % 4) + h // 4
                        link(V.scalar_tensor_tensor(sc, RL[:, p * nk:(p + 1) * nk], wi[:, b, h:h + 1], sc if h else causal,
                                                    ALU.mult, ALU.add))
                    dve.wait_ge(swa_psum, 2 * l + b + 1)
                    S = per_head(Sswa[:, 0:8 * nk])
                    link(V.scalar_tensor_tensor(S, per_head(psf[:, 2048:2048 + 8 * nk]), HD ** -0.5,
                                                bias(masks[:, 0, 256 - nk:256]), ALU.mult, ALU.add))
                    link(V.tensor_reduce(swa_m, S, AX.X, ALU.max))
                    snk = sink[:, bass.ds(l, 1), :].rearrange("p o (a t) -> p (o t) a", t=2)

                    def by_place(ap):
                        return ap.rearrange("p (t a) -> p t a", t=2)

                    link(V.tensor_tensor(by_place(swa_m), by_place(swa_m), snk, ALU.max))
                    V.tensor_scalar(swa_nm, swa_m, -1.0, None, ALU.mult)
                    V.tensor_tensor(by_place(swa_es), snk, by_place(swa_m), ALU.subtract).then_inc(swa_scored, 1)
                    for r in range(TOPK // 8):
                        pause()
                        link(V.max(top8, sc))
                        pause()
                        link(V.match_replace(sc, top8, sc, TAKEN))
                    db = dbias[:, 0:nk]
                    link(V.tensor_scalar(db, sc, TAKEN, NEG, ALU.not_equal, ALU.mult))
                    link(V.tensor_tensor(db, db, causal, ALU.min))
                    dve.wait_ge(dsa_psum, 2 * l + b + 1)
                    S = per_head(Sdsa[:, 0:8 * nk])
                    link(V.scalar_tensor_tensor(S, per_head(psf[:, 0:8 * nk]), HD ** -0.5, bias(db), ALU.mult, ALU.add))
                    link(V.tensor_reduce(dsa_m, S, AX.X, ALU.max))
                    V.tensor_scalar(dsa_nm, dsa_m, -1.0, None, ALU.mult).then_inc(dsa_scored, 1)
                    for kind, expd, den, rd in ((0, swa_exp, swa_den, swa_rd), (1, dsa_exp, dsa_den, dsa_rd)):
                        dve.wait_ge(expd, 8 * (2 * l + b + 1))
                        if kind == 0:
                            link(V.tensor_tensor(den, den, swa_es, ALU.add))
                        link(V.reciprocal(rd, den))
                        dve.wait_ge(pv_psum, 4 * l + 2 * b + kind + 1)
                        V.tensor_tensor(OM[:, b, 512 * kind:512 * kind + 512].rearrange("p (a t d) -> p t a d", t=2, d=HD),
                                        ps[:, 6 + kind, :].rearrange("p (t a d) -> p t a d", t=2, d=HD),
                                        by_place(rd).unsqueeze(3).broadcast_to([128, 2, Q_HEADS // 2, HD]),
                                        ALU.mult).then_inc(om_ready, 1)
                for i in range(2, 4):
                    dve.wait_ge(omT_psum, 4 * l + i + 1)
                    V.tensor_copy(MT2[:, 2 * i:2 * i + 2, :].rearrange("p t n -> p (t n)"), ps[:, i, :]).then_inc(mt2_dve, 1)
                for n in range(2):
                    dve.wait_ge(mix_psum, 2 * l + n + 5)
                    for b in range(NB):
                        x = X[:, b, 512 * n:512 * n + 512]
                        then(V.scalar_tensor_tensor(x, x, ALPHA, ps[:, 4 + 2 * b + n, :], ALU.mult, ALU.add))
                chain.wait()

                def lnrow(k):
                    return lnp[:, bass.ds(l, 1), k, :].rearrange("p o d -> p (o d)")

                layer_norm(2 * l + 1, lnrow(0), lnrow(1))
                features(2 * l + 5, None)
                s0 = B2_STEP0 + STEPS * l
                for h in range(2):
                    split_up(s0, 0, h)
                dve.wait_ge(pg_psum, 2 * l + 2)
                split_stream(l + 1)
                xf = X[:, :, :].rearrange("p b n -> p (b n)")
                dve.wait_ge(sgp_ready, l + 1)
                link(V.tensor_tensor(PLEO, SGP, PLEO, ALU.mult))
                link(V.scalar_tensor_tensor(xf, xf, ALPHA, PLEO, ALU.mult, ALU.add))
                pause()
                feed_forward(s0)
                dve.wait_ge(down_done, B2_STEP0 + STEPS * l + STEPS)
                add_down(lambda b, ins: then(ins))
                chain.wait()
                layer_norm(2 * l + 2, lnrow(2), lnrow(3))
            chain.leave(PER_LAYER, DEPTH)


OUT_SHAPE = (1, SEQ, D)


def kernel(**inputs):
    import concourse.bacc as bacc
    from concourse.bass_utils import run_bass_kernel_spmd

    nc = bacc.Bacc("TRN2", target_bir_lowering=False, num_devices=1, dynamic_dma_scratch_size=1024)
    arrays = {n: np.ascontiguousarray(a) for n, a in inputs.items()}
    arrays.update(shape_constants())
    T = {n: nc.dram_tensor(f"in_{n}", a.shape, mybir.dt.from_np(a.dtype), kind="ExternalInput").ap()
         for n, a in arrays.items()}
    T["out"] = nc.dram_tensor("out", OUT_SHAPE, mybir.dt.float32, kind="ExternalOutput").ap()
    build_program(nc, {n: t[0] if n.startswith("moe_") and n != "moe_router" else t for n, t in T.items()})
    run = run_bass_kernel_spmd(nc, [{f"in_{n}": a for n, a in arrays.items()}], core_ids=[0])
    return run.results[0]["out"]
```
